# Optimizing a Trainium2 kernel written in Bass

```python
import math
import jax, jax.numpy as jnp
from jax import lax
import numpy as np

D_MODEL = 1024
BATCH = 1
SEQ = 512
DEPTH = 1

POOL_WIDTH = D_MODEL // 2
POOL_WINDOWS = (2, 4, 8, 16)
N_POOL_GROUPS = len(POOL_WINDOWS)
POOL_GROUP = POOL_WIDTH // N_POOL_GROUPS
HEAD_DIM = 64
N_HEADS = (D_MODEL // 2) // HEAD_DIM
N_KV = 2
HEADS_PER_KV = N_HEADS // N_KV
Q_WIDTH = N_HEADS * HEAD_DIM
KV_WIDTH = N_KV * HEAD_DIM
CMP_STRIDE = 16
CMP_BLOCK = 2 * CMP_STRIDE
CMP_HIDDEN = 4 * HEAD_DIM
SLC_BLOCK = 64
N_SELECT = 16
WINDOW = 512
Q_BLOCK = SLC_BLOCK
ALIBI_MAX = 8.0
MIX_SIZES = (POOL_WIDTH, Q_WIDTH, KV_WIDTH, KV_WIDTH, KV_WIDTH, KV_WIDTH, KV_WIDTH, KV_WIDTH, 3 * N_HEADS, 2 * D_MODEL)
MIX_IN = sum(MIX_SIZES)
V_SLOTS = (3, 5, 7)
D_FF = 2816
ALPHA = (2.0 * DEPTH) ** 0.25
BETA = (8.0 * DEPTH) ** -0.25
LN_EPS = 1e-5
NEG = -1e30
FORCE = 1e9

kernel_name = 'hybrid_pool_nsa_macaron_block'

def layer_norm(x, g, b):
    xf = x.astype(jnp.float32)
    mu = jnp.mean(xf, axis=-1, keepdims=True)
    var = jnp.mean(jnp.square(xf - mu), axis=-1, keepdims=True)
    return ((xf - mu) * lax.rsqrt(var + LN_EPS) * g + b).astype(x.dtype)

def swiglu(h, w_in, w_out):
    gate, up = jnp.split(h @ w_in, 2, axis=-1)
    return (jax.nn.silu(gate) * up) @ w_out

def masked_softmax(s, mask):
    p = jax.nn.softmax(jnp.where(mask, s, NEG), axis=-1)
    return jnp.where(mask, p, 0.0)

def alibi_slopes(n_heads):
    return (2.0 ** (-ALIBI_MAX * np.arange(1, n_heads + 1) / n_heads)).astype(np.float32)

def cmp_to_slc_overlap(n_cmp, n_slc):
    start = np.arange(n_cmp)[:, None] * CMP_STRIDE
    blk = np.arange(n_slc)[None, :] * SLC_BLOCK
    return ((start < blk + SLC_BLOCK) & (start + CMP_BLOCK > blk)).astype(np.float32)

def pool_mixer(u, pool_w, pool_scale):
    b_, s_, p_ = u.shape
    uf = u.astype(jnp.float32)
    cs = jnp.concatenate([jnp.zeros((b_, 1, p_), jnp.float32), jnp.cumsum(uf, axis=1)], axis=1)
    t = jnp.arange(s_)
    means = []
    for gi, w in enumerate(POOL_WINDOWS):
        csg = cs[:, :, gi * POOL_GROUP:(gi + 1) * POOL_GROUP]
        lo = jnp.maximum(t + 1 - w, 0)
        cnt = (t + 1 - lo).astype(jnp.float32)
        means.append((csg[:, 1:] - csg[:, lo]) / cnt[None, :, None])
    pooled = jnp.stack(means, axis=2)
    delta = (pooled - uf.reshape(b_, s_, N_POOL_GROUPS, POOL_GROUP)).astype(u.dtype)
    mixed = jnp.einsum('bsgc,gcd->bsgd', delta, pool_w)
    return mixed.reshape(b_, s_, p_) * pool_scale

def compress(k, pos, w1, w2):
    b_, g_, s_, d_ = k.shape
    kc = k.reshape(b_, g_, s_ // CMP_STRIDE, CMP_STRIDE, d_)
    blocks = jnp.concatenate([kc[:, :, :-1], kc[:, :, 1:]], axis=3) + pos
    blocks = blocks.reshape(b_, g_, -1, CMP_BLOCK * d_)
    return jax.nn.gelu(blocks @ w1) @ w2

def nsa_attention(q, k_cmp, v_cmp, k_slc, v_slc, k_win, v_win, g_nsa,
                  cmp_pos_k, cmp_k_w1, cmp_k_w2, cmp_pos_v, cmp_v_w1, cmp_v_w2):
    b_, s_, _ = q.shape
    dt = q.dtype
    f32 = jnp.float32
    q = (q * HEAD_DIM ** -0.5).reshape(b_, s_, N_KV, HEADS_PER_KV, HEAD_DIM).transpose(0, 2, 3, 1, 4)
    to_kv = lambda a: a.reshape(b_, s_, N_KV, HEAD_DIM).transpose(0, 2, 1, 3)
    k_cmp, v_cmp, k_slc, v_slc, k_win, v_win = [to_kv(a) for a in (k_cmp, v_cmp, k_slc, v_slc, k_win, v_win)]
    gates = jax.nn.sigmoid(g_nsa).reshape(b_, s_, N_KV, HEADS_PER_KV, 3).transpose(0, 2, 3, 1, 4)
    kc = compress(k_cmp, cmp_pos_k, cmp_k_w1, cmp_k_w2)
    vc = compress(v_cmp, cmp_pos_v, cmp_v_w1, cmp_v_w2)
    n_cmp = kc.shape[2]
    n_slc = s_ // SLC_BLOCK
    n_sel = min(N_SELECT, n_slc)
    ks_blk = k_slc.reshape(b_, N_KV, n_slc, SLC_BLOCK, HEAD_DIM)
    vs_blk = v_slc.reshape(b_, N_KV, n_slc, SLC_BLOCK, HEAD_DIM)
    pad = ((0, 0), (0, 0), (WINDOW, 0), (0, 0))
    kw_pad = jnp.pad(k_win, pad)
    vw_pad = jnp.pad(v_win, pad)
    slopes = jnp.asarray(alibi_slopes(N_HEADS)).reshape(N_KV, HEADS_PER_KV)[None, :, :, None, None]
    cmp_end = jnp.arange(n_cmp) * CMP_STRIDE + CMP_BLOCK - 1
    overlap = jnp.asarray(cmp_to_slc_overlap(n_cmp, n_slc))
    bi = jnp.arange(b_)[:, None, None, None]
    gi = jnp.arange(N_KV)[None, :, None, None]
    blk_ids = jnp.arange(n_slc)
    in_blk = jnp.arange(SLC_BLOCK)
    win_off = jnp.arange(WINDOW + Q_BLOCK) - WINDOW
    m_sel = n_sel * SLC_BLOCK

    def query_block(qb):
        q0 = qb * Q_BLOCK
        t = q0 + jnp.arange(Q_BLOCK)
        qq = lax.dynamic_slice_in_dim(q, q0, Q_BLOCK, axis=3)
        dist = (t[:, None] - cmp_end[None, :]).astype(f32)
        s = jnp.einsum('bghqd,bgnd->bghqn', qq, kc, preferred_element_type=f32)
        p_cmp = masked_softmax(s - slopes * dist, dist >= 0)
        o_cmp = jnp.einsum('bghqn,bgnd->bghqd', p_cmp.astype(dt), vc)
        imp = jnp.einsum('bghqn,nj->bgqj', p_cmp, overlap)
        cur = t // SLC_BLOCK
        forced = (blk_ids[None, :] == 0) | (blk_ids[None, :] == cur[:, None]) | (blk_ids[None, :] == cur[:, None] - 1)
        future = blk_ids[None, :] > cur[:, None]
        score = jnp.where(future, NEG, jnp.where(forced, FORCE, imp))
        _, idx = lax.top_k(score, n_sel)
        k_sel = ks_blk[bi, gi, idx].reshape(b_, N_KV, Q_BLOCK, m_sel, HEAD_DIM)
        v_sel = vs_blk[bi, gi, idx].reshape(b_, N_KV, Q_BLOCK, m_sel, HEAD_DIM)
        pos = (idx[..., None] * SLC_BLOCK + in_blk).reshape(b_, N_KV, Q_BLOCK, m_sel)
        dist = (t[:, None] - pos).astype(f32)[:, :, None]
        s = jnp.einsum('bghqd,bgqmd->bghqm', qq, k_sel, preferred_element_type=f32)
        p = masked_softmax(s - slopes * dist, dist >= 0)
        o_slc = jnp.einsum('bghqm,bgqmd->bghqd', p.astype(dt), v_sel)
        kw = lax.dynamic_slice_in_dim(kw_pad, q0, WINDOW + Q_BLOCK, axis=2)
        vw = lax.dynamic_slice_in_dim(vw_pad, q0, WINDOW + Q_BLOCK, axis=2)
        sp = q0 + win_off
        dist = t[:, None] - sp[None, :]
        valid = (dist >= 0) & (dist < WINDOW) & (sp[None, :] >= 0)
        s = jnp.einsum('bghqd,bgkd->bghqk', qq, kw, preferred_element_type=f32)
        p = masked_softmax(s - slopes * dist.astype(f32), valid)
        o_win = jnp.einsum('bghqk,bgkd->bghqd', p.astype(dt), vw)
        g = lax.dynamic_slice_in_dim(gates, q0, Q_BLOCK, axis=3)
        return g[..., 0:1] * o_cmp + g[..., 1:2] * o_slc + g[..., 2:3] * o_win

    out = lax.map(query_block, jnp.arange(s_ // Q_BLOCK))
    return out.transpose(1, 0, 4, 2, 3, 5).reshape(b_, s_, Q_WIDTH)

def token_mixer(h, w_mix_in, pool_w, pool_scale, cmp_pos_k, cmp_k_w1, cmp_k_w2, cmp_pos_v, cmp_v_w1, cmp_v_w2,
                w_branch_a, w_branch_b, w_mix_out):
    z = h @ w_mix_in
    splits = np.cumsum(MIX_SIZES)[:-1].tolist()
    u_pool, q, k_cmp, v_cmp, k_slc, v_slc, k_win, v_win, g_nsa, g_br = jnp.split(z, splits, axis=-1)
    y_a = pool_mixer(u_pool, pool_w, pool_scale) @ w_branch_a
    y_b = nsa_attention(q, k_cmp, v_cmp, k_slc, v_slc, k_win, v_win, g_nsa,
                        cmp_pos_k, cmp_k_w1, cmp_k_w2, cmp_pos_v, cmp_v_w1, cmp_v_w2) @ w_branch_b
    g_a, g_b = jnp.split(jax.nn.sigmoid(g_br), 2, axis=-1)
    return (g_a * y_a + g_b * y_b) @ w_mix_out

def setup_inputs(seed: int = 0) -> dict:
    key = jax.random.key(seed)
    keys = jax.random.split(key, 40)
    cnt = [0]

    def nrm(shape, scale):
        k = keys[cnt[0]]
        cnt[0] += 1
        return jax.random.normal(k, shape, jnp.float32) * scale

    L, D = DEPTH, D_MODEL
    col_scale = np.concatenate([np.full((n,), BETA if i in V_SLOTS else 1.0) for i, n in enumerate(MIX_SIZES)])
    col_scale = jnp.asarray((col_scale * D ** -0.5).astype(np.float32))
    return {
        'x': nrm((BATCH, SEQ, D), 1.0),
        'c': nrm((BATCH, D), 1.0),
        'ln_in_g': 1.0 + nrm((D,), 0.02),
        'ln_in_b': nrm((D,), 0.02),
        'w_ada': nrm((L, D, 9 * D), D ** -0.5),
        'b_ada': nrm((L, 9 * D), 0.02),
        'ffn1_w_in': nrm((L, D, 2 * D_FF), D ** -0.5),
        'ffn1_w_out': nrm((L, D_FF, D), BETA * D_FF ** -0.5),
        'ln1_g': 1.0 + nrm((L, D), 0.02),
        'ln1_b': nrm((L, D), 0.02),
        'w_mix_in': nrm((L, D, MIX_IN), 1.0) * col_scale,
        'pool_w': nrm((L, N_POOL_GROUPS, POOL_GROUP, POOL_GROUP), POOL_GROUP ** -0.5),
        'pool_scale': 1.0 + nrm((L, POOL_WIDTH), 0.1),
        'cmp_pos_k': nrm((L, CMP_BLOCK, HEAD_DIM), 0.02),
        'cmp_k_w1': nrm((L, CMP_BLOCK * HEAD_DIM, CMP_HIDDEN), (CMP_BLOCK * HEAD_DIM) ** -0.5),
        'cmp_k_w2': nrm((L, CMP_HIDDEN, HEAD_DIM), CMP_HIDDEN ** -0.5),
        'cmp_pos_v': nrm((L, CMP_BLOCK, HEAD_DIM), 0.02),
        'cmp_v_w1': nrm((L, CMP_BLOCK * HEAD_DIM, CMP_HIDDEN), (CMP_BLOCK * HEAD_DIM) ** -0.5),
        'cmp_v_w2': nrm((L, CMP_HIDDEN, HEAD_DIM), CMP_HIDDEN ** -0.5),
        'w_branch_a': nrm((L, POOL_WIDTH, D), BETA * POOL_WIDTH ** -0.5),
        'w_branch_b': nrm((L, Q_WIDTH, D), BETA * Q_WIDTH ** -0.5),
        'w_mix_out': nrm((L, D, D), BETA * D ** -0.5),
        'ln2_g': 1.0 + nrm((L, D), 0.02),
        'ln2_b': nrm((L, D), 0.02),
        'ffn2_w_in': nrm((L, D, 2 * D_FF), D ** -0.5),
        'ffn2_w_out': nrm((L, D_FF, D), BETA * D_FF ** -0.5),
        'ln3_g': 1.0 + nrm((L, D), 0.02),
        'ln3_b': nrm((L, D), 0.02),
    }

def reference(x, c, ln_in_g, ln_in_b, w_ada, b_ada, ffn1_w_in, ffn1_w_out, ln1_g, ln1_b,
              w_mix_in, pool_w, pool_scale, cmp_pos_k, cmp_k_w1, cmp_k_w2, cmp_pos_v, cmp_v_w1, cmp_v_w2,
              w_branch_a, w_branch_b, w_mix_out, ln2_g, ln2_b, ffn2_w_in, ffn2_w_out, ln3_g, ln3_b):
    x = layer_norm(x, ln_in_g, ln_in_b)
    c_act = jax.nn.silu(c)
    for l in range(DEPTH):
        ada = (c_act @ w_ada[l] + b_ada[l]).reshape(c.shape[0], 3, 3, D_MODEL)
        mod = lambda i, j: ada[:, i, j][:, None, :]
        h = x * (1.0 + mod(0, 1)) + mod(0, 0)
        x = layer_norm(ALPHA * x + 0.5 * mod(0, 2) * swiglu(h, ffn1_w_in[l], ffn1_w_out[l]), ln1_g[l], ln1_b[l])
        h = x * (1.0 + mod(1, 1)) + mod(1, 0)
        y = token_mixer(h, w_mix_in[l], pool_w[l], pool_scale[l], cmp_pos_k[l], cmp_k_w1[l], cmp_k_w2[l],
                        cmp_pos_v[l], cmp_v_w1[l], cmp_v_w2[l], w_branch_a[l], w_branch_b[l], w_mix_out[l])
        x = layer_norm(ALPHA * x + mod(1, 2) * y, ln2_g[l], ln2_b[l])
        h = x * (1.0 + mod(2, 1)) + mod(2, 0)
        x = layer_norm(ALPHA * x + 0.5 * mod(2, 2) * swiglu(h, ffn2_w_in[l], ffn2_w_out[l]), ln3_g[l], ln3_b[l])
    return x


_drawn_inputs = setup_inputs


def setup_inputs(seed=0):
    import zlib

    import numpy as np

    out = dict(_drawn_inputs(seed))
    spreads = {}
    factors = {'ln_in_g': 2.737,
     'ln_in_b': 2.95,
     'b_ada': 4.96,
     'ln1_g': 2.98,
     'ln1_b': 2.849,
     'pool_scale': 5.365,
     'cmp_pos_k': 8.0,
     'cmp_k_w1': 8.0,
     'cmp_k_w2': 8.0,
     'cmp_pos_v': 22.978,
     'cmp_v_w1': 2.961,
     'cmp_v_w2': 2.676,
     'ln2_g': 2.809,
     'ln2_b': 2.878,
     'ln3_g': 7.892,
     'ln3_b': 8.716}
    for name, (base, spread) in spreads.items():
        noise = np.random.default_rng([zlib.crc32(name.encode()), seed]).standard_normal(out[name].shape)
        drawn = base * np.exp(spread * noise) if base else spread * noise
        out[name] = __import__('jax').numpy.asarray(drawn.astype(out[name].dtype))
    for name, factor in factors.items():
        out[name] = (out[name] * factor).astype(out[name].dtype)
    return out
```

```python
import math
from contextlib import ExitStack

import numpy as np
import concourse.bass as bass
from concourse import mybir

F32 = mybir.dt.float32
F32R = mybir.dt.float32r
ALU = mybir.AluOpType
ACT = mybir.ActivationFunctionType
AX = mybir.AxisListType

P = 128
D = 1024
T = 512
KT = D // P
TT = T // P
F = 2816
FT = F // P
HEADS, HEAD = 8, 64
GROUPS = 2
HPG = HEADS // GROUPS
STRIDE = 16
N_CMP = T // STRIDE - 1
CPAD = 32
HID_T = 2
PAIRS = 16
WINDOWS = (2, 4, 8, 16)
NEG = -1e30
EPS = 1e-5
ALPHA = 2.0 ** 0.25
GELU_A, GELU_B = math.sqrt(2.0 / math.pi), 0.044715

OUT_SPLIT = (8, 7, 7)
IN_PANELS = 2 * FT
OUT_PANELS = 3 * KT
MIX = ["kc", "vc", "u0", "u1", "u2", "u3", "gate", "q0", "q1", "q2", "q3", "kslc", "kwin",
       "poolw", "vslc", "vwin"]
MIX8 = [n for n in MIX if n != "poolw"]
B_FFN1 = 0
B_MIX = B_FFN1 + IN_PANELS + OUT_PANELS
B_BRANCH = B_MIX + len(MIX)
B_MIXOUT = B_BRANCH + 3 * KT
B_FFN2 = B_MIXOUT + KT
N_PANELS = B_FFN2 + IN_PANELS + OUT_PANELS
assert B_MIX % 4 == 0 and B_FFN2 % 4 == 0

C_BADA, C_LNG, C_LNB, C_PSCALE, C_C = 0, 72, 104, 136, 140
N_COLS = 148
LNS = 4

P_OFF = [0, 128, 384, 768]
P_LEN = 1280
PT_OFF = [0, 512, 896, 1152]
PT_GROUPS = [[0], [1], [2, 3]]
UNITS = [(h, br) for h in range(HEADS) for br in range(2)]

SBUF_BASE = 16512
O_X = SBUF_BASE
O_HHI = O_X + 4 * KT * T
O_HLO = O_HHI + 4 * KT * T
O_RAW = O_HLO + 4 * KT * T
O_WHI = O_RAW + 2 * 4096
O_WLO = O_WHI + 4 * 4096
O_ADARAW = O_WLO + 4 * 4096
O_ACC = O_ADARAW + 3 * 2048
O_SCR = O_ACC + 3 * 4096
O_REGION = O_SCR + 4 * 2048
O_CONST = O_REGION + 2 * FT * 4 * T


def need(eng, sem, value):
    if not isinstance(value, int) or value > 0:
        eng.wait_ge(sem, value)


def build(nc, xT, cols, ada_w, ffn_in, ffn_out, mix_w, pool_w, branch_w, mixout_w,
          w1, w2, pos, ident_in, dist_in, cbias_in, cmask_in, icnt_in, out):
    with ExitStack() as ctx:
        def at(name, shape, offset, dt=F32):
            return nc.alloc_sbuf_tensor_at(name, shape, dt, offset=offset)

        ctx.enter_context(nc.sbuf_tensor("whole", [P, 53200], F32))
        X = at("X", [P, KT, T], O_X)
        h_hi = at("h_hi", [P, KT, T], O_HHI, F32R)
        h_lo = at("h_lo", [P, KT, T], O_HLO, F32R)
        raw = at("raw", [P, 2, 1024], O_RAW)
        w_hi = at("w_hi", [P, 4, 1024], O_WHI, F32R)
        w_lo = at("w_lo", [P, 4, 1024], O_WLO, F32R)
        ada_raw = at("ada_raw", [P, 3, 512], O_ADARAW)
        acc = at("acc", [P, 3, 1024], O_ACC)
        scr = at("scr", [P, 4, T], O_SCR)
        act_hi = at("act_hi", [P, FT, T], O_REGION, F32R)
        act_lo = at("act_lo", [P, FT, T], O_REGION + FT * 2048, F32R)
        ada_start = at("ada_start", [P, KT, 2048], O_REGION)
        R = O_REGION
        qT = at("qT", [P, 4, T], R)
        kT = at("kT", [P, 2, T], R + 8192)
        V = at("V", [P, 2, TT, P], R + 12288)
        vT = at("vT", [P, 2, T], R + 16384)
        w1v = at("w1v", [P, PAIRS, 256], R)
        blocks = at("blocks", [P, 4, 2, 256], R + 20480)
        PT = at("PT", [P, 2, P_LEN], R + 20480)
        Pr = at("Pr", [P, 2, P_LEN], R + 30720)
        pads = at("pads", [P, 4, 528], R + 30720)
        hidden = at("hidden", [P, 4, 62], R + 39168)
        cbias = at("cbias", [P, TT, HEADS, N_CMP], R + 40960)
        PcT = at("PcT", [P, GROUPS, T], R + 40960)
        dist = at("dist", [P, T], R + 45056)
        abias = at("abias", [P, 2, T], R + 47104)
        Pc = at("Pc", [P, TT, HEADS, CPAD], R + 51200)
        cmask = at("cmask", [P, TT, CPAD], R + 55296)
        G = at("G", [P, TT, 24], R + 55808)
        nmax = at("nmax", [P, 64], R + 56192)
        psumv = at("psumv", [P, 64], R + 56448)
        pscl = at("pscl", [P, 64], R + 56704)
        cst = at("cst", [P, 3, 32], R + 56960)
        pool_hi = at("pool_hi", [P, 4, T], R + 57344, F32R)
        pool_lo = at("pool_lo", [P, 4, T], R + 65536, F32R)
        o_hi = at("o_hi", [P, 4, T], R + 73728, F32R)
        o_lo = at("o_lo", [P, 4, T], R + 81920, F32R)
        w1k = at("w1k", [P, PAIRS, 256], R + 73728)
        mixed_hi = at("mixed_hi", [P, KT, T], R, F32R)
        mixed_lo = at("mixed_lo", [P, KT, T], R + 16384, F32R)
        tab = at("tab", [P, 2, 2, T], R + 32768)
        o = O_CONST
        ident = at("ident", [P, P], o)
        ones = at("ones", [P, P], o + 512)
        VC = at("VC", [P, P], o + 1024)
        colv = at("colv", [P, N_COLS], o + 1536)
        ada = at("ada", [P, 72], o + 2144)
        mod = at("mod", [P, 6, 8], o + 2432)
        cact = at("cact", [P, 8], o + 2624)
        onec = at("onec", [P, 2], o + 2656)
        posv = at("posv", [P, 2, PAIRS], o + 2688)
        w2s = at("w2s", [P, 2, HID_T, HEAD], o + 2816)
        icnt = at("icnt", [P, 4, 16], o + 3840)
        kcT = at("kcT", [P, N_CMP], o + 4096)
        assert o + 4224 <= 229344

        psum = ctx.enter_context(nc.psum_tensor("psum", [P, 8, T], F32))

        def bank(n, w=T):
            return psum[:, n, 0:w]

        def sem(name):
            return ctx.enter_context(nc.semaphore(name))

        raw_landed = [sem(f"raw_landed{i}") for i in range(2)]
        ada_landed = [sem(f"ada_landed{i}") for i in range(3)]
        ada0_landed = [sem(f"ada0_landed{i}") for i in range(KT)]
        x_landed = [sem(f"x_landed{i}") for i in range(4)]
        const_landed = sem("const_landed")
        cols_landed = sem("cols_landed")
        mixc_landed = sem("mixc_landed")
        out_stored = sem("out_stored")
        split_hi = sem("split_hi")
        split_done = sem("split_done")
        panels_used = sem("panels_used")
        memset_done = sem("memset_done")
        c_tanh = sem("c_tanh")
        ada_used = sem("ada_used")
        ada_acc_start = sem("ada_acc_start")
        ada_cols = sem("ada_cols")
        ada_taken = sem("ada_taken")
        dve_chain = sem("dve_chain")
        act_chain = sem("act_chain")
        s_added = sem("s_added")
        q_added = sem("q_added")
        sq_done = sem("sq_done")
        stats_ready = sem("stats_ready")
        mean_sq = sem("mean_sq")
        var_done = sem("var_done")
        std_done = sem("std_done")
        mod_ready = sem("mod_ready")
        centered = sem("centered")
        xhat_done = sem("xhat_done")
        h_made = sem("h_made")
        h_hi_done = sem("h_hi_done")
        h_split = sem("h_split")
        x_scaled = sem("x_scaled")
        z_done = sem("z_done")
        tanh_done = sem("tanh_done")
        gated = sem("gated")
        hidden_made = sem("hidden_made")
        act_hi_done = sem("act_hi_done")
        act_split = sem("act_split")
        kv_blocks = sem("kv_blocks")
        act_evac = sem("act_evac")
        pool_delta = sem("pool_delta")
        pool_hi_done = sem("pool_hi_done")
        pool_split = sem("pool_split")
        pool_mixed = sem("pool_mixed")
        poolout_hi = sem("poolout_hi")
        poolout_split = sem("poolout_split")
        cmp_hidden = sem("cmp_hidden")
        cmp_sq = sem("cmp_sq")
        cmp_arg = sem("cmp_arg")
        cmp_tanh = sem("cmp_tanh")
        cmp_act = sem("cmp_act")
        cmp_kv = sem("cmp_kv")
        cmp_kv_taken = sem("cmp_kv_taken")
        gates_T = sem("gates_T")
        gates_taken = sem("gates_taken")
        cmp_scored = sem("cmp_scored")
        cmp_shifted = sem("cmp_shifted")
        cmp_exp = sem("cmp_exp")
        cmp_probs = sem("cmp_probs")
        cmp_PT = sem("cmp_PT")
        cmp_PT_taken = sem("cmp_PT_taken")
        v_turned = sem("v_turned")
        v_taken = sem("v_taken")
        bias_made = sem("bias_made")
        scored = sem("scored")
        shifted = sem("shifted")
        exp_done = sem("exp_done")
        probs_ready = sem("probs_ready")
        turned = sem("turned")
        turned_act = sem("turned_act")
        turned_dve = sem("turned_dve")
        o_made = sem("o_made")
        o_hi_done = sem("o_hi_done")
        o_split = sem("o_split")
        br_tanh = sem("br_tanh")
        br_gated = sem("br_gated")
        br_mixed = sem("br_mixed")
        br_hi = sem("br_hi")
        br_split = sem("br_split")

        block = ctx.enter_context(nc.Block())

        ADA_BASE = {1: 0, "mix": 48, 2: 96}
        N_ADA = {1: 6, "mix": 6, 2: 2}
        ADA_CHUNK = {1: 2, "mix": 5, 2: 8}
        ADA_SLOT = {1: [0, 0, 0], "mix": [16, 16, 16], 2: [32, 32, 32]}

        def ada_slot_count(phase, step, q):
            per = 2 if N_ADA[phase] == 6 else 1
            return ADA_SLOT[phase][q % 3] + per * step + q // 3 + 1

        def in_base(n):
            return B_FFN1 if n == 1 else B_FFN2

        def chunk_base(n):
            return 0 if n == 1 else FT

        @block.sync
        def _(sp):
            def panel(p, src, width=1024, slot=None):
                need(sp, split_done, p - 1)
                sp.dma_start(raw[:, slot, 0:width], src).then_inc(raw_landed[slot], 16)

            def ada_unit(phase, step, q):
                u = ADA_BASE[phase] + N_ADA[phase] * step + q
                need(sp, ada_used, u - (2 if N_ADA[phase] == 6 else 1))
                col = (ADA_CHUNK[phase] + q // 2) * 1024 + (q % 2) * 512
                sp.dma_start(ada_raw[:, q % 3, :], ada_w[step, :, col:col + 512]).then_inc(
                    ada_landed[q % 3], 16)

            def feed_forward(n):
                base = in_base(n)

                def step(it, with_ada, with_panels=True):
                    for j in range(4):
                        c = 2 * it + 2 + j // 2
                        if with_panels:
                            panel(base + 4 * it + 4 + j, ffn_in[n - 1, c, j % 2, :, :], slot=j % 2)
                        if with_ada:
                            per = N_ADA[n]
                            for q in ([0, 1], [2], [3, 4], [5])[j]:
                                if q < per:
                                    ada_unit(n, it, q)

                for j in range(2 if n == 1 else 0, 4):
                    panel(base + j, ffn_in[n - 1, j // 2, j % 2, :, :], slot=j % 2)
                step(0, True)
                with sp.Fori(1, KT) as it:
                    step(it, True)
                with sp.Fori(KT, FT // 2 - 1) as it:
                    step(it, False)
                ob = base + IN_PANELS
                with sp.Fori(0, 2) as it:
                    for m4 in range(4):
                        off = 0
                        for j, kn in enumerate(OUT_SPLIT):
                            i = 3 * m4 + j
                            panel(ob + 12 * it + i,
                                  ffn_out[n - 1, 4 * it + m4, :, off * P:(off + kn) * P],
                                  width=kn * P, slot=i % 2)
                            off += kn

            for i in range(4):
                sp.dma_start(X[:, 2 * i:2 * i + 2, :], xT[:, 2 * i:2 * i + 2, :]).then_inc(
                    x_landed[i], 16)
            for j in range(2):
                panel(j, ffn_in[0, 0, j, :, :], slot=j)
            for k in range(KT):
                sp.dma_start(ada_start[:, k, :], ada_w[k, :, 0:2048]).then_inc(ada0_landed[k], 16)
            feed_forward(1)
            k8 = 0
            for i, name in enumerate(MIX):
                p = B_MIX + i
                if name == "poolw":
                    panel(p, pool_w[:, :], width=512, slot=p % 2)
                else:
                    panel(p, mix_w[k8, :, :], slot=p % 2)
                    k8 += 1

            def branch_panel(i):
                m, j = divmod(i, 3)
                if m < KT:
                    src = branch_w[m, :, :] if j == 2 else mix_w[k8 + 2 * m + j, :, :]
                    panel(B_BRANCH + i, src, slot=(B_BRANCH + i) % 2)

            branch_panel(0)
            branch_panel(1)
            for i in range(3 * KT):
                branch_panel(i + 2)
                for q in range(2 * (i % 3), 2 * (i % 3) + 2):
                    ada_unit("mix", i // 3, q)
            for m in range(KT):
                p = B_MIXOUT + m
                panel(p, mixout_w[m, :, :], slot=p % 2)
            feed_forward(2)
            for m in range(KT):
                sp.wait_ge(x_scaled, 8 * 3 + m + 1)
                sp.dma_start(out[m, :, :], X[:, m, :]).then_inc(out_stored, 16)
            sp.wait_ge(out_stored, 16 * KT)

        @block.gpsimd
        def _(gp):
            gp.memset(ones[:, :], 1.0 / D).then_inc(memset_done, 1)
            gp.memset(onec[:, :], 1.0).then_inc(memset_done, 1)

            with gp.Fori(0, N_PANELS // 4) as it:
                for slot in range(4):
                    gp.wait_ge(split_hi, 4 * it + slot + 1)
                    gp.tensor_tensor(w_lo[:, slot, :], raw[:, slot % 2, :], w_hi[:, slot, :].bitcast(F32),
                                     ALU.subtract).then_inc(split_done, 1)

        @block.tensor
        def _(pe):
            def product(o_, wslot, kk, xh, xl, first, last):
                ws = slice(kk * P, (kk + 1) * P)
                pe.matmul(o_, w_hi[:, wslot, ws], xh, start=first, stop=False)
                pe.matmul(o_, w_hi[:, wslot, ws], xl, start=False, stop=False)
                return pe.matmul(o_, w_lo[:, wslot, ws], xh, start=False, stop=last)

            def panel_over_h(p, wslot, b, h_wait=None):
                pe.wait_ge(split_done, p + 1)
                for k in range(KT):
                    if h_wait is not None:
                        pe.wait_ge(h_split, h_wait + k + 1)
                    ins = product(bank(b), wslot, k, h_hi[:, k, :], h_lo[:, k, :], k == 0, k == KT - 1)
                ins.then_inc(panels_used, 1)

            def modulation_columns(chunks):
                n = 0
                for s in range(chunks):
                    for m in range(8):
                        ins = pe.matmul(psum[:, 6, n:n + 1], acc[:, s, m * P:(m + 1) * P],
                                        onec[:, 0:1], start=True, stop=True)
                        n += 1
                ins.then_inc(ada_cols, 1)

            def norm_stats(L):
                pe.wait_ge(s_added, 7 * (L + 1))
                pe.matmul(bank(6), ones[:, :], scr[:, 0, :], start=True, stop=True).then_inc(stats_ready, 1)
                pe.wait_ge(q_added, 7 * (L + 1))
                pe.matmul(bank(7), ones[:, :], scr[:, 1, :], start=True, stop=True).then_inc(stats_ready, 1)

            def feed_forward(n):
                base, cb = in_base(n), chunk_base(n)

                def chunk(it, c2, first=False):
                    c = 2 * it + c2
                    need(pe, hidden_made, cb + c - 1)
                    for gu in range(2):
                        panel_over_h(base + 2 * c + gu, 2 * c2 + gu, 2 * c2 + gu,
                                     (0 if n == 1 else 16) if first and gu == 0 else None)

                chunk(0, 0, True)
                chunk(0, 1)
                with pe.Fori(1, FT // 2) as it:
                    chunk(it, 0)
                    chunk(it, 1)
                ob = base + IN_PANELS
                pe.wait_ge(ada_used, ADA_BASE[n] + 8 * N_ADA[n])
                modulation_columns(N_ADA[n] // 2)
                pe.wait_ge(act_split, cb + FT)
                zb = 0 if n == 1 else 16

                def out_tiles(it):
                    for m4 in range(4):
                        m = 4 * it + m4
                        if not isinstance(it, int) or m >= 2:
                            pe.wait_ge(z_done, zb + m - 1)
                        k = 0
                        for j, kn in enumerate(OUT_SPLIT):
                            i = 3 * m4 + j
                            pe.wait_ge(split_done, ob + 12 * it + i + 1)
                            for kk in range(kn):
                                ins = product(bank(4 + m4 % 2), i % 4, kk, act_hi[:, k, :],
                                              act_lo[:, k, :], k == 0, k == FT - 1)
                                k += 1
                            ins.then_inc(panels_used, 1)

                out_tiles(0)
                out_tiles(1)
                pe.wait_ge(ada_taken, 2 if n == 1 else 4)
                norm_stats(1 if n == 1 else 3)

            pe.wait_ge(memset_done, 2)
            norm_stats(0)
            pe.wait_ge(ada_acc_start, KT)
            for s in range(2):
                for m in range(8):
                    ins = pe.matmul(psum[:, 5, 8 * s + m:8 * s + m + 1], acc[:, s, m * P:(m + 1) * P],
                                    onec[:, 0:1], start=True, stop=True)
            ins.then_inc(ada_cols, 1)
            feed_forward(1)

            pidx = {name: B_MIX + i for i, name in enumerate(MIX)}

            def k8_panel(name, h_wait=None):
                n = MIX8.index(name)
                b = n % 2
                if n in (2, 3):
                    pe.wait_ge(kv_blocks, 4 * (n - 1))
                if n > 3:
                    pe.wait_ge(act_evac, n - 3)
                p = pidx[name]
                panel_over_h(p, p % 4, b, h_wait)

            pe.wait_ge(const_landed, 16 * 4)
            k8_panel("kc", 8)
            for name in ("vc", "u0", "u1", "u2", "u3"):
                k8_panel(name)
            pe.wait_ge(mixc_landed, 16 * 5)
            pe.wait_ge(kv_blocks, 8)
            for kv in range(2):
                w1s = (w1k, w1v)[kv]
                for half in range(HID_T):
                    n = 2 * kv + half
                    for i in range(PAIRS):
                        src = blocks[:, 2 * kv + i // 8, :, :]
                        rhs = src[:, :, i:i + 8 * (N_CMP - 1) + 1:8]
                        ins = pe.matmul(psum[:, 2, 64 * n:64 * n + 62], w1s[:, i, half * P:(half + 1) * P],
                                        rhs, start=(i == 0), stop=(i == PAIRS - 1))
            ins.then_inc(cmp_hidden, 1)
            k8_panel("gate")
            k8_panel("q0")
            pe.wait_ge(cmp_act, 1)
            for g in range(GROUPS):
                for kt in range(HID_T):
                    pe.matmul(psum[64 * g:64 * g + 64, 3, 0:N_CMP], w2s[:, 0, kt, :],
                              hidden[:, kt, 31 * g:31 * g + 31], start=(kt == 0), stop=(kt == 1))
            for r in range(4):
                for g in range(GROUPS):
                    for kt in range(HID_T):
                        ins = pe.matmul(psum[32 * r:32 * r + 31, 3, 64 + 64 * g:128 + 64 * g],
                                        hidden[:, 2 + kt, 31 * g:31 * g + 31], w2s[:, 1, kt, :],
                                        start=(kt == 0), stop=(kt == 1))
            ins.then_inc(cmp_kv, 1)
            pe.wait_ge(act_evac, MIX8.index("gate") - 1)
            for t in range(TT):
                ins = pe.transpose(psum[:, 4, P * t:P * t + P], vT[:, 0, t * P:(t + 1) * P], ident[:, :])
            ins.then_inc(gates_T, 1)
            for name in ("q1", "q2", "q3"):
                k8_panel(name)
            pe.wait_ge(cmp_kv_taken, 2)
            pe.wait_ge(act_evac, MIX8.index("q3") - 1)
            for g in range(GROUPS):
                for t in range(TT):
                    for j in range(HPG):
                        col = (HPG * t + j) * N_CMP
                        ins = pe.matmul(psum[:, 6 + g, col:col + N_CMP],
                                        qT[64 * g:64 * g + 64, j, t * P:(t + 1) * P],
                                        kcT[64 * g:64 * g + 64, :], start=True, stop=True)
                ins.then_inc(cmp_scored, 1)
            k8_panel("kslc")
            k8_panel("kwin")
            p = pidx["poolw"]
            pe.wait_ge(split_done, p + 1)
            pe.wait_ge(pool_split, 4)
            pe.wait_ge(gates_taken, 1)
            for g in range(4):
                if g >= 2:
                    pe.wait_ge(poolout_split, g - 1)
                ins = product(bank(4 + g % 2), p % 4, g, pool_hi[:, g, :], pool_lo[:, g, :], True, True)
                if g < 3:
                    ins.then_inc(pool_mixed, 1)
            ins.then_inc(panels_used, 1)
            k8_panel("vslc")
            k8_panel("vwin")
            for v in range(2):
                pe.wait_ge(act_evac, MIX8.index("vslc") - 1 + v)
                for t in range(TT):
                    ins = pe.transpose(psum[:, 2 + v, P * t:P * t + P], vT[:, v, t * P:(t + 1) * P], ident[:, :])
                ins.then_inc(v_turned, 1)
            pe.wait_ge(cmp_probs, 1)
            pe.wait_ge(poolout_split, 4)
            for g in range(GROUPS):
                for t in range(TT):
                    ins = pe.transpose(psum[:, 4 + g, P * t:P * t + P],
                                       Pc[:, t, HPG * g:HPG * g + HPG, :].rearrange("p h n -> p (h n)"),
                                       ident[:, :])
                ins.then_inc(cmp_PT, 1)

            def scores(u):
                h, br = UNITS[u]
                j, g = h % HPG, h // HPG
                for t in range(TT):
                    n = 4 * u + t
                    if n >= 2:
                        pe.wait_ge(shifted, n - 1)
                    else:
                        pe.wait_ge(v_taken, n + 1)
                    w = P * (t + 1)
                    pe.matmul(bank(2 + n % 2, w), qT[64 * g:64 * g + 64, j, t * P:(t + 1) * P],
                              kT[64 * g:64 * g + 64, br, 0:w], start=True, stop=True).then_inc(scored, 1)

            def turn(u):
                pe.wait_ge(probs_ready, u + 1)
                for gi, kts in enumerate(PT_GROUPS):
                    n = 3 * u + gi
                    if n < 2:
                        pe.wait_ge(cmp_PT_taken, n + 1)
                    elif gi == 0:
                        pe.wait_ge(turned_dve, u)
                    elif gi == 1:
                        pe.wait_ge(turned_act, 2 * u)
                    else:
                        pe.wait_ge(turned_act, 2 * u + 1)
                    col = 0
                    for kt in kts:
                        for t in range(kt, TT):
                            src = Pr[:, u % 2, P_OFF[t] + kt * P:P_OFF[t] + (kt + 1) * P]
                            ins = pe.transpose(psum[:, 4 + n % 2, col:col + P], src, ident[:, :])
                            col += P
                    ins.then_inc(turned, 1)

            def weigh(u):
                h, br = UNITS[u]
                g = h // HPG
                b = 6 + h % 2
                if br == 0:
                    if h >= 2:
                        pe.wait_ge(o_split, h - 1)
                    r = 32 * (h % HPG)
                    pe.matmul(bank(b), VC[r:r + N_CMP, :], PcT[r:r + N_CMP, g, :],
                              start=True, stop=False)
                pe.wait_ge(turned_act, 2 * u + 2)
                pe.wait_ge(turned_dve, u + 1)
                for kt in range(TT):
                    w = T - kt * P
                    ins = pe.matmul(psum[:, b, kt * P:T], V[:, br, kt, :],
                                    PT[:, u % 2, PT_OFF[kt]:PT_OFF[kt] + w],
                                    start=False, stop=(br == 1 and kt == TT - 1))
                ins.then_inc(o_made, 1)

            for s in range(len(UNITS) + 2):
                if s < len(UNITS):
                    scores(s)
                if 1 <= s <= len(UNITS):
                    turn(s - 1)
                if s >= 2:
                    weigh(s - 2)

            for m in range(KT):
                p = B_BRANCH + 3 * m
                b = 4 * (m % 2)
                if m >= 2:
                    pe.wait_ge(br_mixed, m - 1)
                if m == 0:
                    pe.wait_ge(act_evac, 13)
                if m == 1:
                    pe.wait_ge(o_split, HEADS)
                panel_over_h(p, p % 4, b)
                panel_over_h(p + 1, (p + 1) % 4, b + 1)
                p += 2
                pe.wait_ge(split_done, p + 1)
                if m == 0:
                    pe.wait_ge(o_split, HEADS)
                for k in range(4):
                    product(bank(b + 2), p % 4, k, pool_hi[:, k, :], pool_lo[:, k, :], k == 0, k == 3)
                for k in range(4):
                    ins = product(bank(b + 3), p % 4, 4 + k, o_hi[:, k, :], o_lo[:, k, :], k == 0, k == 3)
                ins.then_inc(panels_used, 1)
            pe.wait_ge(br_mixed, KT)
            pe.wait_ge(ada_used, ADA_BASE["mix"] + 8 * N_ADA["mix"])
            modulation_columns(3)
            for m in range(KT):
                p = B_MIXOUT + m
                if m >= 2:
                    pe.wait_ge(z_done, 8 + m - 1)
                pe.wait_ge(split_done, p + 1)
                for k in range(KT):
                    if m == 0:
                        pe.wait_ge(br_split, k + 1)
                    ins = product(bank(4 + m % 2), p % 4, k, mixed_hi[:, k, :], mixed_lo[:, k, :],
                                  k == 0, k == KT - 1)
                ins.then_inc(panels_used, 1)
            pe.wait_ge(ada_taken, 3)
            norm_stats(2)
            feed_forward(2)

        @block.scalar
        def _(act):
            chain = [0]

            def link(ins):
                chain[0] += 1
                ins.then_inc(act_chain, 1)
                act.wait_ge(act_chain, chain[0])

            def split(p, slot, filled):
                act.wait_ge(raw_landed[slot % 2], 16 * filled)
                need(act, panels_used, p - 3)
                act.activation(w_hi[:, slot, :], raw[:, slot % 2, :], ACT.Copy).then_inc(split_hi, 1)

            todo = [0]

            def split_before(used):
                while todo[0] < min(used + 3, N_PANELS):
                    p = todo[0]
                    split(p, p % 4, p // 2 + 1)
                    todo[0] += 1

            def wait_used(used):
                split_before(used)
                act.wait_ge(panels_used, used)

            def square(L, m):
                if L == 0:
                    if m % 2 == 0:
                        act.wait_ge(x_landed[m // 2], 16)
                else:
                    act.wait_ge(z_done, 8 * (L - 1) + m + 1)
                if m >= 2:
                    act.wait_ge(q_added, 7 * L + max(m - 2, 1))
                elif L:
                    act.wait_ge(h_split, 8 * L)
                act.activation(scr[:, 2 + m % 2, :], X[:, m, :], ACT.Square).then_inc(sq_done, 1)

            def norm(L):
                act.wait_ge(stats_ready, 2 * L + 2)
                act.activation(scr[:, 0, :], bank(6), ACT.Square).then_inc(mean_sq, 1)
                act.wait_ge(var_done, L + 1)
                act.activation(scr[:, 0, :], scr[:, 1, :], ACT.Sqrt).then_inc(std_done, 1)
                if L == 0:
                    split_before(0)
                act.wait_ge(mod_ready, L + 1)
                if L < 3:
                    def make_h(m):
                        act.wait_ge(xhat_done, 8 * L + m + 1)
                        if m >= 2:
                            act.wait_ge(h_split, 8 * L + m - 1)
                        act.activation(scr[:, 2 + m % 2, :], X[:, m, :], ACT.Identity,
                                       bias=mod[:, 1, m:m + 1], scale=mod[:, 0, m:m + 1]).then_inc(h_made, 1)

                    make_h(0)
                    for m in range(KT):
                        if m + 1 < KT:
                            make_h(m + 1)
                        act.wait_ge(h_made, 8 * L + m + 1)
                        act.activation(h_hi[:, m, :], scr[:, 2 + m % 2, :], ACT.Copy).then_inc(h_hi_done, 1)
                for m in range(KT):
                    act.wait_ge(xhat_done, 8 * L + m + 1)
                    act.activation(X[:, m, :], X[:, m, :], ACT.Identity,
                                   bias=mod[:, 3, m:m + 1], scale=mod[:, 2, m:m + 1]).then_inc(x_scaled, 1)

            def feed_forward(n):
                base, cb = in_base(n), chunk_base(n)

                def chunk(it, c2):
                    c = 2 * it + c2
                    if not (isinstance(c, int) and c == 0):
                        act.wait_ge(hidden_made, cb + c)
                        act.activation(act_hi[:, c - 1, :] if isinstance(c, int) else
                                       act_hi[:, bass.ds(c - 1, 1), :].rearrange("p o t -> p (o t)"),
                                       scr[:, 1 - c2, :], ACT.Copy).then_inc(act_hi_done, 1)
                    split(base + 2 * c + 3, (2 * c2 + 3) % 4, base // 2 + c + 2)
                    act.wait_ge(panels_used, base + 2 * c + 1)
                    need(act, act_split, cb + c - 1)
                    act.activation(scr[:, c2, :], bank(2 * c2), ACT.Tanh, scale=0.5).then_inc(tanh_done, 1)
                    split(base + 2 * c + 4, 2 * c2, base // 2 + c + 3)

                assert todo[0] == base + 3
                chunk(0, 0)
                chunk(0, 1)
                with act.Fori(1, FT // 2) as it:
                    chunk(it, 0)
                    chunk(it, 1)
                todo[0] = base + IN_PANELS + 3
                act.wait_ge(hidden_made, cb + FT)
                act.activation(act_hi[:, FT - 1, :], scr[:, (FT - 1) % 2, :], ACT.Copy).then_inc(act_hi_done, 1)

            act.dma_start(colv[:, :], cols[:, :]).then_inc(cols_landed, 16)
            act.dma_start(ident[:, :], ident_in[:, :]).then_inc(const_landed, 16)
            act.dma_start(posv[:, :, :], pos[:, :, :]).then_inc(const_landed, 16)
            act.dma_start(w2s[:, :, :, :], w2[:, :, :, :]).then_inc(const_landed, 16)
            act.dma_start(icnt[:, :, :], icnt_in[:, :, :]).then_inc(const_landed, 16)
            act.wait_ge(cols_landed, 16)
            act.activation(cact[:, :], colv[:, C_C:C_C + 8], ACT.Tanh, scale=0.5).then_inc(c_tanh, 1)
            for m in range(KT):
                square(0, m)
            norm(0)
            feed_forward(1)
            for m in range(KT):
                split_before(B_FFN1 + IN_PANELS + 3 * m + 3)
                square(1, m)
            act.wait_ge(panels_used, B_MIX)
            act.dma_start(w1k[:, :, :], w1[0, :, :, :]).then_inc(mixc_landed, 16)
            act.dma_start(w1v[:, :, :], w1[1, :, :, :]).then_inc(mixc_landed, 16)
            act.dma_start(cbias[:, :, :, :], cbias_in[:, :, :, :]).then_inc(mixc_landed, 16)
            act.dma_start(cmask[:, :, :], cmask_in[:, :, :]).then_inc(mixc_landed, 16)
            act.dma_start(dist[:, :], dist_in[:, :]).then_inc(mixc_landed, 16)
            norm(1)

            def taken(name):
                return B_MIX + MIX.index(name) + 1

            def k8_bank(name):
                return MIX8.index(name) % 2

            for g in range(4):
                wait_used(taken(f"u{g}"))
                if g == 0:
                    act.wait_ge(pool_delta, 1)
                if g >= 2:
                    act.wait_ge(pool_delta, g)
                act.activation(pads[:, g % 2, 16:528], bank(k8_bank(f"u{g}")), ACT.Copy).then_inc(act_evac, 1)
                if g >= 1:
                    act.wait_ge(pool_delta, g + 1)
                    act.activation(pool_hi[:, g - 1, :], pads[:, 2 + (g - 1) % 2, 16:528],
                                   ACT.Copy).then_inc(pool_hi_done, 1)
            act.wait_ge(pool_delta, 5)
            act.activation(pool_hi[:, 3, :], pads[:, 3, 16:528], ACT.Copy).then_inc(pool_hi_done, 1)
            wait_used(taken("gate"))
            act.activation(vT[:, 0, :], bank(k8_bank("gate")), ACT.Tanh, scale=0.5).then_inc(act_evac, 1)
            act.wait_ge(cmp_hidden, 1)
            hb = psum[:, 2, 0:256].rearrange("p (n c) -> p n c", c=64)[:, :, 0:62]
            sq = vT[:, 1, 0:248].rearrange("p (n c) -> p n c", c=62)
            act.activation(sq, hb, ACT.Square).then_inc(cmp_sq, 1)
            wait_used(taken("q0"))
            act.activation(qT[:, 0, :], bank(k8_bank("q0")), ACT.Copy, scale=HEAD ** -0.5).then_inc(act_evac, 1)
            act.wait_ge(cmp_arg, 1)
            act.activation(sq, sq, ACT.Tanh, scale=GELU_A).then_inc(cmp_tanh, 1)
            for j in range(1, 4):
                wait_used(taken(f"q{j}"))
                act.activation(qT[:, j, :], bank(k8_bank(f"q{j}")), ACT.Copy, scale=HEAD ** -0.5).then_inc(act_evac, 1)
            act.wait_ge(cmp_shifted, 1)
            act.activation(Pc[:, :, :, 0:N_CMP], Pc[:, :, :, 0:N_CMP], ACT.Exp).then_inc(cmp_exp, 1)
            for br, name in enumerate(("kslc", "kwin")):
                wait_used(taken(name))
                act.activation(kT[:, br, :], bank(k8_bank(name)), ACT.Copy).then_inc(act_evac, 1)
            for g in range(4):
                act.wait_ge(pool_mixed, g + 1) if g < 3 else wait_used(taken("poolw"))
                act.activation(pool_hi[:, g, :], bank(4 + g % 2), ACT.Copy,
                               scale=colv[:, C_PSCALE + g:C_PSCALE + g + 1]).then_inc(poolout_hi, 1)
            for v, name in enumerate(("vslc", "vwin")):
                wait_used(taken(name))
                act.activation(vT[:, v, :], bank(k8_bank(name)), ACT.Copy).then_inc(act_evac, 1)

            def exps(u):
                for t in range(TT):
                    n = 4 * u + t
                    act.wait_ge(shifted, n + 1)
                    pr = Pr[:, u % 2, P_OFF[t]:P_OFF[t] + P * (t + 1)]
                    act.activation(pr, pr, ACT.Exp, bias=nmax[:, n:n + 1], scale=-1.0,
                                   accum_out=psumv[:, n:n + 1]).then_inc(exp_done, 1)

            def take_turned(u):
                if u >= 2:
                    act.wait_ge(o_made, u - 1)
                for gi in (0, 2):
                    n = 3 * u + gi
                    act.wait_ge(turned, n + 1)
                    w = 512 if gi == 0 else 384
                    off = PT_OFF[PT_GROUPS[gi][0]]
                    act.activation(PT[:, u % 2, off:off + w], bank(4 + n % 2, w), ACT.Copy).then_inc(turned_act, 1)

            def take_head(h):
                j, g = h % HPG, h // HPG
                act.wait_ge(o_made, 2 * h + 2)
                act.activation(o_hi[64 * g:64 * g + 64, j, :], psum[64 * g:64 * g + 64, 6 + h % 2, :],
                               ACT.Copy).then_inc(o_hi_done, 1)

            split_before(B_BRANCH + 1)
            for s in range(len(UNITS) + 2):
                if s < len(UNITS):
                    exps(s)
                if 1 <= s <= len(UNITS):
                    take_turned(s - 1)
                if s >= 2 and UNITS[s - 2][1] == 1:
                    take_head(UNITS[s - 2][0])

            for m in range(KT):
                b = 4 * (m % 2)
                for q in range(2):
                    wait_used(B_BRANCH + 3 * m + q + 1)
                    if m >= 2 and q == 0:
                        act.wait_ge(br_split, m - 1)
                    act.activation(tab[:, m % 2, q, :], bank(b + q), ACT.Tanh, scale=0.5).then_inc(br_tanh, 1)
                act.wait_ge(br_mixed, m + 1)
                act.activation(mixed_hi[:, m, :], tab[:, m % 2, 0, :], ACT.Copy).then_inc(br_hi, 1)
            for m in range(KT):
                split_before(B_MIXOUT + m + 1)
                square(2, m)
            norm(2)
            feed_forward(2)
            for m in range(KT):
                split_before(B_FFN2 + IN_PANELS + 3 * m + 3)
                square(3, m)
            norm(3)

        @block.vector
        def _(dve):
            chain = [0]

            def link(ins):
                chain[0] += 1
                ins.then_inc(dve_chain, 1)
                dve.wait_ge(dve_chain, chain[0])

            def sums(L, m):
                if L == 0 and m % 2 == 0:
                    dve.wait_ge(x_landed[m // 2], 16)
                if m == 0:
                    return
                if m > 1:
                    dve.wait_ge(s_added, 7 * L + m - 1)
                elif L:
                    dve.wait_ge(z_done, 8 * (L - 1) + m + 1)
                if L and m > 1:
                    dve.wait_ge(z_done, 8 * (L - 1) + m + 1)
                a = X[:, 0, :] if m == 1 else scr[:, 0, :]
                dve.tensor_tensor(scr[:, 0, :], a, X[:, m, :], ALU.add).then_inc(s_added, 1)

            def squares(L, m):
                if m == 0:
                    return
                dve.wait_ge(sq_done, 8 * L + m + 1)
                if m > 1:
                    dve.wait_ge(q_added, 7 * L + m - 1)
                a = scr[:, 2, :] if m == 1 else scr[:, 1, :]
                dve.tensor_tensor(scr[:, 1, :], a, scr[:, 2 + m % 2, :], ALU.add).then_inc(q_added, 1)

            def modulation(src_bank, chunk, n):
                w = 8 * n
                dve.tensor_tensor(ada[:, 8 * chunk:8 * chunk + w], psum[:, src_bank, 0:w],
                                  colv[:, C_BADA + 8 * chunk:C_BADA + 8 * chunk + w],
                                  ALU.add).then_inc(ada_taken, 1)

            def norm_columns(L):
                g = colv[:, C_LNG + 8 * L:C_LNG + 8 * L + 8]
                b = colv[:, C_LNB + 8 * L:C_LNB + 8 * L + 8]
                if L < 3:
                    sh = ada[:, 24 * L:24 * L + 8]
                    sc = ada[:, 24 * L + 8:24 * L + 16]
                    link(dve.tensor_scalar(mod[:, 5, :], sc, 1.0, None, ALU.add))
                    dve.tensor_tensor(mod[:, 0, :], mod[:, 5, :], g, ALU.mult)
                    link(dve.tensor_tensor(mod[:, 1, :], mod[:, 5, :], b, ALU.mult))
                    dve.tensor_scalar(mod[:, 2, :], g, ALPHA, None, ALU.mult)
                    dve.tensor_scalar(mod[:, 3, :], b, ALPHA, None, ALU.mult)
                    dve.tensor_tensor(mod[:, 1, :], mod[:, 1, :], sh, ALU.add).then_inc(mod_ready, 1)
                else:
                    dve.tensor_scalar(mod[:, 2, :], g, 1.0, None, ALU.mult)
                    dve.tensor_scalar(mod[:, 3, :], b, 1.0, None, ALU.mult).then_inc(mod_ready, 1)

            def norm(L):
                dve.wait_ge(stats_ready, 2 * L + 2)
                dve.wait_ge(mean_sq, L + 1)
                link(dve.tensor_tensor(scr[:, 1, :], bank(7), scr[:, 0, :], ALU.subtract))
                dve.tensor_scalar(scr[:, 1, :], scr[:, 1, :], 0.0, EPS, ALU.max, ALU.add).then_inc(var_done, 1)

                def center(m):
                    dve.tensor_tensor(X[:, m, :], X[:, m, :], bank(6), ALU.subtract).then_inc(centered, 1)

                def split(m):
                    dve.wait_ge(h_hi_done, 8 * L + m + 1)
                    dve.tensor_tensor(h_lo[:, m, :], scr[:, 2 + m % 2, :],
                                      h_hi[:, m, :].bitcast(F32), ALU.subtract).then_inc(h_split, 1)

                center(0)
                center(1)
                dve.wait_ge(std_done, L + 1)
                link(dve.reciprocal(scr[:, 1, :], scr[:, 0, :]))
                for m in range(KT):
                    if m + 2 < KT:
                        center(m + 2)
                    dve.wait_ge(centered, 8 * L + m + 1)
                    dve.tensor_tensor(X[:, m, :], X[:, m, :], scr[:, 1, :], ALU.mult).then_inc(xhat_done, 1)
                    if L < 3 and m >= 1:
                        split(m - 1)
                if L < 3:
                    split(KT - 1)

            def ada_unit(phase, step, q):
                u = ADA_BASE[phase] + N_ADA[phase] * step + q
                dve.wait_ge(ada_landed[q % 3], 16 * ada_slot_count(phase, step, q))
                a = acc[:, q // 2, (q % 2) * 512:(q % 2) * 512 + 512]
                if isinstance(step, int):
                    sc = cact[:, step:step + 1]
                else:
                    sc = cact[:, bass.ds(step, 1)]
                if isinstance(step, int) and step == 0:
                    dve.tensor_scalar(a, ada_raw[:, q % 3, :], sc, None, ALU.mult).then_inc(ada_used, 1)
                else:
                    dve.wait_ge(ada_used, u - N_ADA[phase] + 1)
                    dve.scalar_tensor_tensor(a, ada_raw[:, q % 3, :], sc, a, ALU.mult, ALU.add).then_inc(ada_used, 1)

            def feed_forward(n):
                base, cb = in_base(n), chunk_base(n)

                def lo(c, b):
                    dve.wait_ge(act_hi_done, cb + c + 1)
                    if isinstance(c, int):
                        hi, lo_ = act_hi[:, c, :], act_lo[:, c, :]
                    else:
                        hi = act_hi[:, bass.ds(c, 1), :].rearrange("p o t -> p (o t)")
                        lo_ = act_lo[:, bass.ds(c, 1), :].rearrange("p o t -> p (o t)")
                    dve.tensor_tensor(lo_, scr[:, b, :], hi.bitcast(F32), ALU.subtract).then_inc(act_split, 1)

                def chunk(it, c2, with_ada):
                    c = 2 * it + c2
                    if not (isinstance(c, int) and c == 0):
                        lo(c - 1, 1 - c2)
                    dve.wait_ge(tanh_done, cb + c + 1)
                    dve.scalar_tensor_tensor(scr[:, c2, :], scr[:, c2, :], 1.0, bank(2 * c2),
                                             ALU.add, ALU.mult).then_inc(gated, 1)
                    if with_ada:
                        per = N_ADA[n] // 2
                        for q in range(per * c2, per * c2 + per):
                            ada_unit(n, it, q)
                    dve.wait_ge(gated, cb + c + 1)
                    dve.wait_ge(panels_used, base + 2 * c + 2)
                    dve.tensor_tensor(scr[:, c2, :], scr[:, c2, :], bank(2 * c2 + 1), ALU.mult).then_inc(hidden_made, 1)

                chunk(0, 0, True)
                chunk(0, 1, True)
                with dve.Fori(1, KT) as it:
                    chunk(it, 0, True)
                    chunk(it, 1, True)
                with dve.Fori(KT, FT // 2) as it:
                    chunk(it, 0, False)
                    chunk(it, 1, False)
                lo(FT - 1, (FT - 1) % 2)

            def residual(L, gate_chunk, factor, used):
                dve.wait_ge(ada_cols, {1: 2, 2: 3, 3: 4}[L])
                modulation(6, {1: 2, 2: 5, 3: 8}[L], 1 if L == 3 else 3)
                dve.wait_ge(ada_taken, {1: 2, 2: 3, 3: 4}[L])
                link(dve.tensor_scalar(mod[:, 4, :], ada[:, 8 * gate_chunk:8 * gate_chunk + 8], factor, None, ALU.mult))
                norm_columns(L)
                for m in range(KT):
                    dve.wait_ge(panels_used, used(m))
                    dve.wait_ge(x_scaled, 8 * (L - 1) + m + 1)
                    dve.scalar_tensor_tensor(X[:, m, :], bank(4 + m % 2), mod[:, 4, m:m + 1], X[:, m, :],
                                             ALU.mult, ALU.add).then_inc(z_done, 1)
                    if m >= 1:
                        squares(L, m - 1)
                    sums(L, m)
                squares(L, KT - 1)

            dve.wait_ge(c_tanh, 1)
            link(dve.scalar_tensor_tensor(cact[:, :], cact[:, :], 1.0, colv[:, C_C:C_C + 8], ALU.add, ALU.mult))
            link(dve.tensor_scalar(cact[:, :], cact[:, :], 0.5, None, ALU.mult))
            a01 = acc[:, 0:2, :].rearrange("p s c -> p (s c)")
            for m in range(KT):
                sums(0, m)
                if m >= 1:
                    squares(0, m)
            for k in range(KT):
                dve.wait_ge(ada0_landed[k], 16)
                if k == 0:
                    dve.tensor_scalar(a01, ada_start[:, 0, :], cact[:, 0:1], None, ALU.mult).then_inc(ada_acc_start, 1)
                else:
                    dve.wait_ge(ada_acc_start, k)
                    dve.scalar_tensor_tensor(a01, ada_start[:, k, :], cact[:, k:k + 1], a01,
                                             ALU.mult, ALU.add).then_inc(ada_acc_start, 1)
            dve.wait_ge(ada_cols, 1)
            modulation(5, 0, 2)
            dve.wait_ge(ada_taken, 1)
            norm_columns(0)
            norm(0)
            feed_forward(1)
            ob1 = B_FFN1 + IN_PANELS
            residual(1, 2, 0.25, lambda m: ob1 + 3 * m + 3)
            norm(1)

            def taken(name):
                return B_MIX + MIX.index(name) + 1

            for i in range(4):
                ins = dve.memset(pads[:, i, 0:16], 0.0)
            ins.then_inc(pool_delta, 1)
            dve.memset(Pc[:, :, :, N_CMP:CPAD], 0.0)
            for kv, name in enumerate(("kc", "vc")):
                dve.wait_ge(panels_used, taken(name))
                for half in range(2):
                    for r in range(2):
                        for g in range(GROUPS):
                            src = psum[64 * g:64 * g + 64, kv, r:T:2].rearrange("p (n i) -> p n i", i=8)
                            dst = blocks[64 * r:64 * r + 64, 2 * kv + half, g, :].rearrange("p (n i) -> p n i", i=8)
                            pp = posv[64 * r:64 * r + 64, kv:kv + 1, 8 * half:8 * half + 8].broadcast_to([64, 32, 8])
                            ins = dve.tensor_tensor(dst, src, pp, ALU.add)
                            if r == 1:
                                ins.then_inc(kv_blocks, 1)
            for g, w in enumerate(WINDOWS):
                dve.wait_ge(act_evac, g + 1)
                u = pads[:, g % 2, :]
                s = pads[:, 2 + g % 2, :]
                if g >= 2:
                    dve.wait_ge(pool_split, g - 1)
                link(dve.tensor_tensor(s[:, 1:528], u[:, 1:528], u[:, 0:527], ALU.add))
                step = 2
                cur, oth = s, scr[:, 2:4, :].rearrange("p a t -> p (a t)")
                while step < w:
                    lo_ = 2 * step - 1
                    link(dve.tensor_tensor(oth[:, lo_:528], cur[:, lo_:528], cur[:, lo_ - step:528 - step], ALU.add))
                    cur, oth = oth, cur
                    step *= 2
                head = cst[:, g % 2, 0:16]
                link(dve.tensor_tensor(head, cur[:, 16:32], icnt[:, g, :], ALU.mult))
                link(dve.scalar_tensor_tensor(s[:, 16:528], cur[:, 16:528], 1.0 / w, u[:, 16:528],
                                              ALU.mult, ALU.subtract))
                dve.tensor_tensor(s[:, 16:32], head, u[:, 16:32], ALU.subtract).then_inc(pool_delta, 1)
                if g >= 1:
                    dve.wait_ge(pool_hi_done, g)
                    dve.tensor_tensor(pool_lo[:, g - 1, :], pads[:, 2 + (g - 1) % 2, 16:528],
                                      pool_hi[:, g - 1, :].bitcast(F32), ALU.subtract).then_inc(pool_split, 1)
            dve.wait_ge(pool_hi_done, 4)
            dve.tensor_tensor(pool_lo[:, 3, :], pads[:, 3, 16:528],
                              pool_hi[:, 3, :].bitcast(F32), ALU.subtract).then_inc(pool_split, 1)
            hb = psum[:, 2, 0:256].rearrange("p (n c) -> p n c", c=64)[:, :, 0:62]
            sq = vT[:, 1, 0:248].rearrange("p (n c) -> p n c", c=62)
            dve.wait_ge(cmp_sq, 1)
            link(dve.tensor_scalar(sq, sq, GELU_B, 1.0, ALU.mult, ALU.add))
            dve.tensor_tensor(sq, sq, hb, ALU.mult).then_inc(cmp_arg, 1)
            dve.wait_ge(cmp_tanh, 1)
            dve.scalar_tensor_tensor(hidden[:, :, :], sq, 1.0, hb, ALU.add, ALU.mult).then_inc(cmp_act, 1)
            dve.wait_ge(cmp_kv, 1)
            dve.tensor_scalar(kcT[:, :], psum[:, 3, 0:N_CMP], 0.5, None, ALU.mult).then_inc(cmp_kv_taken, 1)
            for r in range(4):
                ins = dve.tensor_scalar(VC[32 * r:32 * r + 31, :], psum[32 * r:32 * r + 31, 3, 64:192], 0.5, None, ALU.mult)
            ins.then_inc(cmp_kv_taken, 1)
            dve.wait_ge(gates_T, 1)
            gt = psum[:, 4, :].rearrange("p (t c) -> p t c", c=P)[:, :, 0:24]
            dve.tensor_scalar(G[:, :, :], gt, 0.5, 0.5, ALU.mult, ALU.add).then_inc(gates_taken, 1)
            Pv = Pc[:, :, :, 0:N_CMP]
            dve.wait_ge(mixc_landed, 16 * 5)
            for i in range(2):
                dve.wait_ge(cmp_scored, i + 1)
                src = psum[:, 6 + i, 0:496].rearrange("p (t h n) -> p t h n", t=TT, n=N_CMP)
                hs = slice(HPG * i, HPG * i + HPG)
                last = dve.tensor_tensor(Pc[:, :, hs, 0:N_CMP], src, cbias[:, :, hs, :], ALU.add)
            link(last)
            link(dve.tensor_reduce(cst[:, 0, :], Pv, AX.X, ALU.max))

            def over_blocks(v, t):
                return v[:, 8 * t:8 * t + 8].rearrange("p (h o) -> p h o", o=1).broadcast_to([P, 8, N_CMP])

            for t in range(TT):
                ins = dve.tensor_tensor(Pc[:, t, :, 0:N_CMP], Pc[:, t, :, 0:N_CMP], over_blocks(cst[:, 0, :], t), ALU.subtract)
            ins.then_inc(cmp_shifted, 1)
            dve.wait_ge(cmp_exp, 1)
            link(dve.tensor_reduce(cst[:, 1, :], Pv, AX.X, ALU.add))
            link(dve.reciprocal(cst[:, 1, :], cst[:, 1, :]))
            dve.wait_ge(gates_taken, 1)
            link(dve.tensor_tensor(cst[:, 2, :].rearrange("p (t h) -> p t h", t=TT),
                                   cst[:, 1, :].rearrange("p (t h) -> p t h", t=TT), G[:, :, 0:24:3], ALU.mult))
            for t in range(TT):
                ins = dve.tensor_tensor(Pc[:, t, :, 0:N_CMP], Pc[:, t, :, 0:N_CMP], over_blocks(cst[:, 2, :], t), ALU.mult)
            link(ins)
            for t in range(TT):
                ins = dve.tensor_tensor(Pc[:, t, :, 0:N_CMP], Pc[:, t, :, 0:N_CMP],
                                        cmask[:, t:t + 1, 0:N_CMP].broadcast_to([P, 8, N_CMP]), ALU.mult)
            ins.then_inc(cmp_probs, 1)
            for g in range(4):
                dve.wait_ge(poolout_hi, g + 1)
                dve.scalar_tensor_tensor(pool_lo[:, g, :], bank(4 + g % 2), colv[:, C_PSCALE + g:C_PSCALE + g + 1],
                                         pool_hi[:, g, :].bitcast(F32), ALU.mult, ALU.subtract).then_inc(poolout_split, 1)
            for v in range(2):
                dve.wait_ge(v_turned, v + 1)
                dve.tensor_copy(V[:, v, :, :].rearrange("p t c -> p (t c)"), bank(2 + v)).then_inc(v_taken, 1)
            for g in range(GROUPS):
                dve.wait_ge(cmp_PT, g + 1)
                dve.tensor_copy(PcT[:, g, :], bank(4 + g)).then_inc(cmp_PT_taken, 1)

            def alibi(h):
                dve.tensor_scalar(abias[:, h % 2, :], dist[:, :], 2.0 ** -(h + 1), None, ALU.mult).then_inc(bias_made, 1)

            def shift(u):
                h, br = UNITS[u]
                if br == 0:
                    alibi(h)
                dve.wait_ge(bias_made, h + 1)
                if u >= 2:
                    dve.wait_ge(turned, 3 * (u - 1))
                for t in range(TT):
                    n = 4 * u + t
                    w = P * (t + 1)
                    dve.wait_ge(scored, n + 1)
                    dve.tensor_tensor_reduce(Pr[:, u % 2, P_OFF[t]:P_OFF[t] + w], bank(2 + n % 2, w),
                                             abias[:, h % 2, T - w:T], -1.0, 1e30, ALU.add, ALU.min,
                                             nmax[:, n:n + 1]).then_inc(shifted, 1)

            def normalize(u):
                h, br = UNITS[u]
                dve.wait_ge(exp_done, 4 * u + 4)
                s4 = slice(4 * u, 4 * u + 4)
                link(dve.reciprocal(pscl[:, s4], psumv[:, s4]))
                link(dve.tensor_tensor(pscl[:, s4], pscl[:, s4], G[:, :, 3 * h + 1 + br], ALU.mult))
                for t in range(TT):
                    n = 4 * u + t
                    pr = Pr[:, u % 2, P_OFF[t]:P_OFF[t] + P * (t + 1)]
                    ins = dve.tensor_scalar(pr, pr, pscl[:, n:n + 1], None, ALU.mult)
                ins.then_inc(probs_ready, 1)

            def take_turned(u):
                n = 3 * u + 1
                if u >= 2:
                    dve.wait_ge(o_made, u - 1)
                dve.wait_ge(turned, n + 1)
                off = PT_OFF[1]
                dve.tensor_copy(PT[:, u % 2, off:off + 384], bank(4 + n % 2, 384)).then_inc(turned_dve, 1)

            def take_head(h):
                j, g = h % HPG, h // HPG
                dve.wait_ge(o_hi_done, h + 1)
                rows = slice(64 * g, 64 * g + 64)
                dve.tensor_tensor(o_lo[rows, j, :], psum[rows, 6 + h % 2, :], o_hi[rows, j, :].bitcast(F32),
                                  ALU.subtract).then_inc(o_split, 1)

            for s in range(len(UNITS) + 2):
                if s < len(UNITS):
                    shift(s)
                if 1 <= s <= len(UNITS):
                    take_turned(s - 1)
                if s < len(UNITS):
                    normalize(s)
                if s >= 2 and UNITS[s - 2][1] == 1:
                    take_head(UNITS[s - 2][0])

            def mixed_lo_part(m):
                dve.wait_ge(br_hi, m + 1)
                dve.tensor_tensor(mixed_lo[:, m, :], tab[:, m % 2, 0, :], mixed_hi[:, m, :].bitcast(F32),
                                  ALU.subtract).then_inc(br_split, 1)

            for m in range(KT):
                b = 4 * (m % 2)
                for q in range(6):
                    ada_unit("mix", m, q)
                dve.wait_ge(panels_used, B_BRANCH + 3 * m + 3)
                for q in range(2):
                    dve.wait_ge(br_tanh, 2 * m + q + 1)
                    dve.scalar_tensor_tensor(tab[:, m % 2, q, :], tab[:, m % 2, q, :], 1.0, bank(b + 2 + q),
                                             ALU.add, ALU.mult).then_inc(br_gated, 1)
                dve.wait_ge(br_gated, 2 * m + 2)
                dve.tensor_tensor(tab[:, m % 2, 0, :], tab[:, m % 2, 0, :], tab[:, m % 2, 1, :],
                                  ALU.add).then_inc(br_mixed, 1)
                mixed_lo_part(m)
            residual(2, 5, 0.5, lambda m: B_MIXOUT + m + 1)
            norm(2)
            feed_forward(2)
            ob2 = B_FFN2 + IN_PANELS
            residual(3, 8, 0.25, lambda m: ob2 + 3 * m + 3)
            norm(3)


def _tiles(w):
    K, N = w.shape
    return np.ascontiguousarray(w.reshape(K // P, P, N // P, P).transpose(2, 1, 0, 3)).reshape(N // P, P, K)


def _constants():
    p = np.arange(P)[:, None]
    rel = np.arange(T)[None, :] - (T - P)
    dist = np.where(rel > p, -1e34, -(p - rel)).astype(np.float32)
    t = np.arange(T)
    end = np.arange(N_CMP) * STRIDE + 2 * STRIDE - 1
    d = t[:, None] - end[None, :]
    slopes = 2.0 ** -np.arange(1.0, HEADS + 1)
    cb = np.where(d[:, None, :] < 0, NEG, -slopes[None, :, None] * d[:, None, :]).astype(np.float32)
    cb = cb.reshape(TT, P, HEADS, N_CMP).transpose(1, 0, 2, 3)
    cm = np.zeros((T, CPAD), np.float32)
    cm[:, :N_CMP] = d >= 0
    cm = cm.reshape(TT, P, CPAD).transpose(1, 0, 2)
    ic = np.stack([1.0 / np.minimum(np.arange(16) + 1, w) for w in WINDOWS]).astype(np.float32)
    return {"ident": np.eye(P, dtype=np.float32), "dist": dist, "cbias": np.ascontiguousarray(cb),
            "cmask": np.ascontiguousarray(cm), "icnt": np.ascontiguousarray(np.broadcast_to(ic, (P, 4, 16)))}


def _mixer_columns():
    q0, kv0, g0 = 512, 1024, 1792
    br0 = g0 + 24
    at = {f"u{g}": np.arange(P) + P * g for g in range(4)}
    for j in range(4):
        at[f"q{j}"] = np.concatenate([np.arange(64) + q0 + 64 * j, np.arange(64) + q0 + 64 * (4 + j)])
    for i, n in enumerate(("kc", "vc", "kslc", "vslc", "kwin", "vwin")):
        at[n] = np.arange(P) + kv0 + P * i
    at["gate"] = np.concatenate([np.arange(24) + g0, np.full(P - 24, -1)])
    order = [at[n] for n in MIX8]
    for m in range(KT):
        order += [np.arange(P) + br0 + P * m, np.arange(P) + br0 + D + P * m]
    return np.concatenate(order)


def kernel(**inputs):
    import concourse.bacc as _bacc
    from concourse.bass_utils import run_bass_kernel_spmd as _run

    a = {k: np.asarray(v) for k, v in inputs.items()}

    def column(v):
        return v.reshape(-1, P).T

    arrays = {}
    arrays["xT"] = np.ascontiguousarray(a["x"][0].T.reshape(KT, P, T).transpose(1, 0, 2))
    arrays["cols"] = np.ascontiguousarray(np.concatenate(
        [column(a["b_ada"][0])] + [column(v) for v in (a["ln_in_g"], a["ln1_g"][0], a["ln2_g"][0], a["ln3_g"][0],
                                                      a["ln_in_b"], a["ln1_b"][0], a["ln2_b"][0], a["ln3_b"][0])]
        + [column(a["pool_scale"][0]), column(a["c"][0])], axis=1))
    arrays["ada_w"] = np.ascontiguousarray(a["w_ada"][0]).reshape(KT, P, 9 * D)

    def ffn_in(w):
        return np.stack([_tiles(w[:, :F]), _tiles(w[:, F:])], axis=1)

    arrays["ffn_in"] = np.stack([ffn_in(a["ffn1_w_in"][0]), ffn_in(a["ffn2_w_in"][0])])
    arrays["ffn_out"] = np.stack([_tiles(a["ffn1_w_out"][0]), _tiles(a["ffn2_w_out"][0])])
    cols = _mixer_columns()
    padded = np.concatenate([a["w_mix_in"][0], np.zeros((D, 1), np.float32)], axis=1)
    arrays["mix_w"] = _tiles(padded[:, cols])
    arrays["pool_w"] = np.ascontiguousarray(a["pool_w"][0].transpose(1, 0, 2)).reshape(P, 4 * P)
    heads = np.concatenate([np.concatenate([np.arange(64) + 64 * j, np.arange(64) + 64 * (4 + j)]) for j in range(4)])
    arrays["branch_w"] = np.concatenate([_tiles(a["w_branch_a"][0]), _tiles(a["w_branch_b"][0][heads])], axis=2)
    arrays["mixout_w"] = _tiles(a["w_mix_out"][0])
    arrays["w1"] = np.stack([a[n][0].reshape(PAIRS, P, 256).transpose(1, 0, 2) for n in ("cmp_k_w1", "cmp_v_w1")])
    arrays["w2"] = np.ascontiguousarray(
        np.stack([a[n][0].reshape(HID_T, P, HEAD) for n in ("cmp_k_w2", "cmp_v_w2")]).transpose(2, 0, 1, 3))
    arrays["pos"] = np.ascontiguousarray(
        np.stack([a[n][0].reshape(PAIRS, P).T for n in ("cmp_pos_k", "cmp_pos_v")], axis=1))
    arrays.update(_constants())

    nc = _bacc.Bacc("TRN2", target_bir_lowering=False, num_devices=1)
    ins = {}
    for name in arrays:
        arrays[name] = np.ascontiguousarray(arrays[name])
        ins[name] = nc.dram_tensor(f"in_{name}", arrays[name].shape, F32, kind="ExternalInput").ap()
    out = nc.dram_tensor("out_0", (KT, P, T), F32, kind="ExternalOutput").ap()
    build(nc, *[ins[n] for n in ("xT", "cols", "ada_w", "ffn_in", "ffn_out", "mix_w", "pool_w", "branch_w",
                                 "mixout_w", "w1", "w2", "pos", "ident", "dist", "cbias", "cmask", "icnt")], out)
    r = _run(nc, [{f"in_{n}": v for n, v in arrays.items()}], core_ids=[0])
    got = r.results[0]["out_0"]
    return np.ascontiguousarray(got.reshape(D, T).T).reshape(1, T, D)
```

```python
import math
from contextlib import ExitStack

import numpy as np
import concourse.bass as bass
from concourse import mybir

F32 = mybir.dt.float32
F32R = mybir.dt.float32r
ALU = mybir.AluOpType
ACT = mybir.ActivationFunctionType
AX = mybir.AxisListType

P = 128
D = 1024
T = 512
KT = D // P
TT = T // P
F = 2816
FT = F // P
HEADS, HEAD = 8, 64
GROUPS = 2
HPG = HEADS // GROUPS
STRIDE = 16
N_CMP = T // STRIDE - 1
CROWS = 32 + N_CMP
CPAD = 32
HID_T = 2
PAIRS = 16
WINDOWS = (2, 4, 8, 16)
NEG = -1e30
EPS = 1e-5
ALPHA = 2.0 ** 0.25
GELU_A, GELU_B = math.sqrt(2.0 / math.pi), 0.044715

OUT_SPLIT = (8, 7, 7)
IN_PANELS = 2 * FT
OUT_PANELS = 3 * KT
MIX = ["kc", "vc", "u0", "u1", "u2", "u3", "gate", "q0", "q1", "q2", "q3", "kslc", "kwin",
       "poolw", "vslc", "vwin"]
MIX8 = [n for n in MIX if n != "poolw"]
B_FFN1 = 0
B_MIX = B_FFN1 + IN_PANELS + OUT_PANELS
B_BRANCH = B_MIX + len(MIX)
B_MIXOUT = B_BRANCH + 3 * KT
B_FFN2 = B_MIXOUT + KT
N_PANELS = B_FFN2 + IN_PANELS + OUT_PANELS
assert B_MIX % 4 == 0 and B_FFN2 % 4 == 0

C_BADA, C_LNG, C_LNB, C_PSCALE, C_C = 0, 72, 104, 136, 140
N_COLS = 148
LNS = 4

P_OFF = [0, 128, 384, 768]
P_LEN = 1280
PT_OFF = [0, 512, 896, 1152]
PT_GROUPS = [[0], [1], [2, 3]]
PT_BANK = [4, 5, 0]
ADA_DIRECT = 3
UNITS = [(h, br) for h in range(HEADS) for br in range(2)]

SBUF_BASE = 16512
O_X = SBUF_BASE
O_HHI = O_X + 4 * KT * T
O_HLO = O_HHI + 4 * KT * T
O_RAW = O_HLO + 4 * KT * T
O_WHI = O_RAW + 2 * 4096
O_WLO = O_WHI + 4 * 4096
O_ADARAW = O_WLO + 4 * 4096
O_ACC = O_ADARAW + 3 * 2048
O_SCR = O_ACC + 3 * 4096
O_REGION = O_SCR + 4 * 2048
O_CONST = O_REGION + 2 * FT * 4 * T


def need(eng, sem, value):
    if not isinstance(value, int) or value > 0:
        eng.wait_ge(sem, value)


def build(nc, xT, cols, ada_w, ffn_in, ffn_out, mix_w, pool_w, branch_w, mixout_w,
          w1, w2, pos, ident_in, dist_in, cbias_in, cmask_in, icnt_in, out):
    with ExitStack() as ctx:
        def at(name, shape, offset, dt=F32):
            return nc.alloc_sbuf_tensor_at(name, shape, dt, offset=offset)

        ctx.enter_context(nc.sbuf_tensor("whole", [P, 53200], F32))
        X = at("X", [P, KT, T], O_X)
        h_hi = at("h_hi", [P, KT, T], O_HHI, F32R)
        h_lo = at("h_lo", [P, KT, T], O_HLO, F32R)
        raw = at("raw", [P, 2, 1024], O_RAW)
        w_hi = at("w_hi", [P, 4, 1024], O_WHI, F32R)
        w_lo = at("w_lo", [P, 4, 1024], O_WLO, F32R)
        ada_raw = at("ada_raw", [P, 3, 512], O_ADARAW)
        acc = at("acc", [P, 3, 1024], O_ACC)
        scr = at("scr", [P, 4, T], O_SCR)
        hbuf = at("hbuf", [P, KT, T], O_REGION + 20480)
        act_hi = at("act_hi", [P, FT, T], O_REGION, F32R)
        act_lo = at("act_lo", [P, FT, T], O_REGION + FT * 2048, F32R)
        ada_start = at("ada_start", [P, KT, 2048], O_REGION)
        R = O_REGION
        qT = at("qT", [P, 4, T], R)
        kT = at("kT", [P, 2, T], R + 8192)
        V = at("V", [P, 2, TT, P], R + 12288)
        vT = at("vT", [P, 2, T], R + 16384)
        w1v = at("w1v", [P, PAIRS, 256], R)
        blocks = at("blocks", [P, 4, PAIRS // 2, 64], R + 20480)
        PT = at("PT", [P, 2, P_LEN], R + 20480)
        Pr = at("Pr", [P, 2, P_LEN], R + 30720)
        pads = at("pads", [P, 4, 528], R + 30720)
        hidden = at("hidden", [P, 4, 64], R + 39168)
        cbias = at("cbias", [P, TT, HEADS, N_CMP], R + 40960)
        PcT = at("PcT", [P, GROUPS, T], R + 40960)
        dist = at("dist", [P, T], R + 45056)
        abias = at("abias", [P, 2, T], R + 47104)
        Pc = at("Pc", [P, TT, HEADS, CPAD], R + 51200)
        cmask = at("cmask", [P, TT, CPAD], R + 55296)
        G = at("G", [P, TT, 24], R + 55808)
        nmax = at("nmax", [P, 64], R + 56192)
        psumv = at("psumv", [P, 64], R + 56448)
        pscl = at("pscl", [P, 64], R + 56704)
        cst = at("cst", [P, 3, 32], R + 56960)
        pool_hi = at("pool_hi", [P, 4, T], R + 57344, F32R)
        pool_lo = at("pool_lo", [P, 4, T], R + 65536, F32R)
        o_hi = at("o_hi", [P, 4, T], R + 73728, F32R)
        o_lo = at("o_lo", [P, 4, T], R + 81920, F32R)
        w1k = at("w1k", [P, PAIRS, 256], R + 73728)
        mixed_hi = at("mixed_hi", [P, KT, T], R, F32R)
        mixed_lo = at("mixed_lo", [P, KT, T], R + 16384, F32R)
        tab = at("tab", [P, 2, 2, T], R + 32768)
        o = O_CONST
        ident = at("ident", [P, P], o)
        ones = at("ones", [P, P], o + 512)
        VC = at("VC", [P, P], o + 1024)
        colv = at("colv", [P, N_COLS], o + 1536)
        ada = at("ada", [P, 72], o + 2144)
        mod = at("mod", [P, 6, 8], o + 2432)
        cact = at("cact", [P, 8], o + 2624)
        posv = at("posv", [P, 2, PAIRS], o + 2688)
        w2s = at("w2s", [P, 2, HID_T, HEAD], o + 2816)
        icnt = at("icnt", [P, 4, 16], o + 3840)
        kcB = at("kcB", [P, 2 * N_CMP], o + 4096)
        st = at("st", [P, 8, TT], o + 4352)
        colp = at("colp", [P, 24], o + 4480)
        assert o + 4576 <= 229344

        psum = ctx.enter_context(nc.psum_tensor("psum", [P, 8, T], F32))

        def bank(n, w=T):
            return psum[:, n, 0:w]

        def sem(name):
            return ctx.enter_context(nc.semaphore(name))

        raw_landed = [sem(f"raw_landed{i}") for i in range(2)]
        ada_landed = [sem(f"ada_landed{i}") for i in range(3)]
        ada0_landed = [sem(f"ada0_landed{i}") for i in range(KT)]
        x_landed = [sem(f"x_landed{i}") for i in range(4)]
        const_landed = sem("const_landed")
        cols_landed = sem("cols_landed")
        mixc_landed = sem("mixc_landed")
        out_stored = sem("out_stored")
        split_hi = sem("split_hi")
        split_done = sem("split_done")
        panels_used = sem("panels_used")
        memset_done = sem("memset_done")
        c_tanh = sem("c_tanh")
        ada_used = sem("ada_used")
        ada_acc_start = sem("ada_acc_start")
        ada_cols = sem("ada_cols")
        ada_taken = sem("ada_taken")
        dve_chain = sem("dve_chain")
        act_chain = sem("act_chain")
        s_added = sem("s_added")
        q_added = sem("q_added")
        sq_done = sem("sq_done")
        stats_ready = sem("stats_ready")
        stats_small = sem("stats_small")
        rows_made = sem("rows_made")
        rows_ready = sem("rows_ready")
        ada_direct = sem("ada_direct")
        cmp_turned = sem("cmp_turned")
        cmp_hidden_T = sem("cmp_hidden_T")
        var_done = sem("var_done")
        std_done = sem("std_done")
        mod_ready = sem("mod_ready")
        scaled = sem("scaled")
        xhat_done = sem("xhat_done")
        h_made = sem("h_made")
        h_hi_done = sem("h_hi_done")
        h_split = sem("h_split")
        x_scaled = sem("x_scaled")
        z_done = sem("z_done")
        tanh_done = sem("tanh_done")
        gated = sem("gated")
        hidden_made = sem("hidden_made")
        act_hi_done = sem("act_hi_done")
        act_split = sem("act_split")
        kv_blocks = sem("kv_blocks")
        act_evac = sem("act_evac")
        pool_delta = sem("pool_delta")
        pool_hi_done = sem("pool_hi_done")
        pool_split = sem("pool_split")
        pool_mixed = sem("pool_mixed")
        poolout_hi = sem("poolout_hi")
        poolout_split = sem("poolout_split")
        cmp_hidden = sem("cmp_hidden")
        cmp_sq = sem("cmp_sq")
        cmp_arg = sem("cmp_arg")
        cmp_tanh = sem("cmp_tanh")
        cmp_act = sem("cmp_act")
        cmp_kv = sem("cmp_kv")
        cmp_kv_taken = sem("cmp_kv_taken")
        gates_T = sem("gates_T")
        gates_taken = sem("gates_taken")
        cmp_scored = sem("cmp_scored")
        cmp_shifted = sem("cmp_shifted")
        cmp_exp = sem("cmp_exp")
        cmp_probs = sem("cmp_probs")
        cmp_PT = sem("cmp_PT")
        cmp_PT_taken = sem("cmp_PT_taken")
        v_turned = sem("v_turned")
        v_taken = sem("v_taken")
        bias_made = sem("bias_made")
        scored = sem("scored")
        shifted = sem("shifted")
        exp_done = sem("exp_done")
        probs_ready = sem("probs_ready")
        turned = sem("turned")
        turned_act = sem("turned_act")
        turned_dve = sem("turned_dve")
        o_made = sem("o_made")
        o_hi_done = sem("o_hi_done")
        o_split = sem("o_split")
        br_tanh = sem("br_tanh")
        br_gated = sem("br_gated")
        br_mixed = sem("br_mixed")
        br_hi = sem("br_hi")
        br_split = sem("br_split")

        block = ctx.enter_context(nc.Block())

        ADA_BASE = {1: 0, "mix": 48, 2: 96}
        N_ADA = {1: 6, "mix": 6, 2: 2}
        ADA_CHUNK = {1: 2, "mix": 5, 2: 8}
        ADA_SLOT = {1: [0, 0, 0], "mix": [16, 16, 16], 2: [32, 32, 32]}

        def ada_slot_count(phase, step, q):
            per = 2 if N_ADA[phase] == 6 else 1
            return ADA_SLOT[phase][q % 3] + per * step + q // 3 + 1

        def in_base(n):
            return B_FFN1 if n == 1 else B_FFN2

        def chunk_base(n):
            return 0 if n == 1 else FT

        @block.sync
        def _(sp):
            def panel(p, src, width=1024, slot=None):
                need(sp, split_done, p - 1)
                sp.dma_start(raw[:, slot, 0:width], src).then_inc(raw_landed[slot], 16)

            def ada_unit(phase, step, q):
                u = ADA_BASE[phase] + N_ADA[phase] * step + q
                need(sp, ada_used, u - (2 if N_ADA[phase] == 6 else 1))
                col = (ADA_CHUNK[phase] + q // 2) * 1024 + (q % 2) * 512
                sp.dma_start(ada_raw[:, q % 3, :], ada_w[step, :, col:col + 512]).then_inc(
                    ada_landed[q % 3], 16)

            def feed_forward(n):
                base = in_base(n)

                def step(it, with_ada, with_panels=True):
                    for j in range(4):
                        c = 2 * it + 2 + j // 2
                        if with_panels:
                            panel(base + 4 * it + 4 + j, ffn_in[n - 1, c, j % 2, :, :], slot=j % 2)
                        if with_ada:
                            per = N_ADA[n]
                            for q in ([0, 1], [2], [3, 4], [5])[j]:
                                if q < per:
                                    ada_unit(n, it, q)

                for j in range(2 if n == 1 else 0, 4):
                    panel(base + j, ffn_in[n - 1, j // 2, j % 2, :, :], slot=j % 2)
                step(0, True)
                with sp.Fori(1, KT) as it:
                    step(it, True)
                with sp.Fori(KT, FT // 2 - 1) as it:
                    step(it, False)
                ob = base + IN_PANELS
                with sp.Fori(0, 2) as it:
                    for m4 in range(4):
                        off = 0
                        for j, kn in enumerate(OUT_SPLIT):
                            i = 3 * m4 + j
                            panel(ob + 12 * it + i,
                                  ffn_out[n - 1, 4 * it + m4, :, off * P:(off + kn) * P],
                                  width=kn * P, slot=i % 2)
                            off += kn

            for i in range(4):
                sp.dma_start(X[:, 2 * i:2 * i + 2, :], xT[:, 2 * i:2 * i + 2, :]).then_inc(
                    x_landed[i], 16)
            for j in range(2):
                panel(j, ffn_in[0, 0, j, :, :], slot=j)
            for k in range(KT):
                sp.dma_start(ada_start[:, k, :], ada_w[k, :, 0:2048]).then_inc(ada0_landed[k], 16)
            feed_forward(1)
            k8 = 0
            for i, name in enumerate(MIX):
                p = B_MIX + i
                if name == "poolw":
                    panel(p, pool_w[:, :], width=512, slot=p % 2)
                else:
                    panel(p, mix_w[k8, :, :], slot=p % 2)
                    k8 += 1

            def branch_panel(i):
                m, j = divmod(i, 3)
                if m < KT:
                    src = branch_w[m, :, :] if j == 2 else mix_w[k8 + 2 * m + j, :, :]
                    panel(B_BRANCH + i, src, slot=(B_BRANCH + i) % 2)

            branch_panel(0)
            branch_panel(1)
            for i in range(3 * KT):
                branch_panel(i + 2)
                for q in range(2 * (i % 3), 2 * (i % 3) + 2):
                    ada_unit("mix", i // 3, q)
            for m in range(KT):
                p = B_MIXOUT + m
                panel(p, mixout_w[m, :, :], slot=p % 2)
            feed_forward(2)
            for m in range(KT):
                sp.wait_ge(x_scaled, 8 * 3 + m + 1)
                sp.dma_start(out[m, :, :], X[:, m, :]).then_inc(out_stored, 16)
            sp.wait_ge(out_stored, 16 * KT)

        @block.gpsimd
        def _(gp):
            gp.memset(ones[:, :], 1.0).then_inc(memset_done, 1)

            def split(p, slot):
                gp.wait_ge(split_hi, p + 1)
                gp.tensor_tensor(w_lo[:, slot, :], raw[:, slot % 2, :], w_hi[:, slot, :].bitcast(F32),
                                 ALU.subtract).then_inc(split_done, 1)

            def splits(start, end):
                head, tail = -(-start // 4), end // 4
                for p in range(start, 4 * head):
                    split(p, p % 4)
                with gp.Fori(head, tail) as it:
                    for slot in range(4):
                        split(4 * it + slot, slot)
                for p in range(4 * tail, end):
                    split(p, p % 4)

            start = 0
            for L, end in enumerate((B_FFN1, B_MIX, B_FFN2)):
                if end:
                    splits(start, end + 3)
                else:
                    for p in range(3):
                        split(p, p)
                start = end + 3
                for m in range(KT):
                    gp.wait_ge(h_hi_done, 8 * L + m + 1)
                    gp.tensor_tensor(h_lo[:, m, :], hbuf[:, m, :], h_hi[:, m, :].bitcast(F32),
                                     ALU.subtract).then_inc(h_split, 1)
            splits(start, N_PANELS)

        @block.tensor
        def _(pe):
            def product(o_, wslot, kk, xh, xl, first, last):
                ws = slice(kk * P, (kk + 1) * P)
                pe.matmul(o_, w_hi[:, wslot, ws], xh, start=first, stop=False)
                pe.matmul(o_, w_hi[:, wslot, ws], xl, start=False, stop=False)
                return pe.matmul(o_, w_lo[:, wslot, ws], xh, start=False, stop=last)

            def panel_over_h(p, wslot, b, h_wait=None):
                pe.wait_ge(split_done, p + 1)
                for k in range(KT):
                    if h_wait is not None:
                        pe.wait_ge(h_split, h_wait + k + 1)
                    ins = product(bank(b), wslot, k, h_hi[:, k, :], h_lo[:, k, :], k == 0, k == KT - 1)
                ins.then_inc(panels_used, 1)

            def turn_modulation(s, b, count, taken=None):
                if taken is not None:
                    pe.wait_ge(ada_taken, taken)
                for m in range(8):
                    ins = pe.transpose(psum[:, b + m // 4, (m % 4) * P:(m % 4) * P + P],
                                       acc[:, s, m * P:(m + 1) * P], ident[:, :])
                if count:
                    ins.then_inc(ada_cols, 1)

            def norm_stats(L):
                for i, added in enumerate((s_added, q_added)):
                    pe.wait_ge(added, 7 * (L + 1))
                    for t in range(TT):
                        ins = pe.transpose(psum[:, 6 + i, t * P:(t + 1) * P],
                                           scr[:, i, t * P:(t + 1) * P], ident[:, :])
                    ins.then_inc(stats_ready, 1)
                for i in range(2):
                    pe.wait_ge(rows_made, 2 * L + i + 1)
                    pe.matmul(bank(6 + i), ones[:, :], scr[:, i, :], start=True, stop=True).then_inc(rows_ready, 1)

            def feed_forward(n):
                base, cb = in_base(n), chunk_base(n)

                def chunk(it, c2, first=False):
                    c = 2 * it + c2
                    need(pe, hidden_made, cb + c - 1)
                    for gu in range(2):
                        panel_over_h(base + 2 * c + gu, 2 * c2 + gu, 2 * c2 + gu,
                                     (0 if n == 1 else 16) if first and gu == 0 else None)

                chunk(0, 0, True)
                chunk(0, 1)
                with pe.Fori(1, FT // 2) as it:
                    chunk(it, 0)
                    chunk(it, 1)
                ob = base + IN_PANELS
                pe.wait_ge(ada_used, ADA_BASE[n] + 8 * N_ADA[n])
                pe.wait_ge(act_split, cb + FT)
                zb = 0 if n == 1 else 16
                ada0 = 1 if n == 1 else 7

                def out_tiles(it):
                    for m4 in range(4):
                        m = 4 * it + m4
                        if it == 0 and m4 < N_ADA[n] // 2:
                            turn_modulation(m4, 6, True, ada0 + m4)
                        if not isinstance(it, int) or m >= 2:
                            pe.wait_ge(z_done, zb + m - 1)
                        k = 0
                        for j, kn in enumerate(OUT_SPLIT):
                            i = 3 * m4 + j
                            pe.wait_ge(split_done, ob + 12 * it + i + 1)
                            for kk in range(kn):
                                ins = product(bank(4 + m4 % 2), i % 4, kk, act_hi[:, k, :],
                                              act_lo[:, k, :], k == 0, k == FT - 1)
                                k += 1
                            ins.then_inc(panels_used, 1)

                out_tiles(0)
                out_tiles(1)
                pe.wait_ge(ada_taken, ada0 + N_ADA[n] // 2)
                norm_stats(1 if n == 1 else 3)

            pe.wait_ge(memset_done, 1)
            pe.wait_ge(const_landed, 16 * 4)
            norm_stats(0)
            for k in range(ADA_DIRECT):
                pe.wait_ge(ada0_landed[k], 16)
            pe.wait_ge(ada_acc_start, 1)
            for c in range(16):
                for k in range(ADA_DIRECT):
                    ins = pe.matmul(psum[:, 5, c:c + 1], ada_start[:, k, c * P:(c + 1) * P], cact[:, k:k + 1],
                                    start=(k == 0), stop=(k == ADA_DIRECT - 1))
            ins.then_inc(ada_direct, 1)
            pe.wait_ge(ada_acc_start, KT - ADA_DIRECT + 1)
            turn_modulation(0, 0, False)
            turn_modulation(1, 2, True)
            feed_forward(1)

            pidx = {name: B_MIX + i for i, name in enumerate(MIX)}

            def k8_panel(name, h_wait=None):
                n = MIX8.index(name)
                b = n % 2
                if n in (2, 3):
                    pe.wait_ge(kv_blocks, 4 * (n - 1))
                if n > 3:
                    pe.wait_ge(act_evac, n - 3)
                p = pidx[name]
                panel_over_h(p, p % 4, b, h_wait)

            k8_panel("kc", 8)
            for name in ("vc", "u0", "u1", "u2", "u3"):
                k8_panel(name)
            pe.wait_ge(mixc_landed, 16 * 5)
            pe.wait_ge(kv_blocks, 8)
            for kv in range(2):
                for i in range(PAIRS):
                    half = i // 8
                    ins = pe.matmul(psum[0:CROWS, 2, 256 * kv:256 * kv + 256],
                                    blocks[:, 2 * kv + half, i % 8, half:half + CROWS], (w1k, w1v)[kv][:, i, :],
                                    start=(i == 0), stop=(i == PAIRS - 1))
            ins.then_inc(cmp_hidden, 1)
            k8_panel("gate")
            pe.wait_ge(cmp_act, 1)
            for n in range(4):
                ins = pe.transpose(psum[:, 3, 64 * n:64 * n + CROWS], scr[0:CROWS, 0, P * n:P * n + P],
                                   ident[0:CROWS, 0:CROWS])
            ins.then_inc(cmp_turned, 1)
            k8_panel("q0")
            pe.wait_ge(cmp_hidden_T, 1)
            for g in range(GROUPS):
                for kt in range(HID_T):
                    pe.matmul(psum[64 * g:64 * g + 64, 2, 0:N_CMP], w2s[:, 0, kt, :],
                              hidden[:, kt, 32 * g:32 * g + N_CMP], start=(kt == 0), stop=(kt == 1))
            for g in range(GROUPS):
                for kt in range(HID_T):
                    ins = pe.matmul(psum[0:31, 2, 64 + 64 * g:128 + 64 * g],
                                    hidden[:, 2 + kt, 32 * g:32 * g + N_CMP], w2s[:, 1, kt, :],
                                    start=(kt == 0), stop=(kt == 1))
            ins.then_inc(cmp_kv, 1)
            pe.wait_ge(act_evac, MIX8.index("gate") - 1)
            for t in range(TT):
                ins = pe.transpose(psum[:, 4, P * t:P * t + P], vT[:, 0, t * P:(t + 1) * P], ident[:, :])
            ins.then_inc(gates_T, 1)
            for name in ("q1", "q2", "q3"):
                k8_panel(name)
            pe.wait_ge(cmp_kv_taken, 2)
            pe.wait_ge(act_evac, MIX8.index("q3") - 1)
            for t in range(TT):
                for j in range(HPG):
                    col = ((t % 2) * HPG + j) * 2 * N_CMP
                    ins = pe.matmul(psum[:, 6 + t // 2, col:col + 2 * N_CMP], qT[:, j, t * P:(t + 1) * P],
                                    kcB[:, :], start=True, stop=True)
                if t % 2:
                    ins.then_inc(cmp_scored, 1)
            k8_panel("kslc")
            k8_panel("kwin")
            p = pidx["poolw"]
            pe.wait_ge(split_done, p + 1)
            pe.wait_ge(pool_split, 4)
            pe.wait_ge(gates_taken, 1)
            for g in range(4):
                if g >= 2:
                    pe.wait_ge(poolout_split, g - 1)
                ins = product(bank(4 + g % 2), p % 4, g, pool_hi[:, g, :], pool_lo[:, g, :], True, True)
                if g < 3:
                    ins.then_inc(pool_mixed, 1)
            ins.then_inc(panels_used, 1)
            k8_panel("vslc")
            k8_panel("vwin")
            for v in range(2):
                pe.wait_ge(act_evac, MIX8.index("vslc") - 1 + v)
                for t in range(TT):
                    ins = pe.transpose(psum[:, 2 + v, P * t:P * t + P], vT[:, v, t * P:(t + 1) * P], ident[:, :])
                ins.then_inc(v_turned, 1)
            pe.wait_ge(cmp_probs, 1)
            pe.wait_ge(poolout_split, 4)
            for g in range(GROUPS):
                for t in range(TT):
                    ins = pe.transpose(psum[:, 4 + g, P * t:P * t + P],
                                       Pc[:, t, HPG * g:HPG * g + HPG, :].rearrange("p h n -> p (h n)"),
                                       ident[:, :])
                ins.then_inc(cmp_PT, 1)

            def scores(u):
                h, br = UNITS[u]
                j, g = h % HPG, h // HPG
                for t in range(TT):
                    n = 4 * u + t
                    if n >= 3:
                        pe.wait_ge(shifted, n - 2)
                    elif n:
                        pe.wait_ge(v_taken, n)
                    w = P * (t + 1)
                    pe.matmul(bank(1 + n % 3, w), qT[64 * g:64 * g + 64, j, t * P:(t + 1) * P],
                              kT[64 * g:64 * g + 64, br, 0:w], start=True, stop=True).then_inc(scored, 1)

            def turn(u):
                pe.wait_ge(probs_ready, u + 1)
                for gi, kts in enumerate(PT_GROUPS):
                    if u == 0:
                        if gi < 2:
                            pe.wait_ge(cmp_PT_taken, gi + 1)
                    elif gi == 1:
                        pe.wait_ge(turned_dve, u)
                    else:
                        pe.wait_ge(turned_act, 2 * u - 1 + gi // 2)
                    col = 0
                    for kt in kts:
                        for t in range(kt, TT):
                            src = Pr[:, u % 2, P_OFF[t] + kt * P:P_OFF[t] + (kt + 1) * P]
                            ins = pe.transpose(psum[:, PT_BANK[gi], col:col + P], src, ident[:, :])
                            col += P
                    ins.then_inc(turned, 1)

            def weigh(u):
                h, br = UNITS[u]
                g = h // HPG
                b = 6 + h % 2
                if br == 0:
                    if h >= 2:
                        pe.wait_ge(o_split, h - 1)
                    r = 32 * (h % HPG)
                    pe.matmul(bank(b), VC[r:r + N_CMP, :], PcT[r:r + N_CMP, g, :],
                              start=True, stop=False)
                pe.wait_ge(turned_act, 2 * u + 2)
                pe.wait_ge(turned_dve, u + 1)
                for kt in range(TT):
                    w = T - kt * P
                    ins = pe.matmul(psum[:, b, kt * P:T], V[:, br, kt, :],
                                    PT[:, u % 2, PT_OFF[kt]:PT_OFF[kt] + w],
                                    start=False, stop=(br == 1 and kt == TT - 1))
                ins.then_inc(o_made, 1)

            for s in range(len(UNITS) + 2):
                if s < len(UNITS):
                    scores(s)
                if 1 <= s <= len(UNITS):
                    turn(s - 1)
                if s >= 2:
                    weigh(s - 2)

            for m in range(KT):
                p = B_BRANCH + 3 * m
                b = 4 * (m % 2)
                if m >= 2:
                    pe.wait_ge(br_mixed, m - 1)
                if m == 0:
                    pe.wait_ge(turned_act, 2 * len(UNITS))
                    pe.wait_ge(shifted, 4 * len(UNITS))
                if m == 1:
                    pe.wait_ge(o_split, HEADS)
                panel_over_h(p, p % 4, b)
                panel_over_h(p + 1, (p + 1) % 4, b + 1)
                p += 2
                pe.wait_ge(split_done, p + 1)
                if m == 0:
                    pe.wait_ge(o_split, HEADS)
                for k in range(4):
                    product(bank(b + 2), p % 4, k, pool_hi[:, k, :], pool_lo[:, k, :], k == 0, k == 3)
                for k in range(4):
                    ins = product(bank(b + 3), p % 4, 4 + k, o_hi[:, k, :], o_lo[:, k, :], k == 0, k == 3)
                ins.then_inc(panels_used, 1)
            pe.wait_ge(br_mixed, KT)
            pe.wait_ge(ada_used, ADA_BASE["mix"] + 8 * N_ADA["mix"])
            for m in range(KT):
                p = B_MIXOUT + m
                if m < 3:
                    turn_modulation(m, 6, True, 4 + m)
                if m >= 2:
                    pe.wait_ge(z_done, 8 + m - 1)
                pe.wait_ge(split_done, p + 1)
                for k in range(KT):
                    if m == 0:
                        pe.wait_ge(br_split, k + 1)
                    ins = product(bank(4 + m % 2), p % 4, k, mixed_hi[:, k, :], mixed_lo[:, k, :],
                                  k == 0, k == KT - 1)
                ins.then_inc(panels_used, 1)
            pe.wait_ge(ada_taken, 7)
            norm_stats(2)
            feed_forward(2)

        @block.scalar
        def _(act):
            chain = [0]

            def link(ins):
                chain[0] += 1
                ins.then_inc(act_chain, 1)
                act.wait_ge(act_chain, chain[0])

            def split(p, slot, filled):
                act.wait_ge(raw_landed[slot % 2], 16 * filled)
                need(act, panels_used, p - 3)
                act.activation(w_hi[:, slot, :], raw[:, slot % 2, :], ACT.Copy).then_inc(split_hi, 1)

            todo = [0]

            def split_before(used):
                while todo[0] < min(used + 3, N_PANELS):
                    p = todo[0]
                    split(p, p % 4, p // 2 + 1)
                    todo[0] += 1

            def wait_used(used):
                split_before(used)
                act.wait_ge(panels_used, used)

            def square(L, m):
                if L == 0:
                    if m % 2 == 0:
                        act.wait_ge(x_landed[m // 2], 16)
                else:
                    act.wait_ge(z_done, 8 * (L - 1) + m + 1)
                if m >= 2:
                    act.wait_ge(q_added, 7 * L + max(m - 2, 1))
                act.activation(scr[:, 2 + m % 2, :], X[:, m, :], ACT.Square).then_inc(sq_done, 1)

            def norm(L):
                act.wait_ge(var_done, L + 1)
                act.activation(st[:, 4, :], st[:, 3, :], ACT.Sqrt).then_inc(std_done, 1)
                if L == 0:
                    split_before(0)
                act.wait_ge(mod_ready, L + 1)
                if L < 3:
                    def make_h(m):
                        act.wait_ge(xhat_done, 8 * L + m + 1)
                        act.activation(hbuf[:, m, :], X[:, m, :], ACT.Identity,
                                       bias=mod[:, 1, m:m + 1], scale=mod[:, 0, m:m + 1]).then_inc(h_made, 1)

                    make_h(0)
                    for m in range(KT):
                        if m + 1 < KT:
                            make_h(m + 1)
                        act.wait_ge(h_made, 8 * L + m + 1)
                        act.activation(h_hi[:, m, :], hbuf[:, m, :], ACT.Copy).then_inc(h_hi_done, 1)
                for m in range(KT):
                    act.wait_ge(xhat_done, 8 * L + m + 1)
                    act.activation(X[:, m, :], X[:, m, :], ACT.Identity,
                                   bias=mod[:, 3, m:m + 1], scale=mod[:, 2, m:m + 1]).then_inc(x_scaled, 1)

            def feed_forward(n):
                base, cb = in_base(n), chunk_base(n)

                def chunk(it, c2):
                    c = 2 * it + c2
                    if not (isinstance(c, int) and c == 0):
                        act.wait_ge(hidden_made, cb + c)
                        act.activation(act_hi[:, c - 1, :] if isinstance(c, int) else
                                       act_hi[:, bass.ds(c - 1, 1), :].rearrange("p o t -> p (o t)"),
                                       scr[:, 1 - c2, :], ACT.Copy).then_inc(act_hi_done, 1)
                    split(base + 2 * c + 3, (2 * c2 + 3) % 4, base // 2 + c + 2)
                    act.wait_ge(panels_used, base + 2 * c + 1)
                    need(act, act_split, cb + c - 1)
                    act.activation(scr[:, c2, :], bank(2 * c2), ACT.Tanh, scale=0.5).then_inc(tanh_done, 1)
                    split(base + 2 * c + 4, 2 * c2, base // 2 + c + 3)

                assert todo[0] == base + 3
                chunk(0, 0)
                chunk(0, 1)
                with act.Fori(1, FT // 2) as it:
                    chunk(it, 0)
                    chunk(it, 1)
                todo[0] = base + IN_PANELS + 3
                act.wait_ge(hidden_made, cb + FT)
                act.activation(act_hi[:, FT - 1, :], scr[:, (FT - 1) % 2, :], ACT.Copy).then_inc(act_hi_done, 1)

            act.dma_start(colv[:, :], cols[:, :]).then_inc(cols_landed, 16)
            act.dma_start(ident[:, :], ident_in[:, :]).then_inc(const_landed, 16)
            act.dma_start(posv[:, :, :], pos[:, :, :]).then_inc(const_landed, 16)
            act.dma_start(w2s[:, :, :, :], w2[:, :, :, :]).then_inc(const_landed, 16)
            act.dma_start(icnt[:, :, :], icnt_in[:, :, :]).then_inc(const_landed, 16)
            act.wait_ge(cols_landed, 16)
            act.activation(cact[:, :], colv[:, C_C:C_C + 8], ACT.Tanh, scale=0.5).then_inc(c_tanh, 1)
            act.preload_act_table(ACT.Sqrt)
            for m in range(KT):
                square(0, m)
            norm(0)
            feed_forward(1)
            act.preload_act_table(ACT.Sqrt)
            for m in range(KT):
                split_before(B_FFN1 + IN_PANELS + 3 * m + 3)
                square(1, m)
            act.wait_ge(panels_used, B_MIX)
            act.dma_start(w1k[:, :, :], w1[0, :, :, :]).then_inc(mixc_landed, 16)
            act.dma_start(w1v[:, :, :], w1[1, :, :, :]).then_inc(mixc_landed, 16)
            act.dma_start(cbias[:, :, :, :], cbias_in[:, :, :, :]).then_inc(mixc_landed, 16)
            act.dma_start(cmask[:, :, :], cmask_in[:, :, :]).then_inc(mixc_landed, 16)
            act.dma_start(dist[:, :], dist_in[:, :]).then_inc(mixc_landed, 16)
            norm(1)

            def taken(name):
                return B_MIX + MIX.index(name) + 1

            def k8_bank(name):
                return MIX8.index(name) % 2

            for g in range(4):
                wait_used(taken(f"u{g}"))
                if g == 0:
                    act.wait_ge(pool_delta, 1)
                if g >= 2:
                    act.wait_ge(pool_delta, g)
                act.activation(pads[:, g % 2, 16:528], bank(k8_bank(f"u{g}")), ACT.Copy).then_inc(act_evac, 1)
                if g >= 1:
                    act.wait_ge(pool_delta, g + 1)
                    act.activation(pool_hi[:, g - 1, :], pads[:, 2 + (g - 1) % 2, 16:528],
                                   ACT.Copy).then_inc(pool_hi_done, 1)
            act.wait_ge(pool_delta, 5)
            act.activation(pool_hi[:, 3, :], pads[:, 3, 16:528], ACT.Copy).then_inc(pool_hi_done, 1)
            wait_used(taken("gate"))
            act.activation(vT[:, 0, :], bank(k8_bank("gate")), ACT.Tanh, scale=0.5).then_inc(act_evac, 1)
            act.wait_ge(cmp_hidden, 1)
            hb = psum[0:CROWS, 2, :]
            sq = scr[0:CROWS, 1, :]
            act.activation(sq, hb, ACT.Square).then_inc(cmp_sq, 1)
            act.wait_ge(cmp_arg, 1)
            act.activation(sq, sq, ACT.Tanh, scale=GELU_A).then_inc(cmp_tanh, 1)
            wait_used(taken("q0"))
            act.activation(qT[:, 0, :], bank(k8_bank("q0")), ACT.Copy, scale=HEAD ** -0.5).then_inc(act_evac, 1)
            for j in range(1, 4):
                wait_used(taken(f"q{j}"))
                act.activation(qT[:, j, :], bank(k8_bank(f"q{j}")), ACT.Copy, scale=HEAD ** -0.5).then_inc(act_evac, 1)
            act.wait_ge(cmp_shifted, 1)
            act.activation(Pc[:, :, :, 0:N_CMP], Pc[:, :, :, 0:N_CMP], ACT.Exp).then_inc(cmp_exp, 1)
            for br, name in enumerate(("kslc", "kwin")):
                wait_used(taken(name))
                act.activation(kT[:, br, :], bank(k8_bank(name)), ACT.Copy).then_inc(act_evac, 1)
            for g in range(4):
                act.wait_ge(pool_mixed, g + 1) if g < 3 else wait_used(taken("poolw"))
                act.activation(pool_hi[:, g, :], bank(4 + g % 2), ACT.Copy,
                               scale=colv[:, C_PSCALE + g:C_PSCALE + g + 1]).then_inc(poolout_hi, 1)
            for v, name in enumerate(("vslc", "vwin")):
                wait_used(taken(name))
                act.activation(vT[:, v, :], bank(k8_bank(name)), ACT.Copy).then_inc(act_evac, 1)

            def exps(u):
                for t in range(TT):
                    n = 4 * u + t
                    act.wait_ge(shifted, n + 1)
                    pr = Pr[:, u % 2, P_OFF[t]:P_OFF[t] + P * (t + 1)]
                    act.activation(pr, pr, ACT.Exp, bias=nmax[:, n:n + 1], scale=-1.0,
                                   accum_out=psumv[:, n:n + 1]).then_inc(exp_done, 1)

            def take_turned(u):
                if u >= 2:
                    act.wait_ge(o_made, u - 1)
                for gi in (0, 2):
                    act.wait_ge(turned, 3 * u + gi + 1)
                    w = 512 if gi == 0 else 384
                    off = PT_OFF[PT_GROUPS[gi][0]]
                    act.activation(PT[:, u % 2, off:off + w], bank(PT_BANK[gi], w), ACT.Copy).then_inc(turned_act, 1)

            def take_head(h):
                j, g = h % HPG, h // HPG
                act.wait_ge(o_made, 2 * h + 2)
                act.activation(o_hi[64 * g:64 * g + 64, j, :], psum[64 * g:64 * g + 64, 6 + h % 2, :],
                               ACT.Copy).then_inc(o_hi_done, 1)

            split_before(B_BRANCH + 1)
            for s in range(len(UNITS) + 2):
                if s < len(UNITS):
                    exps(s)
                if 1 <= s <= len(UNITS):
                    take_turned(s - 1)
                if s >= 2 and UNITS[s - 2][1] == 1:
                    take_head(UNITS[s - 2][0])

            for m in range(KT):
                b = 4 * (m % 2)
                for q in range(2):
                    wait_used(B_BRANCH + 3 * m + q + 1)
                    if m >= 2 and q == 0:
                        act.wait_ge(br_split, m - 1)
                    act.activation(tab[:, m % 2, q, :], bank(b + q), ACT.Tanh, scale=0.5).then_inc(br_tanh, 1)
                act.wait_ge(br_mixed, m + 1)
                act.activation(mixed_hi[:, m, :], tab[:, m % 2, 0, :], ACT.Copy).then_inc(br_hi, 1)
            act.preload_act_table(ACT.Sqrt)
            for m in range(KT):
                split_before(B_MIXOUT + m + 1)
                square(2, m)
            norm(2)
            feed_forward(2)
            act.preload_act_table(ACT.Sqrt)
            for m in range(KT):
                split_before(B_FFN2 + IN_PANELS + 3 * m + 3)
                square(3, m)
            norm(3)

        @block.vector
        def _(dve):
            chain = [0]

            def link(ins):
                chain[0] += 1
                ins.then_inc(dve_chain, 1)
                dve.wait_ge(dve_chain, chain[0])

            def sums(L, m):
                if L == 0 and m % 2 == 0:
                    dve.wait_ge(x_landed[m // 2], 16)
                if m == 0:
                    return
                if m > 1:
                    dve.wait_ge(s_added, 7 * L + m - 1)
                elif L:
                    dve.wait_ge(z_done, 8 * (L - 1) + m + 1)
                if L and m > 1:
                    dve.wait_ge(z_done, 8 * (L - 1) + m + 1)
                a = X[:, 0, :] if m == 1 else scr[:, 0, :]
                dve.tensor_tensor(scr[:, 0, :], a, X[:, m, :], ALU.add).then_inc(s_added, 1)

            def squares(L, m):
                if m == 0:
                    return
                dve.wait_ge(sq_done, 8 * L + m + 1)
                if m > 1:
                    dve.wait_ge(q_added, 7 * L + m - 1)
                a = scr[:, 2, :] if m == 1 else scr[:, 1, :]
                dve.tensor_tensor(scr[:, 1, :], a, scr[:, 2 + m % 2, :], ALU.add).then_inc(q_added, 1)

            def modulation(b, chunk):
                for i in range(2):
                    ins = dve.tensor_reduce(colp[:, 4 * i:4 * i + 4],
                                            bank(b + i).rearrange("p (m c) -> p m c", c=P), AX.X, ALU.add)
                link(ins)
                dve.tensor_tensor(ada[:, 8 * chunk:8 * chunk + 8], colp[:, 0:8],
                                  colv[:, C_BADA + 8 * chunk:C_BADA + 8 * chunk + 8],
                                  ALU.add).then_inc(ada_taken, 1)

            def norm_columns(L):
                g = colv[:, C_LNG + 8 * L:C_LNG + 8 * L + 8]
                b = colv[:, C_LNB + 8 * L:C_LNB + 8 * L + 8]
                if L < 3:
                    sh = ada[:, 24 * L:24 * L + 8]
                    sc = ada[:, 24 * L + 8:24 * L + 16]
                    link(dve.tensor_scalar(mod[:, 5, :], sc, 1.0, None, ALU.add))
                    dve.tensor_tensor(mod[:, 0, :], mod[:, 5, :], g, ALU.mult)
                    link(dve.tensor_tensor(mod[:, 1, :], mod[:, 5, :], b, ALU.mult))
                    dve.tensor_scalar(mod[:, 2, :], g, ALPHA, None, ALU.mult)
                    dve.tensor_scalar(mod[:, 3, :], b, ALPHA, None, ALU.mult)
                    dve.tensor_tensor(mod[:, 1, :], mod[:, 1, :], sh, ALU.add).then_inc(mod_ready, 1)
                else:
                    dve.tensor_scalar(mod[:, 2, :], g, 1.0, None, ALU.mult)
                    dve.tensor_scalar(mod[:, 3, :], b, 1.0, None, ALU.mult).then_inc(mod_ready, 1)

            def norm(L):
                for i in range(2):
                    dve.wait_ge(stats_ready, 2 * L + i + 1)
                    ins = dve.tensor_reduce(st[:, 6 * i, :], bank(6 + i).rearrange("p (t c) -> p t c", c=P),
                                            AX.X, ALU.add)
                    if i == 0:
                        link(ins)
                        ins = dve.tensor_scalar(st[:, 1, :], st[:, 0, :], 1.0 / D, None, ALU.mult)
                    link(ins)
                link(dve.tensor_tensor(st[:, 2, :], st[:, 1, :], st[:, 1, :], ALU.mult))
                link(dve.scalar_tensor_tensor(st[:, 3, :], st[:, 6, :], 1.0 / D, st[:, 2, :], ALU.mult, ALU.subtract))
                dve.tensor_scalar(st[:, 3, :], st[:, 3, :], 0.0, EPS, ALU.max, ALU.add).then_inc(var_done, 1)
                dve.wait_ge(std_done, L + 1)
                link(dve.reciprocal(st[:, 5, :], st[:, 4, :]))
                link(dve.tensor_tensor(st[:, 6, :], st[:, 5, :], st[:, 5, :], ALU.mult))
                link(dve.tensor_tensor(st[:, 6, :], st[:, 6, :], st[:, 3, :], ALU.mult))
                link(dve.tensor_scalar(st[:, 6, :], st[:, 6, :], -0.5, 1.5, ALU.mult, ALU.add))
                link(dve.tensor_tensor(st[:, 5, :], st[:, 5, :], st[:, 6, :], ALU.mult))
                dve.tensor_tensor(st[:, 7, :], st[:, 1, :], st[:, 5, :], ALU.mult).then_inc(stats_small, 1)
                for i, row in enumerate((5, 7)):
                    if i:
                        dve.wait_ge(stats_small, L + 1)
                    dve.tensor_tensor(scr[:, i, :].rearrange("p (t c) -> p t c", c=P),
                                      ident[:, :].rearrange("p (o c) -> p o c", o=1).broadcast_to([P, TT, P]),
                                      st[:, row, :].rearrange("p (t o) -> p t o", o=1).broadcast_to([P, TT, P]),
                                      ALU.mult).then_inc(rows_made, 1)

            def normalize_tile(L, m):
                if m < KT:
                    dve.wait_ge(rows_ready, 2 * L + 1)
                    dve.tensor_tensor(X[:, m, :], X[:, m, :], bank(6), ALU.mult).then_inc(scaled, 1)
                if m >= 1:
                    dve.wait_ge(rows_ready, 2 * L + 2)
                    dve.wait_ge(scaled, 8 * L + m)
                    dve.tensor_tensor(X[:, m - 1, :], X[:, m - 1, :], bank(7), ALU.subtract).then_inc(xhat_done, 1)

            def norm_tiles(L):
                for m in range(KT + 1):
                    normalize_tile(L, m)

            def ada_unit(phase, step, q):
                u = ADA_BASE[phase] + N_ADA[phase] * step + q
                dve.wait_ge(ada_landed[q % 3], 16 * ada_slot_count(phase, step, q))
                a = acc[:, q // 2, (q % 2) * 512:(q % 2) * 512 + 512]
                if isinstance(step, int):
                    sc = cact[:, step:step + 1]
                else:
                    sc = cact[:, bass.ds(step, 1)]
                if isinstance(step, int) and step == 0:
                    dve.tensor_scalar(a, ada_raw[:, q % 3, :], sc, None, ALU.mult).then_inc(ada_used, 1)
                else:
                    dve.wait_ge(ada_used, u - N_ADA[phase] + 1)
                    dve.scalar_tensor_tensor(a, ada_raw[:, q % 3, :], sc, a, ALU.mult, ALU.add).then_inc(ada_used, 1)

            def feed_forward(n):
                base, cb = in_base(n), chunk_base(n)

                def lo(c, b):
                    dve.wait_ge(act_hi_done, cb + c + 1)
                    if isinstance(c, int):
                        hi, lo_ = act_hi[:, c, :], act_lo[:, c, :]
                    else:
                        hi = act_hi[:, bass.ds(c, 1), :].rearrange("p o t -> p (o t)")
                        lo_ = act_lo[:, bass.ds(c, 1), :].rearrange("p o t -> p (o t)")
                    dve.tensor_tensor(lo_, scr[:, b, :], hi.bitcast(F32), ALU.subtract).then_inc(act_split, 1)

                def chunk(it, c2, with_ada):
                    c = 2 * it + c2
                    if not (isinstance(c, int) and c == 0):
                        lo(c - 1, 1 - c2)
                    dve.wait_ge(tanh_done, cb + c + 1)
                    dve.scalar_tensor_tensor(scr[:, c2, :], scr[:, c2, :], 1.0, bank(2 * c2),
                                             ALU.add, ALU.mult).then_inc(gated, 1)
                    if with_ada:
                        per = N_ADA[n] // 2
                        for q in range(per * c2, per * c2 + per):
                            ada_unit(n, it, q)
                    dve.wait_ge(gated, cb + c + 1)
                    dve.wait_ge(panels_used, base + 2 * c + 2)
                    dve.tensor_tensor(scr[:, c2, :], scr[:, c2, :], bank(2 * c2 + 1), ALU.mult).then_inc(hidden_made, 1)

                chunk(0, 0, True)
                chunk(0, 1, True)
                with dve.Fori(1, KT) as it:
                    chunk(it, 0, True)
                    chunk(it, 1, True)
                with dve.Fori(KT, FT // 2) as it:
                    chunk(it, 0, False)
                    chunk(it, 1, False)
                lo(FT - 1, (FT - 1) % 2)

            def residual(L, gate_chunk, factor, used):
                chunks = 1 if L == 3 else 3
                cols0 = {1: 1, 2: 4, 3: 7}[L]
                for m in range(KT):
                    if m < chunks:
                        dve.wait_ge(ada_cols, cols0 + m + 1)
                        modulation(6, gate_chunk + m)
                    if m == 0:
                        dve.wait_ge(ada_taken, cols0 + 1)
                        link(dve.tensor_scalar(mod[:, 4, :], ada[:, 8 * gate_chunk:8 * gate_chunk + 8], factor,
                                               None, ALU.mult))
                    if m == 3:
                        dve.wait_ge(ada_taken, cols0 + chunks)
                        dve.wait_ge(x_scaled, 8 * L)
                        norm_columns(L)
                    dve.wait_ge(panels_used, used(m))
                    dve.wait_ge(x_scaled, 8 * (L - 1) + m + 1)
                    dve.scalar_tensor_tensor(X[:, m, :], bank(4 + m % 2), mod[:, 4, m:m + 1], X[:, m, :],
                                             ALU.mult, ALU.add).then_inc(z_done, 1)
                    if m >= 1:
                        squares(L, m - 1)
                    sums(L, m)
                squares(L, KT - 1)

            dve.wait_ge(c_tanh, 1)
            link(dve.scalar_tensor_tensor(cact[:, :], cact[:, :], 1.0, colv[:, C_C:C_C + 8], ALU.add, ALU.mult))
            dve.tensor_scalar(cact[:, :], cact[:, :], 0.5, None, ALU.mult).then_inc(ada_acc_start, 1)
            a01 = acc[:, 0:2, :].rearrange("p s c -> p (s c)")
            for m in range(KT):
                sums(0, m)
                if m >= 1:
                    squares(0, m)
            norm(0)
            for k in range(KT):
                normalize_tile(0, k)
                if k >= ADA_DIRECT:
                    dve.wait_ge(ada0_landed[k], 16)
                    dve.wait_ge(ada_acc_start, k - ADA_DIRECT + 1)
                    if k == ADA_DIRECT:
                        ins = dve.tensor_scalar(a01, ada_start[:, k, :], cact[:, k:k + 1], None, ALU.mult)
                    else:
                        ins = dve.scalar_tensor_tensor(a01, ada_start[:, k, :], cact[:, k:k + 1], a01,
                                                       ALU.mult, ALU.add)
                    ins.then_inc(ada_acc_start, 1)
            normalize_tile(0, KT)
            dve.wait_ge(ada_direct, 1)
            link(dve.tensor_tensor(ada[:, 0:16], psum[:, 5, 0:16], colv[:, C_BADA:C_BADA + 16], ALU.add))
            dve.wait_ge(ada_cols, 1)
            link(dve.tensor_reduce(colp[:, 0:16], psum[:, 0:4, :].rearrange("p b (m c) -> p (b m) c", c=P),
                                   AX.X, ALU.add))
            dve.tensor_tensor(ada[:, 0:16], ada[:, 0:16], colp[:, 0:16], ALU.add).then_inc(ada_taken, 1)
            dve.wait_ge(ada_taken, 1)
            norm_columns(0)
            feed_forward(1)
            ob1 = B_FFN1 + IN_PANELS
            residual(1, 2, 0.25, lambda m: ob1 + 3 * m + 3)
            norm(1)
            norm_tiles(1)

            def taken(name):
                return B_MIX + MIX.index(name) + 1

            dve.wait_ge(h_split, 16)
            for i in range(4):
                ins = dve.memset(pads[:, i, 0:16], 0.0)
            ins.then_inc(pool_delta, 1)
            dve.memset(Pc[:, :, :, N_CMP:CPAD], 0.0)
            for kv, name in enumerate(("kc", "vc")):
                dve.wait_ge(panels_used, taken(name))
                for half in range(2):
                    for r in range(2):
                        for g in range(GROUPS):
                            src = psum[64 * g:64 * g + 64, kv, r:T:2].rearrange("p (n i) -> p i n", i=8)
                            dst = blocks[64 * r:64 * r + 64, 2 * kv + half, :, 32 * g:32 * g + 32]
                            pp = posv[64 * r:64 * r + 64, kv:kv + 1, 8 * half:8 * half + 8]\
                                .rearrange("p o i -> p i o").broadcast_to([64, 8, 32])
                            ins = dve.tensor_tensor(dst, src, pp, ALU.add)
                            if r == 1:
                                ins.then_inc(kv_blocks, 1)
            for g, w in enumerate(WINDOWS):
                dve.wait_ge(act_evac, g + 1)
                u = pads[:, g % 2, :]
                s = pads[:, 2 + g % 2, :]
                if g >= 2:
                    dve.wait_ge(pool_split, g - 1)
                link(dve.tensor_tensor(s[:, 1:528], u[:, 1:528], u[:, 0:527], ALU.add))
                step = 2
                cur, oth = s, scr[:, 2:4, :].rearrange("p a t -> p (a t)")
                while step < w:
                    lo_ = 2 * step - 1
                    link(dve.tensor_tensor(oth[:, lo_:528], cur[:, lo_:528], cur[:, lo_ - step:528 - step], ALU.add))
                    cur, oth = oth, cur
                    step *= 2
                head = cst[:, g % 2, 0:16]
                link(dve.tensor_tensor(head, cur[:, 16:32], icnt[:, g, :], ALU.mult))
                link(dve.scalar_tensor_tensor(s[:, 16:528], cur[:, 16:528], 1.0 / w, u[:, 16:528],
                                              ALU.mult, ALU.subtract))
                dve.tensor_tensor(s[:, 16:32], head, u[:, 16:32], ALU.subtract).then_inc(pool_delta, 1)
                if g >= 1:
                    dve.wait_ge(pool_hi_done, g)
                    dve.tensor_tensor(pool_lo[:, g - 1, :], pads[:, 2 + (g - 1) % 2, 16:528],
                                      pool_hi[:, g - 1, :].bitcast(F32), ALU.subtract).then_inc(pool_split, 1)
            dve.wait_ge(pool_hi_done, 4)
            dve.tensor_tensor(pool_lo[:, 3, :], pads[:, 3, 16:528],
                              pool_hi[:, 3, :].bitcast(F32), ALU.subtract).then_inc(pool_split, 1)
            hb = psum[0:CROWS, 2, :]
            sq = scr[0:CROWS, 1, :]
            dve.wait_ge(cmp_sq, 1)
            link(dve.tensor_scalar(sq, sq, GELU_B, 1.0, ALU.mult, ALU.add))
            dve.tensor_tensor(sq, sq, hb, ALU.mult).then_inc(cmp_arg, 1)
            dve.memset(kcB[:, :], 0.0)
            dve.wait_ge(cmp_tanh, 1)
            dve.scalar_tensor_tensor(scr[0:CROWS, 0, :], sq, 1.0, hb, ALU.add, ALU.mult).then_inc(cmp_act, 1)
            dve.wait_ge(cmp_turned, 1)
            dve.tensor_copy(hidden[:, :, 0:CROWS], psum[:, 3, 0:256].rearrange("p (n c) -> p n c", c=64)[:, :, 0:CROWS])\
               .then_inc(cmp_hidden_T, 1)
            dve.wait_ge(cmp_kv, 1)
            for g in range(GROUPS):
                rows = slice(64 * g, 64 * g + 64)
                ins = dve.tensor_scalar(kcB[rows, N_CMP * g:N_CMP * g + N_CMP], psum[rows, 2, 0:N_CMP], 0.5, None, ALU.mult)
            ins.then_inc(cmp_kv_taken, 1)
            for r in range(4):
                ins = dve.tensor_scalar(VC[32 * r:32 * r + 31, :], psum[0:31, 2, 64:192], 0.5, None, ALU.mult)
            ins.then_inc(cmp_kv_taken, 1)
            dve.wait_ge(gates_T, 1)
            gt = psum[:, 4, :].rearrange("p (t c) -> p t c", c=P)[:, :, 0:24]
            dve.tensor_scalar(G[:, :, :], gt, 0.5, 0.5, ALU.mult, ALU.add).then_inc(gates_taken, 1)
            Pv = Pc[:, :, :, 0:N_CMP]
            dve.wait_ge(mixc_landed, 16 * 5)
            for t in range(TT):
                dve.wait_ge(cmp_scored, t // 2 + 1)
                col = (t % 2) * HEADS * N_CMP
                src = psum[:, 6 + t // 2, col:col + HEADS * N_CMP].rearrange("p (j g n) -> p g j n", g=2, n=N_CMP)
                last = dve.tensor_tensor(Pc[:, t, :, 0:N_CMP].rearrange("p (g j) n -> p g j n", g=2), src,
                                         cbias[:, t, :, :].rearrange("p (g j) n -> p g j n", g=2), ALU.add)
            link(last)
            link(dve.tensor_reduce(cst[:, 0, :], Pv, AX.X, ALU.max))

            def over_blocks(v, t):
                return v[:, 8 * t:8 * t + 8].rearrange("p (h o) -> p h o", o=1).broadcast_to([P, 8, N_CMP])

            for t in range(TT):
                ins = dve.tensor_tensor(Pc[:, t, :, 0:N_CMP], Pc[:, t, :, 0:N_CMP], over_blocks(cst[:, 0, :], t), ALU.subtract)
            ins.then_inc(cmp_shifted, 1)
            dve.wait_ge(cmp_exp, 1)
            link(dve.tensor_reduce(cst[:, 1, :], Pv, AX.X, ALU.add))
            link(dve.reciprocal(cst[:, 1, :], cst[:, 1, :]))
            dve.wait_ge(gates_taken, 1)
            link(dve.tensor_tensor(cst[:, 2, :].rearrange("p (t h) -> p t h", t=TT),
                                   cst[:, 1, :].rearrange("p (t h) -> p t h", t=TT), G[:, :, 0:24:3], ALU.mult))
            for t in range(TT):
                ins = dve.tensor_tensor(Pc[:, t, :, 0:N_CMP], Pc[:, t, :, 0:N_CMP], over_blocks(cst[:, 2, :], t), ALU.mult)
            link(ins)
            for t in range(TT):
                ins = dve.tensor_tensor(Pc[:, t, :, 0:N_CMP], Pc[:, t, :, 0:N_CMP],
                                        cmask[:, t:t + 1, 0:N_CMP].broadcast_to([P, 8, N_CMP]), ALU.mult)
            ins.then_inc(cmp_probs, 1)
            for g in range(4):
                dve.wait_ge(poolout_hi, g + 1)
                dve.scalar_tensor_tensor(pool_lo[:, g, :], bank(4 + g % 2), colv[:, C_PSCALE + g:C_PSCALE + g + 1],
                                         pool_hi[:, g, :].bitcast(F32), ALU.mult, ALU.subtract).then_inc(poolout_split, 1)
            for v in range(2):
                dve.wait_ge(v_turned, v + 1)
                dve.tensor_copy(V[:, v, :, :].rearrange("p t c -> p (t c)"), bank(2 + v)).then_inc(v_taken, 1)
            for g in range(GROUPS):
                dve.wait_ge(cmp_PT, g + 1)
                dve.tensor_copy(PcT[:, g, :], bank(4 + g)).then_inc(cmp_PT_taken, 1)

            def alibi(h):
                dve.tensor_scalar(abias[:, h % 2, :], dist[:, :], 2.0 ** -(h + 1), None, ALU.mult).then_inc(bias_made, 1)

            def shift(u):
                h, br = UNITS[u]
                if br == 0:
                    alibi(h)
                dve.wait_ge(bias_made, h + 1)
                if u >= 2:
                    dve.wait_ge(turned, 3 * (u - 1))
                for t in range(TT):
                    n = 4 * u + t
                    w = P * (t + 1)
                    dve.wait_ge(scored, n + 1)
                    dve.tensor_tensor_reduce(Pr[:, u % 2, P_OFF[t]:P_OFF[t] + w], bank(1 + n % 3, w),
                                             abias[:, h % 2, T - w:T], -1.0, 1e30, ALU.add, ALU.min,
                                             nmax[:, n:n + 1]).then_inc(shifted, 1)

            def normalize(u):
                h, br = UNITS[u]
                dve.wait_ge(exp_done, 4 * u + 4)
                s4 = slice(4 * u, 4 * u + 4)
                link(dve.reciprocal(pscl[:, s4], psumv[:, s4]))
                link(dve.tensor_tensor(pscl[:, s4], pscl[:, s4], G[:, :, 3 * h + 1 + br], ALU.mult))
                for t in range(TT):
                    n = 4 * u + t
                    pr = Pr[:, u % 2, P_OFF[t]:P_OFF[t] + P * (t + 1)]
                    ins = dve.tensor_scalar(pr, pr, pscl[:, n:n + 1], None, ALU.mult)
                ins.then_inc(probs_ready, 1)

            def take_turned(u):
                if u >= 2:
                    dve.wait_ge(o_made, u - 1)
                dve.wait_ge(turned, 3 * u + 2)
                off = PT_OFF[1]
                dve.tensor_copy(PT[:, u % 2, off:off + 384], bank(PT_BANK[1], 384)).then_inc(turned_dve, 1)

            def take_head(h):
                j, g = h % HPG, h // HPG
                dve.wait_ge(o_hi_done, h + 1)
                rows = slice(64 * g, 64 * g + 64)
                dve.tensor_tensor(o_lo[rows, j, :], psum[rows, 6 + h % 2, :], o_hi[rows, j, :].bitcast(F32),
                                  ALU.subtract).then_inc(o_split, 1)

            for s in range(len(UNITS) + 2):
                if s < len(UNITS):
                    shift(s)
                if 1 <= s <= len(UNITS):
                    take_turned(s - 1)
                if s < len(UNITS):
                    normalize(s)
                if s >= 2 and UNITS[s - 2][1] == 1:
                    take_head(UNITS[s - 2][0])

            def mixed_lo_part(m):
                dve.wait_ge(br_hi, m + 1)
                dve.tensor_tensor(mixed_lo[:, m, :], tab[:, m % 2, 0, :], mixed_hi[:, m, :].bitcast(F32),
                                  ALU.subtract).then_inc(br_split, 1)

            for m in range(KT):
                b = 4 * (m % 2)
                for q in range(6):
                    ada_unit("mix", m, q)
                dve.wait_ge(panels_used, B_BRANCH + 3 * m + 3)
                for q in range(2):
                    dve.wait_ge(br_tanh, 2 * m + q + 1)
                    dve.scalar_tensor_tensor(tab[:, m % 2, q, :], tab[:, m % 2, q, :], 1.0, bank(b + 2 + q),
                                             ALU.add, ALU.mult).then_inc(br_gated, 1)
                dve.wait_ge(br_gated, 2 * m + 2)
                dve.tensor_tensor(tab[:, m % 2, 0, :], tab[:, m % 2, 0, :], tab[:, m % 2, 1, :],
                                  ALU.add).then_inc(br_mixed, 1)
                mixed_lo_part(m)
            residual(2, 5, 0.5, lambda m: B_MIXOUT + m + 1)
            norm(2)
            norm_tiles(2)
            feed_forward(2)
            ob2 = B_FFN2 + IN_PANELS
            residual(3, 8, 0.25, lambda m: ob2 + 3 * m + 3)
            norm(3)
            norm_tiles(3)


def _tiles(w):
    K, N = w.shape
    return np.ascontiguousarray(w.reshape(K // P, P, N // P, P).transpose(2, 1, 0, 3)).reshape(N // P, P, K)


def _constants():
    p = np.arange(P)[:, None]
    rel = np.arange(T)[None, :] - (T - P)
    dist = np.where(rel > p, -1e34, -(p - rel)).astype(np.float32)
    t = np.arange(T)
    end = np.arange(N_CMP) * STRIDE + 2 * STRIDE - 1
    d = t[:, None] - end[None, :]
    slopes = 2.0 ** -np.arange(1.0, HEADS + 1)
    cb = np.where(d[:, None, :] < 0, NEG, -slopes[None, :, None] * d[:, None, :]).astype(np.float32)
    cb = cb.reshape(TT, P, HEADS, N_CMP).transpose(1, 0, 2, 3)
    cm = np.zeros((T, CPAD), np.float32)
    cm[:, :N_CMP] = d >= 0
    cm = cm.reshape(TT, P, CPAD).transpose(1, 0, 2)
    ic = np.stack([1.0 / np.minimum(np.arange(16) + 1, w) for w in WINDOWS]).astype(np.float32)
    return {"ident": np.eye(P, dtype=np.float32), "dist": dist, "cbias": np.ascontiguousarray(cb),
            "cmask": np.ascontiguousarray(cm), "icnt": np.ascontiguousarray(np.broadcast_to(ic, (P, 4, 16)))}


def _mixer_columns():
    q0, kv0, g0 = 512, 1024, 1792
    br0 = g0 + 24
    at = {f"u{g}": np.arange(P) + P * g for g in range(4)}
    for j in range(4):
        at[f"q{j}"] = np.concatenate([np.arange(64) + q0 + 64 * j, np.arange(64) + q0 + 64 * (4 + j)])
    for i, n in enumerate(("kc", "vc", "kslc", "vslc", "kwin", "vwin")):
        at[n] = np.arange(P) + kv0 + P * i
    at["gate"] = np.concatenate([np.arange(24) + g0, np.full(P - 24, -1)])
    order = [at[n] for n in MIX8]
    for m in range(KT):
        order += [np.arange(P) + br0 + P * m, np.arange(P) + br0 + D + P * m]
    return np.concatenate(order)


def kernel(**inputs):
    import concourse.bacc as _bacc
    from concourse.bass_utils import run_bass_kernel_spmd as _run

    a = {k: np.asarray(v) for k, v in inputs.items()}

    def column(v):
        return v.reshape(-1, P).T

    arrays = {}
    arrays["xT"] = np.ascontiguousarray(a["x"][0].T.reshape(KT, P, T).transpose(1, 0, 2))
    arrays["cols"] = np.ascontiguousarray(np.concatenate(
        [column(a["b_ada"][0])] + [column(v) for v in (a["ln_in_g"], a["ln1_g"][0], a["ln2_g"][0], a["ln3_g"][0],
                                                      a["ln_in_b"], a["ln1_b"][0], a["ln2_b"][0], a["ln3_b"][0])]
        + [column(a["pool_scale"][0]), column(a["c"][0])], axis=1))
    arrays["ada_w"] = np.ascontiguousarray(a["w_ada"][0]).reshape(KT, P, 9 * D)

    def ffn_in(w):
        return np.stack([_tiles(w[:, :F]), _tiles(w[:, F:])], axis=1)

    arrays["ffn_in"] = np.stack([ffn_in(a["ffn1_w_in"][0]), ffn_in(a["ffn2_w_in"][0])])
    arrays["ffn_out"] = np.stack([_tiles(a["ffn1_w_out"][0]), _tiles(a["ffn2_w_out"][0])])
    cols = _mixer_columns()
    padded = np.concatenate([a["w_mix_in"][0], np.zeros((D, 1), np.float32)], axis=1)
    arrays["mix_w"] = _tiles(padded[:, cols])
    arrays["pool_w"] = np.ascontiguousarray(a["pool_w"][0].transpose(1, 0, 2)).reshape(P, 4 * P)
    heads = np.concatenate([np.concatenate([np.arange(64) + 64 * j, np.arange(64) + 64 * (4 + j)]) for j in range(4)])
    arrays["branch_w"] = np.concatenate([_tiles(a["w_branch_a"][0]), _tiles(a["w_branch_b"][0][heads])], axis=2)
    arrays["mixout_w"] = _tiles(a["w_mix_out"][0])
    arrays["w1"] = np.stack([a[n][0].reshape(PAIRS, P, 256).transpose(1, 0, 2) for n in ("cmp_k_w1", "cmp_v_w1")])
    arrays["w2"] = np.ascontiguousarray(
        np.stack([a[n][0].reshape(HID_T, P, HEAD) for n in ("cmp_k_w2", "cmp_v_w2")]).transpose(2, 0, 1, 3))
    arrays["pos"] = np.ascontiguousarray(
        np.stack([a[n][0].reshape(PAIRS, P).T for n in ("cmp_pos_k", "cmp_pos_v")], axis=1))
    arrays.update(_constants())

    nc = _bacc.Bacc("TRN2", target_bir_lowering=False, num_devices=1)
    ins = {}
    for name in arrays:
        arrays[name] = np.ascontiguousarray(arrays[name])
        ins[name] = nc.dram_tensor(f"in_{name}", arrays[name].shape, F32, kind="ExternalInput").ap()
    out = nc.dram_tensor("out_0", (KT, P, T), F32, kind="ExternalOutput").ap()
    build(nc, *[ins[n] for n in ("xT", "cols", "ada_w", "ffn_in", "ffn_out", "mix_w", "pool_w", "branch_w",
                                 "mixout_w", "w1", "w2", "pos", "ident", "dist", "cbias", "cmask", "icnt")], out)
    r = _run(nc, [{f"in_{n}": v for n, v in arrays.items()}], core_ids=[0])
    got = r.results[0]["out_0"]
    return np.ascontiguousarray(got.reshape(D, T).T).reshape(1, T, D)
```

```python
import math
from contextlib import ExitStack

import numpy as np
import concourse.bass as bass
from concourse import mybir

F32 = mybir.dt.float32
F32R = mybir.dt.float32r
ALU = mybir.AluOpType
ACT = mybir.ActivationFunctionType
AX = mybir.AxisListType

P = 128
D = 1024
T = 512
KT = D // P
TT = T // P
F = 2816
FT = F // P
HEADS, HEAD = 8, 64
GROUPS = 2
HPG = HEADS // GROUPS
STRIDE = 16
N_CMP = T // STRIDE - 1
CROWS = 32 + N_CMP
CPAD = 32
HID_T = 2
PAIRS = 16
WINDOWS = (2, 4, 8, 16)
NEG = -1e30
EPS = 1e-5
ALPHA = 2.0 ** 0.25
GELU_A, GELU_B = math.sqrt(2.0 / math.pi), 0.044715

OUT_SPLIT = (8, 7, 7)
IN_PANELS = 2 * FT
OUT_PANELS = 3 * KT
MIX = ["kc", "vc", "u0", "u1", "u2", "u3", "gate", "q0", "q1", "q2", "q3", "kslc", "kwin",
       "poolw", "vslc", "vwin"]
MIX8 = [n for n in MIX if n != "poolw"]
B_FFN1 = 0
B_MIX = B_FFN1 + IN_PANELS + OUT_PANELS
B_BRANCH = B_MIX + len(MIX)
B_MIXOUT = B_BRANCH + 3 * KT
B_FFN2 = B_MIXOUT + KT
N_PANELS = B_FFN2 + IN_PANELS + OUT_PANELS
assert B_MIX % 4 == 0 and B_FFN2 % 4 == 0

C_BADA, C_LNG, C_LNB, C_PSCALE, C_C = 0, 72, 104, 136, 140
N_COLS = 148
LNS = 4

P_OFF = [0, 128, 384, 768]
P_LEN = 1280
PT_OFF = [0, 512, 896, 1152]
PT_GROUPS = [[0], [1], [2, 3]]
PT_BANK = [4, 5, 0]
FIRST = 6
FIRST_LOADS = [[0, 1], [], [2], [3], [], [4], [5], [6]]
FIRST_SPLITS = [[2], [3], [], [4], [5], [], [6], []]
POOL_NORM = 5
LAST_ORDER = [0, 1, 5, 2, 3, 6, 4, 7]
UNITS = [(h, br) for h in range(HEADS) for br in range(2)]

SBUF_BASE = 16512
O_X = SBUF_BASE
O_HHI = O_X + 4 * KT * T
O_HLO = O_HHI + 4 * KT * T
O_RAW = O_HLO + 4 * KT * T
O_WHI = O_RAW + 2 * 4096
O_WLO = O_WHI + 4 * 4096
O_ADARAW = O_WLO + 4 * 4096
O_ACC = O_ADARAW + 3 * 2048
O_SCR = O_ACC + 3 * 4096
O_REGION = O_SCR + 4 * 2048
O_CONST = O_REGION + 2 * FT * 4 * T


def need(eng, sem, value):
    if not isinstance(value, int) or value > 0:
        eng.wait_ge(sem, value)


def build(nc, xT, cols, ada_w, ada1, ffn_in, ffn_out, mix_w, pool_w, branch_w, mixout_w,
          w1, w2, pos, ident_in, dist_in, cbias_in, cmask_in, icnt_in, out):
    with ExitStack() as ctx:
        def at(name, shape, offset, dt=F32):
            return nc.alloc_sbuf_tensor_at(name, shape, dt, offset=offset)

        ctx.enter_context(nc.sbuf_tensor("whole", [P, 53200], F32))
        X = at("X", [P, KT, T], O_X)
        h_hi = at("h_hi", [P, KT, T], O_HHI, F32R)
        h_lo = at("h_lo", [P, KT, T], O_HLO, F32R)
        raw = at("raw", [P, 2, 1024], O_RAW)
        w_hi = at("w_hi", [P, 4, 1024], O_WHI, F32R)
        w_lo = at("w_lo", [P, 4, 1024], O_WLO, F32R)
        ada_raw = at("ada_raw", [P, 3, 512], O_ADARAW)
        acc = at("acc", [P, 3, 1024], O_ACC)
        scr = at("scr", [P, 4, T], O_SCR)
        hbuf = at("hbuf", [P, KT, T], O_REGION + 20480)
        act_hi = at("act_hi", [P, FT, T], O_REGION, F32R)
        act_lo = at("act_lo", [P, FT, T], O_REGION + FT * 2048, F32R)
        ada_first = [at(f"ada_first{k}", [P, KT, 2 * P], O_REGION + (8192 * k if k < 2 else 20480 + 8192 * k))
                     for k in range(KT)]
        R = O_REGION
        qT = at("qT", [P, 4, T], R)
        kT = at("kT", [P, 2, T], R + 8192)
        V = at("V", [P, 2, TT, P], R + 12288)
        vT = at("vT", [P, 2, T], R + 16384)
        w1v = at("w1v", [P, PAIRS, 256], R)
        blocks = at("blocks", [P, 4, PAIRS // 2, 64], R + 20480)
        PT = at("PT", [P, 2, P_LEN], R + 20480)
        Pr = at("Pr", [P, 2, P_LEN], R + 30720)
        pads = at("pads", [P, 4, 528], R + 30720)
        hidden = at("hidden", [P, 4, 64], R + 39168)
        cbias = at("cbias", [P, TT, HEADS, N_CMP], R + 40960)
        PcT = at("PcT", [P, GROUPS, T], R + 40960)
        dist = at("dist", [P, T], R + 45056)
        abias = at("abias", [P, 2, T], R + 47104)
        Pc = at("Pc", [P, TT, HEADS, CPAD], R + 51200)
        cmask = at("cmask", [P, TT, CPAD], R + 55296)
        G = at("G", [P, TT, 24], R + 55808)
        nmax = at("nmax", [P, 64], R + 56192)
        psumv = at("psumv", [P, 64], R + 56448)
        pscl = at("pscl", [P, 64], R + 56704)
        cst = at("cst", [P, 3, 32], R + 56960)
        pool_hi = at("pool_hi", [P, 4, T], R + 57344, F32R)
        pool_lo = at("pool_lo", [P, 4, T], R + 65536, F32R)
        o_hi = at("o_hi", [P, 4, T], R + 73728, F32R)
        o_lo = at("o_lo", [P, 4, T], R + 81920, F32R)
        w1k = at("w1k", [P, PAIRS, 256], R + 73728)
        mixed_hi = at("mixed_hi", [P, KT, T], R, F32R)
        mixed_lo = at("mixed_lo", [P, KT, T], R + 16384, F32R)
        tab = at("tab", [P, 2, 2, T], R + 32768)
        o = O_CONST
        ident = at("ident", [P, P], o)
        ones = at("ones", [P, P], o + 512)
        VC = at("VC", [P, P], o + 1024)
        colv = at("colv", [P, N_COLS], o + 1536)
        ada = at("ada", [P, 72], o + 2144)
        mod = at("mod", [P, 6, 8], o + 2432)
        cact = at("cact", [P, 8], o + 2624)
        posv = at("posv", [P, 2, PAIRS], o + 2688)
        w2s = at("w2s", [P, 2, HID_T, HEAD], o + 2816)
        icnt = at("icnt", [P, 4, 16], o + 3840)
        kcB = at("kcB", [P, 2 * N_CMP], o + 4096)
        st = at("st", [P, 8, TT], o + 4352)
        colp = at("colp", [P, 24], o + 4480)
        assert o + 4576 <= 229344

        psum = ctx.enter_context(nc.psum_tensor("psum", [P, 8, T], F32))

        def bank(n, w=T):
            return psum[:, n, 0:w]

        def sem(name):
            return ctx.enter_context(nc.semaphore(name))

        raw_landed = [sem(f"raw_landed{i}") for i in range(2)]
        ada_landed = [sem(f"ada_landed{i}") for i in range(3)]
        ada0_landed = [sem(f"ada0_landed{i}") for i in range(KT)]
        x_landed = [sem(f"x_landed{i}") for i in range(4)]
        const_landed = sem("const_landed")
        cols_landed = sem("cols_landed")
        mixc_landed = sem("mixc_landed")
        out_stored = sem("out_stored")
        split_hi = sem("split_hi")
        split_done = sem("split_done")
        panels_used = sem("panels_used")
        memset_done = sem("memset_done")
        c_tanh = sem("c_tanh")
        ada_used = sem("ada_used")
        ada_acc_start = sem("ada_acc_start")
        ada_cols = sem("ada_cols")
        ada_taken = sem("ada_taken")
        dve_chain = sem("dve_chain")
        act_chain = sem("act_chain")
        s_added = sem("s_added")
        q_added = sem("q_added")
        sq_done = sem("sq_done")
        stats_ready = sem("stats_ready")
        stats_small = sem("stats_small")
        rows_made = sem("rows_made")
        rows_ready = sem("rows_ready")
        rows_copied = sem("rows_copied")
        first_step = sem("first_step")
        first_acc = sem("first_acc")
        first_cols = sem("first_cols")
        first_summed = sem("first_summed")
        first_mod = sem("first_mod")
        xhat_pool = sem("xhat_pool")
        pool_scaled = sem("pool_scaled")
        cmp_turned = sem("cmp_turned")
        cmp_hidden_T = sem("cmp_hidden_T")
        var_done = sem("var_done")
        std_done = sem("std_done")
        mod_ready = sem("mod_ready")
        scaled = sem("scaled")
        xhat_done = sem("xhat_done")
        h_made = sem("h_made")
        h_hi_done = sem("h_hi_done")
        h_split = sem("h_split")
        x_scaled = sem("x_scaled")
        z_done = sem("z_done")
        tanh_done = sem("tanh_done")
        gated = sem("gated")
        hidden_made = sem("hidden_made")
        act_hi_done = sem("act_hi_done")
        act_split = sem("act_split")
        kv_blocks = sem("kv_blocks")
        act_evac = sem("act_evac")
        pool_delta = sem("pool_delta")
        pool_hi_done = sem("pool_hi_done")
        pool_split = sem("pool_split")
        pool_mixed = sem("pool_mixed")
        poolout_hi = sem("poolout_hi")
        poolout_split = sem("poolout_split")
        cmp_hidden = sem("cmp_hidden")
        cmp_sq = sem("cmp_sq")
        cmp_arg = sem("cmp_arg")
        cmp_tanh = sem("cmp_tanh")
        cmp_act = sem("cmp_act")
        cmp_kv = sem("cmp_kv")
        cmp_kv_taken = sem("cmp_kv_taken")
        gates_T = sem("gates_T")
        gates_taken = sem("gates_taken")
        cmp_scored = sem("cmp_scored")
        cmp_shifted = sem("cmp_shifted")
        cmp_exp = sem("cmp_exp")
        cmp_probs = sem("cmp_probs")
        cmp_PT = sem("cmp_PT")
        cmp_PT_taken = sem("cmp_PT_taken")
        v_turned = sem("v_turned")
        v_taken = sem("v_taken")
        bias_made = sem("bias_made")
        scored = sem("scored")
        shifted = sem("shifted")
        exp_done = sem("exp_done")
        probs_ready = sem("probs_ready")
        turned = sem("turned")
        turned_act = sem("turned_act")
        turned_dve = sem("turned_dve")
        o_made = sem("o_made")
        o_hi_done = sem("o_hi_done")
        o_split = sem("o_split")
        br_tanh = sem("br_tanh")
        br_gated = sem("br_gated")
        br_mixed = sem("br_mixed")
        br_hi = sem("br_hi")
        br_split = sem("br_split")

        block = ctx.enter_context(nc.Block())

        ADA_BASE = {1: 0, "mix": 48, 2: 96}
        N_ADA = {1: 6, "mix": 6, 2: 2}
        ADA_CHUNK = {1: 2, "mix": 5, 2: 8}
        ADA_SLOT = {1: [0, 0, 0], "mix": [16, 16, 16], 2: [32, 32, 32]}

        def ada_slot_count(phase, step, q):
            per = 2 if N_ADA[phase] == 6 else 1
            return ADA_SLOT[phase][q % 3] + per * step + q // 3 + 1

        def in_base(n):
            return B_FFN1 if n == 1 else B_FFN2

        def chunk_base(n):
            return 0 if n == 1 else FT

        @block.sync
        def _(sp):
            def panel(p, src, width=1024, slot=None):
                need(sp, split_done, p - 1)
                sp.dma_start(raw[:, slot, 0:width], src).then_inc(raw_landed[slot], 16)

            def ada_unit(phase, step, q):
                u = ADA_BASE[phase] + N_ADA[phase] * step + q
                need(sp, ada_used, u - (2 if N_ADA[phase] == 6 else 1))
                col = (ADA_CHUNK[phase] + q // 2) * 1024 + (q % 2) * 512
                sp.dma_start(ada_raw[:, q % 3, :], ada_w[step, :, col:col + 512]).then_inc(
                    ada_landed[q % 3], 16)

            def feed_forward(n):
                base = in_base(n)

                def step(it, with_ada, with_panels=True):
                    for j in range(4):
                        c = 2 * it + 2 + j // 2
                        if with_panels:
                            panel(base + 4 * it + 4 + j, ffn_in[n - 1, c, j % 2, :, :], slot=j % 2)
                        if with_ada:
                            per = N_ADA[n]
                            for q in ([0, 1], [2], [3, 4], [5])[j]:
                                if q < per:
                                    ada_unit(n, it, q)

                for p in range(7 if n == 1 else 0, 8):
                    panel(base + p, ffn_in[n - 1, p // 2, p % 2, :, :], slot=p % 2)
                step(0, True, False)
                with sp.Fori(1, KT) as it:
                    step(it, True)
                with sp.Fori(KT, FT // 2 - 1) as it:
                    step(it, False)
                ob = base + IN_PANELS
                with sp.Fori(0, 2) as it:
                    for m4 in range(4):
                        off = 0
                        for j, kn in enumerate(OUT_SPLIT):
                            i = 3 * m4 + j
                            panel(ob + 12 * it + i,
                                  ffn_out[n - 1, 4 * it + m4, :, off * P:(off + kn) * P],
                                  width=kn * P, slot=i % 2)
                            off += kn

            for i in range(4):
                sp.dma_start(X[:, 2 * i:2 * i + 2, :], xT[:, 2 * i:2 * i + 2, :]).then_inc(
                    x_landed[i], 16)
            sp.dma_start(ada_first[0][:, :, :], ada1[0, :, :, :]).then_inc(ada0_landed[0], 16)
            for k in range(KT):
                for p in FIRST_LOADS[k]:
                    panel(p, ffn_in[0, p // 2, p % 2, :, :], slot=p % 2)
                if k:
                    sp.dma_start(ada_first[k][:, :, :], ada1[k, :, :, :]).then_inc(ada0_landed[k], 16)
            feed_forward(1)
            k8 = 0
            for i, name in enumerate(MIX):
                p = B_MIX + i
                if name == "poolw":
                    panel(p, pool_w[:, :], width=512, slot=p % 2)
                else:
                    panel(p, mix_w[k8, :, :], slot=p % 2)
                    k8 += 1

            def branch_panel(i):
                m, j = divmod(i, 3)
                if m < KT:
                    src = branch_w[m, :, :] if j == 2 else mix_w[k8 + 2 * m + j, :, :]
                    panel(B_BRANCH + i, src, slot=(B_BRANCH + i) % 2)

            branch_panel(0)
            branch_panel(1)
            for i in range(3 * KT):
                branch_panel(i + 2)
                for q in range(2 * (i % 3), 2 * (i % 3) + 2):
                    ada_unit("mix", i // 3, q)
            for m in range(KT):
                p = B_MIXOUT + m
                panel(p, mixout_w[m, :, :], slot=p % 2)
            feed_forward(2)
            for i, m in enumerate(LAST_ORDER):
                sp.wait_ge(x_scaled, 8 * 3 + i + 1)
                sp.dma_start(out[m, :, :], X[:, m, :]).then_inc(out_stored, 16)
            sp.wait_ge(out_stored, 16 * KT)

        @block.gpsimd
        def _(gp):
            gp.memset(ones[:, :], 1.0).then_inc(memset_done, 1)

            for m in range(1, KT):
                if m % 2 == 0 or m == 1:
                    gp.wait_ge(x_landed[m // 2], 16)
                need(gp, s_added, m - 1)
                a = X[:, 0, :] if m == 1 else scr[:, 0, :]
                gp.tensor_tensor(scr[:, 0, :], a, X[:, m, :], ALU.add).then_inc(s_added, 1)

            def split(p, slot):
                gp.wait_ge(split_hi, p + 1)
                gp.tensor_tensor(w_lo[:, slot, :], raw[:, slot % 2, :], w_hi[:, slot, :].bitcast(F32),
                                 ALU.subtract).then_inc(split_done, 1)

            def splits(start, end):
                head, tail = -(-start // 4), end // 4
                for p in range(start, 4 * head):
                    split(p, p % 4)
                with gp.Fori(head, tail) as it:
                    for slot in range(4):
                        split(4 * it + slot, slot)
                for p in range(4 * tail, end):
                    split(p, p % 4)

            split(0, 0)
            split(1, 1)
            for L, end in enumerate((B_FFN1, B_MIX, B_FFN2)):
                if L:
                    splits(start, end + 3)
                start = end + 3 if L else 7
                for m in range(KT):
                    if L == 0:
                        for p in FIRST_SPLITS[m]:
                            split(p, p % 4)
                    gp.wait_ge(h_hi_done, 8 * L + m + 1)
                    gp.tensor_tensor(h_lo[:, m, :], hbuf[:, m, :], h_hi[:, m, :].bitcast(F32),
                                     ALU.subtract).then_inc(h_split, 1)
            splits(start, N_PANELS)
            gp.wait_ge(z_done, 8 * 3)
            for m in range(POOL_NORM, KT):
                gp.wait_ge(rows_copied, 2 * 1 + 1)
                gp.tensor_tensor(X[:, m, :], X[:, m, :], scr[:, 2, :], ALU.mult).then_inc(pool_scaled, 1)
                gp.wait_ge(rows_copied, 2 * 1 + 2)
                gp.wait_ge(pool_scaled, m - POOL_NORM + 1)
                gp.tensor_tensor(X[:, m, :], X[:, m, :], scr[:, 3, :], ALU.subtract).then_inc(xhat_pool, 1)

        @block.tensor
        def _(pe):
            def product(o_, wslot, kk, xh, xl, first, last):
                ws = slice(kk * P, (kk + 1) * P)
                pe.matmul(o_, w_hi[:, wslot, ws], xh, start=first, stop=False)
                pe.matmul(o_, w_hi[:, wslot, ws], xl, start=False, stop=False)
                return pe.matmul(o_, w_lo[:, wslot, ws], xh, start=False, stop=last)

            def panel_over_h(p, wslot, b, h_wait=None):
                pe.wait_ge(split_done, p + 1)
                for k in range(KT):
                    if h_wait is not None:
                        pe.wait_ge(h_split, h_wait + k + 1)
                    ins = product(bank(b), wslot, k, h_hi[:, k, :], h_lo[:, k, :], k == 0, k == KT - 1)
                ins.then_inc(panels_used, 1)

            def turn_modulation(s, b, taken):
                need(pe, ada_taken, taken)
                for m in range(8):
                    ins = pe.transpose(psum[:, b + m // 4, (m % 4) * P:(m % 4) * P + P],
                                       acc[:, s, m * P:(m + 1) * P], ident[:, :])
                ins.then_inc(ada_cols, 1)

            def turn_first(k):
                pe.wait_ge(first_acc, 2 * (k + 1))
                if k == 0:
                    pe.wait_ge(rows_copied, 2)
                if k >= 2:
                    pe.wait_ge(first_summed, k - 1)
                for q in range(4):
                    ins = pe.transpose(psum[:, 6 + k % 2, q * P:(q + 1) * P],
                                       acc[:, k % 2, q * P:(q + 1) * P], ident[:, :])
                ins.then_inc(first_cols, 1)

            def norm_stats(L):
                for i, added in enumerate((s_added, q_added)):
                    pe.wait_ge(added, 7 * (L + 1))
                    for t in range(TT):
                        ins = pe.transpose(psum[:, 6 + i, t * P:(t + 1) * P],
                                           scr[:, i, t * P:(t + 1) * P], ident[:, :])
                    ins.then_inc(stats_ready, 1)
                for i in range(2):
                    pe.wait_ge(rows_made, 2 * L + i + 1)
                    pe.matmul(bank(6 + i), ones[:, :], scr[:, i, :], start=True, stop=True).then_inc(rows_ready, 1)

            def feed_forward(n):
                base, cb = in_base(n), chunk_base(n)

                def chunk(it, c2, b):
                    c = 2 * it + c2
                    need(pe, hidden_made, cb + c - 1 if b == 2 * c2 else 0)
                    for gu in range(2):
                        panel_over_h(base + 2 * c + gu, 2 * c2 + gu, b + gu)

                h0 = 0 if n == 1 else 16
                if n == 1:
                    turn_first(0)
                for i in range(FIRST * KT):
                    k, m = divmod(i, FIRST)
                    if m == 0:
                        if n == 1 and k + 1 < KT:
                            turn_first(k + 1)
                        pe.wait_ge(h_split, h0 + k + 1)
                    if i % 8 == 0:
                        pe.wait_ge(split_done, base + i // 8 + 1)
                    ins = product(bank(m), (i // 8) % 4, i % 8, h_hi[:, k, :], h_lo[:, k, :], k == 0, k == KT - 1)
                    if i % 8 == 7:
                        ins.then_inc(panels_used, 1)
                chunk(1, 1, 6)
                with pe.Fori(2, FT // 2) as it:
                    chunk(it, 0, 0)
                    chunk(it, 1, 2)
                ob = base + IN_PANELS
                pe.wait_ge(ada_used, ADA_BASE[n] + 8 * N_ADA[n])
                zb = 0 if n == 1 else 16
                ada0 = 0 if n == 1 else 6

                def out_tiles(it):
                    for m4 in range(4):
                        m = 4 * it + m4
                        if it == 0 and m4 < N_ADA[n] // 2:
                            turn_modulation(m4, 6, ada0 + m4)
                        if not isinstance(it, int) or m >= 2:
                            pe.wait_ge(z_done, zb + m - 1)
                        k = 0
                        for j, kn in enumerate(OUT_SPLIT):
                            i = 3 * m4 + j
                            pe.wait_ge(split_done, ob + 12 * it + i + 1)
                            if it == 0 and m4 == 0:
                                pe.wait_ge(act_split, cb + k + kn)
                            for kk in range(kn):
                                ins = product(bank(4 + m4 % 2), i % 4, kk, act_hi[:, k, :],
                                              act_lo[:, k, :], k == 0, k == FT - 1)
                                k += 1
                            ins.then_inc(panels_used, 1)

                out_tiles(0)
                out_tiles(1)
                pe.wait_ge(ada_taken, ada0 + N_ADA[n] // 2)
                norm_stats(1 if n == 1 else 3)

            pe.wait_ge(memset_done, 1)
            pe.wait_ge(const_landed, 16 * 4)
            norm_stats(0)
            feed_forward(1)

            pidx = {name: B_MIX + i for i, name in enumerate(MIX)}

            def k8_panel(name, h_wait=None):
                n = MIX8.index(name)
                b = n % 2
                if n in (2, 3):
                    pe.wait_ge(kv_blocks, 4 * (n - 1))
                if n > 3:
                    pe.wait_ge(act_evac, n - 3)
                p = pidx[name]
                panel_over_h(p, p % 4, b, h_wait)

            k8_panel("kc", 8)
            for name in ("vc", "u0", "u1", "u2", "u3"):
                k8_panel(name)
            pe.wait_ge(mixc_landed, 16 * 5)
            pe.wait_ge(kv_blocks, 8)
            for kv in range(2):
                for i in range(PAIRS):
                    half = i // 8
                    ins = pe.matmul(psum[0:CROWS, 2, 256 * kv:256 * kv + 256],
                                    blocks[:, 2 * kv + half, i % 8, half:half + CROWS], (w1k, w1v)[kv][:, i, :],
                                    start=(i == 0), stop=(i == PAIRS - 1))
            ins.then_inc(cmp_hidden, 1)
            k8_panel("gate")
            pe.wait_ge(cmp_act, 1)
            for n in range(4):
                ins = pe.transpose(psum[:, 3, 64 * n:64 * n + CROWS], scr[0:CROWS, 0, P * n:P * n + P],
                                   ident[0:CROWS, 0:CROWS])
            ins.then_inc(cmp_turned, 1)
            k8_panel("q0")
            pe.wait_ge(cmp_hidden_T, 1)
            for g in range(GROUPS):
                for kt in range(HID_T):
                    pe.matmul(psum[64 * g:64 * g + 64, 2, 0:N_CMP], w2s[:, 0, kt, :],
                              hidden[:, kt, 32 * g:32 * g + N_CMP], start=(kt == 0), stop=(kt == 1))
            for g in range(GROUPS):
                for kt in range(HID_T):
                    ins = pe.matmul(psum[0:31, 2, 64 + 64 * g:128 + 64 * g],
                                    hidden[:, 2 + kt, 32 * g:32 * g + N_CMP], w2s[:, 1, kt, :],
                                    start=(kt == 0), stop=(kt == 1))
            ins.then_inc(cmp_kv, 1)
            pe.wait_ge(act_evac, MIX8.index("gate") - 1)
            for t in range(TT):
                ins = pe.transpose(psum[:, 4, P * t:P * t + P], vT[:, 0, t * P:(t + 1) * P], ident[:, :])
            ins.then_inc(gates_T, 1)
            for name in ("q1", "q2", "q3"):
                k8_panel(name)
            pe.wait_ge(cmp_kv_taken, 2)
            pe.wait_ge(act_evac, MIX8.index("q3") - 1)
            for t in range(TT):
                for j in range(HPG):
                    col = ((t % 2) * HPG + j) * 2 * N_CMP
                    ins = pe.matmul(psum[:, 6 + t // 2, col:col + 2 * N_CMP], qT[:, j, t * P:(t + 1) * P],
                                    kcB[:, :], start=True, stop=True)
                if t % 2:
                    ins.then_inc(cmp_scored, 1)
            k8_panel("kslc")
            k8_panel("kwin")
            p = pidx["poolw"]
            pe.wait_ge(split_done, p + 1)
            pe.wait_ge(pool_split, 4)
            pe.wait_ge(gates_taken, 1)
            for g in range(4):
                if g >= 2:
                    pe.wait_ge(poolout_split, g - 1)
                ins = product(bank(4 + g % 2), p % 4, g, pool_hi[:, g, :], pool_lo[:, g, :], True, True)
                if g < 3:
                    ins.then_inc(pool_mixed, 1)
            ins.then_inc(panels_used, 1)
            k8_panel("vslc")
            k8_panel("vwin")
            for v in range(2):
                pe.wait_ge(act_evac, MIX8.index("vslc") - 1 + v)
                for t in range(TT):
                    ins = pe.transpose(psum[:, 2 + v, P * t:P * t + P], vT[:, v, t * P:(t + 1) * P], ident[:, :])
                ins.then_inc(v_turned, 1)
            pe.wait_ge(cmp_probs, 1)
            pe.wait_ge(poolout_split, 4)
            for g in range(GROUPS):
                for t in range(TT):
                    ins = pe.transpose(psum[:, 4 + g, P * t:P * t + P],
                                       Pc[:, t, HPG * g:HPG * g + HPG, :].rearrange("p h n -> p (h n)"),
                                       ident[:, :])
                ins.then_inc(cmp_PT, 1)

            def scores(u):
                h, br = UNITS[u]
                j, g = h % HPG, h // HPG
                for t in range(TT):
                    n = 4 * u + t
                    if n >= 3:
                        pe.wait_ge(shifted, n - 2)
                    elif n:
                        pe.wait_ge(v_taken, n)
                    w = P * (t + 1)
                    pe.matmul(bank(1 + n % 3, w), qT[64 * g:64 * g + 64, j, t * P:(t + 1) * P],
                              kT[64 * g:64 * g + 64, br, 0:w], start=True, stop=True).then_inc(scored, 1)

            def turn(u):
                pe.wait_ge(probs_ready, u + 1)
                for gi, kts in enumerate(PT_GROUPS):
                    if u == 0:
                        if gi < 2:
                            pe.wait_ge(cmp_PT_taken, gi + 1)
                    elif gi == 1:
                        pe.wait_ge(turned_dve, u)
                    else:
                        pe.wait_ge(turned_act, 2 * u - 1 + gi // 2)
                    col = 0
                    for kt in kts:
                        for t in range(kt, TT):
                            src = Pr[:, u % 2, P_OFF[t] + kt * P:P_OFF[t] + (kt + 1) * P]
                            ins = pe.transpose(psum[:, PT_BANK[gi], col:col + P], src, ident[:, :])
                            col += P
                    ins.then_inc(turned, 1)

            def weigh(u):
                h, br = UNITS[u]
                g = h // HPG
                b = 6 + h % 2
                if br == 0:
                    if h >= 2:
                        pe.wait_ge(o_split, h - 1)
                    r = 32 * (h % HPG)
                    pe.matmul(bank(b), VC[r:r + N_CMP, :], PcT[r:r + N_CMP, g, :],
                              start=True, stop=False)
                pe.wait_ge(turned_act, 2 * u + 2)
                pe.wait_ge(turned_dve, u + 1)
                for kt in range(TT):
                    w = T - kt * P
                    ins = pe.matmul(psum[:, b, kt * P:T], V[:, br, kt, :],
                                    PT[:, u % 2, PT_OFF[kt]:PT_OFF[kt] + w],
                                    start=False, stop=(br == 1 and kt == TT - 1))
                ins.then_inc(o_made, 1)

            for s in range(len(UNITS) + 2):
                if s < len(UNITS):
                    scores(s)
                if 1 <= s <= len(UNITS):
                    turn(s - 1)
                if s >= 2:
                    weigh(s - 2)

            for m in range(KT):
                p = B_BRANCH + 3 * m
                b = 4 * (m % 2)
                if m >= 2:
                    pe.wait_ge(br_mixed, m - 1)
                if m == 0:
                    pe.wait_ge(turned_act, 2 * len(UNITS))
                    pe.wait_ge(shifted, 4 * len(UNITS))
                if m == 1:
                    pe.wait_ge(o_split, HEADS)
                panel_over_h(p, p % 4, b)
                panel_over_h(p + 1, (p + 1) % 4, b + 1)
                p += 2
                pe.wait_ge(split_done, p + 1)
                if m == 0:
                    pe.wait_ge(o_split, HEADS)
                for k in range(4):
                    product(bank(b + 2), p % 4, k, pool_hi[:, k, :], pool_lo[:, k, :], k == 0, k == 3)
                for k in range(4):
                    ins = product(bank(b + 3), p % 4, 4 + k, o_hi[:, k, :], o_lo[:, k, :], k == 0, k == 3)
                ins.then_inc(panels_used, 1)
            pe.wait_ge(br_mixed, KT - 1)
            pe.wait_ge(ada_used, ADA_BASE["mix"] + 8 * N_ADA["mix"])
            for m in range(KT):
                p = B_MIXOUT + m
                if m < 3:
                    turn_modulation(m, 2, 3 + m)
                if m >= 2:
                    pe.wait_ge(z_done, 8 + m - 1)
                pe.wait_ge(split_done, p + 1)
                for k in range(KT):
                    if m == 0:
                        pe.wait_ge(br_split, k + 1)
                    ins = product(bank(m % 2), p % 4, k, mixed_hi[:, k, :], mixed_lo[:, k, :],
                                  k == 0, k == KT - 1)
                ins.then_inc(panels_used, 1)
            pe.wait_ge(ada_taken, 6)
            norm_stats(2)
            feed_forward(2)

        @block.scalar
        def _(act):
            chain = [0]

            def link(ins):
                chain[0] += 1
                ins.then_inc(act_chain, 1)
                act.wait_ge(act_chain, chain[0])

            def split(p, slot, filled):
                act.wait_ge(raw_landed[slot % 2], 16 * filled)
                need(act, panels_used, p - 3)
                act.activation(w_hi[:, slot, :], raw[:, slot % 2, :], ACT.Copy).then_inc(split_hi, 1)

            todo = [0]

            def split_before(used):
                while todo[0] < min(used + 3, N_PANELS):
                    p = todo[0]
                    split(p, p % 4, p // 2 + 1)
                    todo[0] += 1

            def wait_used(used):
                split_before(used)
                act.wait_ge(panels_used, used)

            def square(L, m):
                if L == 0:
                    if m % 2 == 0:
                        act.wait_ge(x_landed[m // 2], 16)
                else:
                    act.wait_ge(z_done, 8 * (L - 1) + m + 1)
                if m >= 2:
                    act.wait_ge(q_added, 7 * L + max(m - 2, 1))
                act.activation(scr[:, 2 + m % 2, :], X[:, m, :], ACT.Square).then_inc(sq_done, 1)

            def norm(L):
                act.wait_ge(var_done, L + 1)
                act.activation(st[:, 4, :], st[:, 3, :], ACT.Sqrt).then_inc(std_done, 1)
                if L in (0, 3):
                    for i in range(2):
                        act.wait_ge(rows_ready, 2 * L + i + 1)
                        act.activation(scr[:, 2 + i, :], bank(6 + i), ACT.Copy).then_inc(rows_copied, 1)
                if L:
                    act.wait_ge(mod_ready, L + 1)
                if L < 3:
                    def make_h(m):
                        act.wait_ge(xhat_done, 8 * L + m + 1)
                        if L == 0:
                            act.wait_ge(first_mod, m + 1)
                        act.activation(hbuf[:, m, :], X[:, m, :], ACT.Identity,
                                       bias=mod[:, 1, m:m + 1], scale=mod[:, 0, m:m + 1]).then_inc(h_made, 1)

                    if L:
                        make_h(0)
                    for m in range(KT):
                        if L == 0:
                            for p in FIRST_SPLITS[m]:
                                split(p, p % 4, p // 2 + 1)
                                todo[0] += 1
                            make_h(m)
                        elif m and m + 1 < KT:
                            make_h(m + 1)
                        act.wait_ge(h_made, 8 * L + m + 1)
                        act.activation(h_hi[:, m, :], hbuf[:, m, :], ACT.Copy).then_inc(h_hi_done, 1)
                        if L and m == 0:
                            make_h(1)
                if L == 0:
                    act.wait_ge(mod_ready, 1)
                for m in range(KT) if L < 3 else LAST_ORDER:
                    if L == 3 and m >= POOL_NORM:
                        act.wait_ge(xhat_pool, m - POOL_NORM + 1)
                    else:
                        act.wait_ge(xhat_done, 8 * L + m + 1)
                    act.activation(X[:, m, :], X[:, m, :], ACT.Identity,
                                   bias=mod[:, 3, m:m + 1], scale=mod[:, 2, m:m + 1]).then_inc(x_scaled, 1)

            def feed_forward(n):
                base, cb = in_base(n), chunk_base(n)

                def chunk(it, c2, b=None):
                    c = 2 * it + c2
                    if not (isinstance(c, int) and c == 0):
                        act.wait_ge(hidden_made, cb + c)
                        act.activation(act_hi[:, c - 1, :] if isinstance(c, int) else
                                       act_hi[:, bass.ds(c - 1, 1), :].rearrange("p o t -> p (o t)"),
                                       scr[:, 1 - c2, :], ACT.Copy).then_inc(act_hi_done, 1)
                    if b is None:
                        split(base + 2 * c + 3, (2 * c2 + 3) % 4, base // 2 + c + 2)
                        act.wait_ge(panels_used, base + 2 * c + 1)
                    need(act, act_split, cb + c - 1)
                    act.activation(scr[:, c2, :], bank(2 * c2 if b is None else b), ACT.Tanh,
                                   scale=0.5).then_inc(tanh_done, 1)
                    if b is None:
                        split(base + 2 * c + 4, 2 * c2, base // 2 + c + 3)

                split_before(base + 5)
                act.wait_ge(panels_used, base + FIRST)
                for c in range(FIRST // 2):
                    chunk(c // 2, c % 2, 2 * c)
                    if c == 0:
                        split_before(base + 6)
                p = base + 9
                split(p, p % 4, p // 2 + 1)
                act.wait_ge(panels_used, base + 7)
                chunk(1, 1, 6)
                split(p + 1, (p + 1) % 4, (p + 1) // 2 + 1)
                with act.Fori(2, FT // 2) as it:
                    chunk(it, 0)
                    chunk(it, 1)
                todo[0] = base + IN_PANELS + 3
                act.wait_ge(hidden_made, cb + FT)
                act.activation(act_hi[:, FT - 1, :], scr[:, (FT - 1) % 2, :], ACT.Copy).then_inc(act_hi_done, 1)

            act.dma_start(colv[:, :], cols[:, :]).then_inc(cols_landed, 16)
            act.dma_start(ident[:, :], ident_in[:, :]).then_inc(const_landed, 16)
            act.dma_start(posv[:, :, :], pos[:, :, :]).then_inc(const_landed, 16)
            act.dma_start(w2s[:, :, :, :], w2[:, :, :, :]).then_inc(const_landed, 16)
            act.dma_start(icnt[:, :, :], icnt_in[:, :, :]).then_inc(const_landed, 16)
            act.wait_ge(cols_landed, 16)
            act.activation(cact[:, :], colv[:, C_C:C_C + 8], ACT.Tanh, scale=0.5).then_inc(c_tanh, 1)
            act.preload_act_table(ACT.Sqrt)
            for m in range(KT):
                square(0, m)
            split_before(-1)
            norm(0)
            feed_forward(1)
            act.preload_act_table(ACT.Sqrt)
            for m in range(KT):
                split_before(B_FFN1 + IN_PANELS + 3 * m + 3)
                square(1, m)
            act.wait_ge(panels_used, B_MIX)
            act.dma_start(w1k[:, :, :], w1[0, :, :, :]).then_inc(mixc_landed, 16)
            act.dma_start(w1v[:, :, :], w1[1, :, :, :]).then_inc(mixc_landed, 16)
            act.dma_start(cbias[:, :, :, :], cbias_in[:, :, :, :]).then_inc(mixc_landed, 16)
            act.dma_start(cmask[:, :, :], cmask_in[:, :, :]).then_inc(mixc_landed, 16)
            act.dma_start(dist[:, :], dist_in[:, :]).then_inc(mixc_landed, 16)
            norm(1)

            def taken(name):
                return B_MIX + MIX.index(name) + 1

            def k8_bank(name):
                return MIX8.index(name) % 2

            for g in range(4):
                wait_used(taken(f"u{g}"))
                if g == 0:
                    act.wait_ge(pool_delta, 1)
                if g >= 2:
                    act.wait_ge(pool_delta, g)
                act.activation(pads[:, g % 2, 16:528], bank(k8_bank(f"u{g}")), ACT.Copy).then_inc(act_evac, 1)
                if g >= 1:
                    act.wait_ge(pool_delta, g + 1)
                    act.activation(pool_hi[:, g - 1, :], pads[:, 2 + (g - 1) % 2, 16:528],
                                   ACT.Copy).then_inc(pool_hi_done, 1)
            act.wait_ge(pool_delta, 5)
            act.activation(pool_hi[:, 3, :], pads[:, 3, 16:528], ACT.Copy).then_inc(pool_hi_done, 1)
            act.wait_ge(cmp_hidden, 1)
            hb = psum[0:CROWS, 2, :]
            sq = scr[0:CROWS, 1, :]
            act.activation(sq, hb, ACT.Square).then_inc(cmp_sq, 1)
            act.wait_ge(cmp_arg, 1)
            act.activation(sq, sq, ACT.Tanh, scale=GELU_A).then_inc(cmp_tanh, 1)
            wait_used(taken("gate"))
            act.activation(vT[:, 0, :], bank(k8_bank("gate")), ACT.Tanh, scale=0.5).then_inc(act_evac, 1)
            wait_used(taken("q0"))
            act.activation(qT[:, 0, :], bank(k8_bank("q0")), ACT.Copy, scale=HEAD ** -0.5).then_inc(act_evac, 1)
            for j in range(1, 4):
                wait_used(taken(f"q{j}"))
                act.activation(qT[:, j, :], bank(k8_bank(f"q{j}")), ACT.Copy, scale=HEAD ** -0.5).then_inc(act_evac, 1)
            act.wait_ge(cmp_shifted, 1)
            act.activation(Pc[:, :, :, 0:N_CMP], Pc[:, :, :, 0:N_CMP], ACT.Exp).then_inc(cmp_exp, 1)
            for br, name in enumerate(("kslc", "kwin")):
                wait_used(taken(name))
                act.activation(kT[:, br, :], bank(k8_bank(name)), ACT.Copy).then_inc(act_evac, 1)
            for g in range(4):
                act.wait_ge(pool_mixed, g + 1) if g < 3 else wait_used(taken("poolw"))
                act.activation(pool_hi[:, g, :], bank(4 + g % 2), ACT.Copy,
                               scale=colv[:, C_PSCALE + g:C_PSCALE + g + 1]).then_inc(poolout_hi, 1)
            for v, name in enumerate(("vslc", "vwin")):
                wait_used(taken(name))
                act.activation(vT[:, v, :], bank(k8_bank(name)), ACT.Copy).then_inc(act_evac, 1)

            def exps(u):
                for t in range(TT):
                    n = 4 * u + t
                    act.wait_ge(shifted, n + 1)
                    pr = Pr[:, u % 2, P_OFF[t]:P_OFF[t] + P * (t + 1)]
                    act.activation(pr, pr, ACT.Exp, bias=nmax[:, n:n + 1], scale=-1.0,
                                   accum_out=psumv[:, n:n + 1]).then_inc(exp_done, 1)

            def take_turned(u):
                if u >= 2:
                    act.wait_ge(o_made, u - 1)
                for gi in (0, 2):
                    act.wait_ge(turned, 3 * u + gi + 1)
                    w = 512 if gi == 0 else 384
                    off = PT_OFF[PT_GROUPS[gi][0]]
                    act.activation(PT[:, u % 2, off:off + w], bank(PT_BANK[gi], w), ACT.Copy).then_inc(turned_act, 1)

            def take_head(h):
                j, g = h % HPG, h // HPG
                act.wait_ge(o_made, 2 * h + 2)
                act.activation(o_hi[64 * g:64 * g + 64, j, :], psum[64 * g:64 * g + 64, 6 + h % 2, :],
                               ACT.Copy).then_inc(o_hi_done, 1)

            split_before(B_BRANCH + 1)
            for s in range(len(UNITS) + 2):
                if s < len(UNITS):
                    exps(s)
                if 1 <= s <= len(UNITS):
                    take_turned(s - 1)
                if s >= 2 and UNITS[s - 2][1] == 1:
                    take_head(UNITS[s - 2][0])

            for m in range(KT):
                b = 4 * (m % 2)
                for q in range(2):
                    wait_used(B_BRANCH + 3 * m + q + 1)
                    if m >= 2 and q == 0:
                        act.wait_ge(br_split, m - 1)
                    act.activation(tab[:, m % 2, q, :], bank(b + q), ACT.Tanh, scale=0.5).then_inc(br_tanh, 1)
                act.wait_ge(br_mixed, m + 1)
                act.activation(mixed_hi[:, m, :], tab[:, m % 2, 0, :], ACT.Copy).then_inc(br_hi, 1)
            act.preload_act_table(ACT.Sqrt)
            for m in range(KT):
                split_before(B_MIXOUT + m + 1)
                square(2, m)
            norm(2)
            feed_forward(2)
            act.preload_act_table(ACT.Sqrt)
            for m in range(KT):
                split_before(B_FFN2 + IN_PANELS + 3 * m + 3)
                square(3, m)
            norm(3)

        @block.vector
        def _(dve):
            chain = [0]

            def link(ins):
                chain[0] += 1
                ins.then_inc(dve_chain, 1)
                dve.wait_ge(dve_chain, chain[0])

            def sums(L, m):
                if m == 0:
                    return
                if m > 1:
                    dve.wait_ge(s_added, 7 * L + m - 1)
                elif L:
                    dve.wait_ge(z_done, 8 * (L - 1) + m + 1)
                if L and m > 1:
                    dve.wait_ge(z_done, 8 * (L - 1) + m + 1)
                a = X[:, 0, :] if m == 1 else scr[:, 0, :]
                dve.tensor_tensor(scr[:, 0, :], a, X[:, m, :], ALU.add).then_inc(s_added, 1)

            def squares(L, m):
                if m == 0:
                    return
                dve.wait_ge(sq_done, 8 * L + m + 1)
                if m > 1:
                    dve.wait_ge(q_added, 7 * L + m - 1)
                a = scr[:, 2, :] if m == 1 else scr[:, 1, :]
                dve.tensor_tensor(scr[:, 1, :], a, scr[:, 2 + m % 2, :], ALU.add).then_inc(q_added, 1)

            def modulation(b, chunk):
                for i in range(2):
                    ins = dve.tensor_reduce(colp[:, 4 * i:4 * i + 4],
                                            bank(b + i).rearrange("p (m c) -> p m c", c=P), AX.X, ALU.add)
                link(ins)
                dve.tensor_tensor(ada[:, 8 * chunk:8 * chunk + 8], colp[:, 0:8],
                                  colv[:, C_BADA + 8 * chunk:C_BADA + 8 * chunk + 8],
                                  ALU.add).then_inc(ada_taken, 1)

            def norm_columns(L):
                g = colv[:, C_LNG + 8 * L:C_LNG + 8 * L + 8]
                b = colv[:, C_LNB + 8 * L:C_LNB + 8 * L + 8]
                if L < 3:
                    sh = ada[:, 24 * L:24 * L + 8]
                    sc = ada[:, 24 * L + 8:24 * L + 16]
                    link(dve.tensor_scalar(mod[:, 5, :], sc, 1.0, None, ALU.add))
                    dve.tensor_tensor(mod[:, 0, :], mod[:, 5, :], g, ALU.mult)
                    link(dve.tensor_tensor(mod[:, 1, :], mod[:, 5, :], b, ALU.mult))
                    dve.tensor_scalar(mod[:, 2, :], g, ALPHA, None, ALU.mult)
                    dve.tensor_scalar(mod[:, 3, :], b, ALPHA, None, ALU.mult)
                    dve.tensor_tensor(mod[:, 1, :], mod[:, 1, :], sh, ALU.add).then_inc(mod_ready, 1)
                else:
                    dve.tensor_scalar(mod[:, 2, :], g, 1.0, None, ALU.mult)
                    dve.tensor_scalar(mod[:, 3, :], b, 1.0, None, ALU.mult).then_inc(mod_ready, 1)

            def norm(L):
                for i in range(2):
                    dve.wait_ge(stats_ready, 2 * L + i + 1)
                    ins = dve.tensor_reduce(st[:, 6 * i, :], bank(6 + i).rearrange("p (t c) -> p t c", c=P),
                                            AX.X, ALU.add)
                    if i == 0:
                        link(ins)
                        ins = dve.tensor_scalar(st[:, 1, :], st[:, 0, :], 1.0 / D, None, ALU.mult)
                    link(ins)
                link(dve.tensor_tensor(st[:, 2, :], st[:, 1, :], st[:, 1, :], ALU.mult))
                link(dve.scalar_tensor_tensor(st[:, 3, :], st[:, 6, :], 1.0 / D, st[:, 2, :], ALU.mult, ALU.subtract))
                dve.tensor_scalar(st[:, 3, :], st[:, 3, :], 0.0, EPS, ALU.max, ALU.add).then_inc(var_done, 1)
                dve.wait_ge(std_done, L + 1)
                link(dve.reciprocal(st[:, 5, :], st[:, 4, :]))
                link(dve.tensor_tensor(st[:, 6, :], st[:, 5, :], st[:, 5, :], ALU.mult))
                link(dve.tensor_tensor(st[:, 6, :], st[:, 6, :], st[:, 3, :], ALU.mult))
                link(dve.tensor_scalar(st[:, 6, :], st[:, 6, :], -0.5, 1.5, ALU.mult, ALU.add))
                link(dve.tensor_tensor(st[:, 5, :], st[:, 5, :], st[:, 6, :], ALU.mult))
                dve.tensor_tensor(st[:, 7, :], st[:, 1, :], st[:, 5, :], ALU.mult).then_inc(stats_small, 1)
                for i, row in enumerate((5, 7)):
                    if i:
                        dve.wait_ge(stats_small, L + 1)
                    dve.tensor_tensor(scr[:, i, :].rearrange("p (t c) -> p t c", c=P),
                                      ident[:, :].rearrange("p (o c) -> p o c", o=1).broadcast_to([P, TT, P]),
                                      st[:, row, :].rearrange("p (t o) -> p t o", o=1).broadcast_to([P, TT, P]),
                                      ALU.mult).then_inc(rows_made, 1)

            def normalize_tile(L, m):
                if m < (POOL_NORM if L == 3 else KT):
                    if L in (1, 2):
                        dve.wait_ge(rows_ready, 2 * L + 1)
                    else:
                        dve.wait_ge(rows_copied, 2 * (L // 3) + 1)
                    dve.tensor_tensor(X[:, m, :], X[:, m, :], bank(6) if L in (1, 2) else scr[:, 2, :],
                                      ALU.mult).then_inc(scaled, 1)
                if m >= 1:
                    if L in (1, 2):
                        dve.wait_ge(rows_ready, 2 * L + 2)
                    else:
                        dve.wait_ge(rows_copied, 2 * (L // 3) + 2)
                    dve.wait_ge(scaled, 8 * L + m)
                    dve.tensor_tensor(X[:, m - 1, :], X[:, m - 1, :], bank(7) if L in (1, 2) else scr[:, 3, :],
                                      ALU.subtract).then_inc(xhat_done, 1)

            def norm_tiles(L):
                for m in range((POOL_NORM if L == 3 else KT) + 1):
                    normalize_tile(L, m)

            def ada_unit(phase, step, q):
                u = ADA_BASE[phase] + N_ADA[phase] * step + q
                dve.wait_ge(ada_landed[q % 3], 16 * ada_slot_count(phase, step, q))
                a = acc[:, q // 2, (q % 2) * 512:(q % 2) * 512 + 512]
                if isinstance(step, int):
                    sc = cact[:, step:step + 1]
                else:
                    sc = cact[:, bass.ds(step, 1)]
                if isinstance(step, int) and step == 0:
                    dve.tensor_scalar(a, ada_raw[:, q % 3, :], sc, None, ALU.mult).then_inc(ada_used, 1)
                else:
                    dve.wait_ge(ada_used, u - N_ADA[phase] + 1)
                    dve.scalar_tensor_tensor(a, ada_raw[:, q % 3, :], sc, a, ALU.mult, ALU.add).then_inc(ada_used, 1)

            def feed_forward(n):
                base, cb = in_base(n), chunk_base(n)

                def lo(c, b):
                    dve.wait_ge(act_hi_done, cb + c + 1)
                    if isinstance(c, int):
                        hi, lo_ = act_hi[:, c, :], act_lo[:, c, :]
                    else:
                        hi = act_hi[:, bass.ds(c, 1), :].rearrange("p o t -> p (o t)")
                        lo_ = act_lo[:, bass.ds(c, 1), :].rearrange("p o t -> p (o t)")
                    dve.tensor_tensor(lo_, scr[:, b, :], hi.bitcast(F32), ALU.subtract).then_inc(act_split, 1)

                def chunk(it, c2, with_ada, b=None):
                    c = 2 * it + c2
                    if not (isinstance(c, int) and c == 0):
                        lo(c - 1, 1 - c2)
                    dve.wait_ge(tanh_done, cb + c + 1)
                    b0 = 2 * c2 if b is None else b
                    dve.scalar_tensor_tensor(scr[:, c2, :], scr[:, c2, :], 1.0, bank(b0),
                                             ALU.add, ALU.mult).then_inc(gated, 1)
                    if with_ada:
                        per = N_ADA[n] // 2
                        for q in range(per * c2, per * c2 + per):
                            ada_unit(n, it, q)
                    dve.wait_ge(gated, cb + c + 1)
                    dve.wait_ge(panels_used, base + (FIRST if b is not None and b < FIRST else 2 * c + 2))
                    dve.tensor_tensor(scr[:, c2, :], scr[:, c2, :], bank(b0 + 1), ALU.mult).then_inc(hidden_made, 1)

                for q in range(N_ADA[n]):
                    ada_unit(n, 0, q)
                for c in range(4):
                    chunk(c // 2, c % 2, c >= 2, 2 * c)
                with dve.Fori(2, KT) as it:
                    chunk(it, 0, True)
                    chunk(it, 1, True)
                with dve.Fori(KT, FT // 2) as it:
                    chunk(it, 0, False)
                    chunk(it, 1, False)
                lo(FT - 1, (FT - 1) % 2)

            def residual(L, gate_chunk, factor, used):
                chunks = 1 if L == 3 else 3
                y_bank, mod_bank = (0, 2) if L == 2 else (4, 6)
                cols0 = {1: 0, 2: 3, 3: 6}[L]
                for m in range(KT):
                    if m >= 2:
                        squares(L, m - 1)
                    if m < chunks:
                        dve.wait_ge(ada_cols, cols0 + m + 1)
                        modulation(mod_bank, gate_chunk + m)
                    if m == 0:
                        dve.wait_ge(ada_taken, cols0 + 1)
                        link(dve.tensor_scalar(mod[:, 4, :], ada[:, 8 * gate_chunk:8 * gate_chunk + 8], factor,
                                               None, ALU.mult))
                    if m == 3:
                        dve.wait_ge(ada_taken, cols0 + chunks)
                        dve.wait_ge(x_scaled, 8 * L)
                        norm_columns(L)
                    dve.wait_ge(panels_used, used(m))
                    dve.wait_ge(x_scaled, 8 * (L - 1) + m + 1)
                    dve.scalar_tensor_tensor(X[:, m, :], bank(y_bank + m % 2), mod[:, 4, m:m + 1], X[:, m, :],
                                             ALU.mult, ALU.add).then_inc(z_done, 1)
                    sums(L, m)
                squares(L, KT - 1)

            dve.wait_ge(c_tanh, 1)
            link(dve.scalar_tensor_tensor(cact[:, :], cact[:, :], 1.0, colv[:, C_C:C_C + 8], ALU.add, ALU.mult))
            dve.tensor_scalar(cact[:, :], cact[:, :], 0.5, None, ALU.mult).then_inc(ada_acc_start, 1)
            for m in range(KT):
                squares(0, m)
            g0, b0 = colv[:, C_LNG:C_LNG + 8], colv[:, C_LNB:C_LNB + 8]
            dve.tensor_scalar(mod[:, 2, :], g0, ALPHA, None, ALU.mult)
            dve.tensor_scalar(mod[:, 3, :], b0, ALPHA, None, ALU.mult).then_inc(mod_ready, 1)

            def first_sums(k):
                dve.wait_ge(ada0_landed[k], 16)
                if k >= 2:
                    dve.wait_ge(first_cols, k - 1)
                for r in range(KT):
                    a = acc[:, k % 2, (r % 2) * 2 * P:(r % 2) * 2 * P + 2 * P]
                    w = ada_first[k][:, r, :]
                    if r < 2:
                        ins = dve.tensor_scalar(a, w, cact[:, r:r + 1], None, ALU.mult)
                    else:
                        dve.wait_ge(first_step, (KT - 2) * k + r - 1)
                        ins = dve.scalar_tensor_tensor(a, w, cact[:, r:r + 1], a, ALU.mult, ALU.add)
                    ins.then_inc(first_step if r < KT - 2 else first_acc, 1)

            def first_columns(k):
                dve.wait_ge(first_cols, k + 1)
                dve.tensor_reduce(colp[:, 0:2], bank(6 + k % 2).rearrange("p (a s c) -> p s a c", a=2, s=2),
                                  AX.XY, ALU.add).then_inc(first_summed, 1)
                dve.wait_ge(first_summed, k + 1)
                link(dve.tensor_tensor(ada[:, k:16:8], colp[:, 0:2], colv[:, C_BADA + k:C_BADA + 16:8], ALU.add))
                link(dve.tensor_scalar(mod[:, 5, k:k + 1], ada[:, 8 + k:9 + k], 1.0, None, ALU.add))
                dve.tensor_tensor(mod[:, 0, k:k + 1], mod[:, 5, k:k + 1], g0[:, k:k + 1], ALU.mult)
                dve.scalar_tensor_tensor(mod[:, 1, k:k + 1], b0[:, k:k + 1], mod[:, 5, k:k + 1], ada[:, k:k + 1],
                                         ALU.mult, ALU.add).then_inc(first_mod, 1)

            norm(0)
            first_sums(0)
            normalize_tile(0, 0)
            for k in range(KT):
                normalize_tile(0, k + 1)
                first_columns(k)
                if k + 1 < KT:
                    first_sums(k + 1)
            feed_forward(1)
            ob1 = B_FFN1 + IN_PANELS
            residual(1, 2, 0.25, lambda m: ob1 + 3 * m + 3)
            norm(1)
            norm_tiles(1)

            def taken(name):
                return B_MIX + MIX.index(name) + 1

            dve.wait_ge(h_split, 16)
            for i in range(4):
                ins = dve.memset(pads[:, i, 0:16], 0.0)
            ins.then_inc(pool_delta, 1)
            dve.memset(Pc[:, :, :, N_CMP:CPAD], 0.0)
            for kv, name in enumerate(("kc", "vc")):
                dve.wait_ge(panels_used, taken(name))
                for half in range(2):
                    for r in range(2):
                        for g in range(GROUPS):
                            src = psum[64 * g:64 * g + 64, kv, r:T:2].rearrange("p (n i) -> p i n", i=8)
                            dst = blocks[64 * r:64 * r + 64, 2 * kv + half, :, 32 * g:32 * g + 32]
                            pp = posv[64 * r:64 * r + 64, kv:kv + 1, 8 * half:8 * half + 8]\
                                .rearrange("p o i -> p i o").broadcast_to([64, 8, 32])
                            ins = dve.tensor_tensor(dst, src, pp, ALU.add)
                            if r == 1:
                                ins.then_inc(kv_blocks, 1)
            for g, w in enumerate(WINDOWS):
                dve.wait_ge(act_evac, g + 1)
                u = pads[:, g % 2, :]
                s = pads[:, 2 + g % 2, :]
                if g >= 2:
                    dve.wait_ge(pool_split, g - 1)
                link(dve.tensor_tensor(s[:, 1:528], u[:, 1:528], u[:, 0:527], ALU.add))
                step = 2
                cur, oth = s, scr[:, 2:4, :].rearrange("p a t -> p (a t)")
                while step < w:
                    lo_ = 2 * step - 1
                    link(dve.tensor_tensor(oth[:, lo_:528], cur[:, lo_:528], cur[:, lo_ - step:528 - step], ALU.add))
                    cur, oth = oth, cur
                    step *= 2
                head = cst[:, g % 2, 0:16]
                link(dve.tensor_tensor(head, cur[:, 16:32], icnt[:, g, :], ALU.mult))
                link(dve.scalar_tensor_tensor(s[:, 16:528], cur[:, 16:528], 1.0 / w, u[:, 16:528],
                                              ALU.mult, ALU.subtract))
                dve.tensor_tensor(s[:, 16:32], head, u[:, 16:32], ALU.subtract).then_inc(pool_delta, 1)
                if g >= 1:
                    dve.wait_ge(pool_hi_done, g)
                    dve.tensor_tensor(pool_lo[:, g - 1, :], pads[:, 2 + (g - 1) % 2, 16:528],
                                      pool_hi[:, g - 1, :].bitcast(F32), ALU.subtract).then_inc(pool_split, 1)
            dve.wait_ge(pool_hi_done, 4)
            dve.tensor_tensor(pool_lo[:, 3, :], pads[:, 3, 16:528],
                              pool_hi[:, 3, :].bitcast(F32), ALU.subtract).then_inc(pool_split, 1)
            hb = psum[0:CROWS, 2, :]
            sq = scr[0:CROWS, 1, :]
            dve.wait_ge(cmp_sq, 1)
            link(dve.tensor_scalar(sq, sq, GELU_B, 1.0, ALU.mult, ALU.add))
            dve.tensor_tensor(sq, sq, hb, ALU.mult).then_inc(cmp_arg, 1)
            dve.memset(kcB[:, :], 0.0)
            dve.wait_ge(cmp_tanh, 1)
            dve.scalar_tensor_tensor(scr[0:CROWS, 0, :], sq, 1.0, hb, ALU.add, ALU.mult).then_inc(cmp_act, 1)
            dve.wait_ge(cmp_turned, 1)
            dve.tensor_copy(hidden[:, :, 0:CROWS], psum[:, 3, 0:256].rearrange("p (n c) -> p n c", c=64)[:, :, 0:CROWS])\
               .then_inc(cmp_hidden_T, 1)
            dve.wait_ge(cmp_kv, 1)
            for g in range(GROUPS):
                rows = slice(64 * g, 64 * g + 64)
                ins = dve.tensor_scalar(kcB[rows, N_CMP * g:N_CMP * g + N_CMP], psum[rows, 2, 0:N_CMP], 0.5, None, ALU.mult)
            ins.then_inc(cmp_kv_taken, 1)
            for r in range(4):
                ins = dve.tensor_scalar(VC[32 * r:32 * r + 31, :], psum[0:31, 2, 64:192], 0.5, None, ALU.mult)
            ins.then_inc(cmp_kv_taken, 1)
            dve.wait_ge(gates_T, 1)
            gt = psum[:, 4, :].rearrange("p (t c) -> p t c", c=P)[:, :, 0:24]
            dve.tensor_scalar(G[:, :, :], gt, 0.5, 0.5, ALU.mult, ALU.add).then_inc(gates_taken, 1)
            Pv = Pc[:, :, :, 0:N_CMP]
            dve.wait_ge(mixc_landed, 16 * 5)
            for t in range(TT):
                dve.wait_ge(cmp_scored, t // 2 + 1)
                col = (t % 2) * HEADS * N_CMP
                src = psum[:, 6 + t // 2, col:col + HEADS * N_CMP].rearrange("p (j g n) -> p g j n", g=2, n=N_CMP)
                last = dve.tensor_tensor(Pc[:, t, :, 0:N_CMP].rearrange("p (g j) n -> p g j n", g=2), src,
                                         cbias[:, t, :, :].rearrange("p (g j) n -> p g j n", g=2), ALU.add)
            link(last)
            link(dve.tensor_reduce(cst[:, 0, :], Pv, AX.X, ALU.max))

            def over_blocks(v, t):
                return v[:, 8 * t:8 * t + 8].rearrange("p (h o) -> p h o", o=1).broadcast_to([P, 8, N_CMP])

            for t in range(TT):
                ins = dve.tensor_tensor(Pc[:, t, :, 0:N_CMP], Pc[:, t, :, 0:N_CMP], over_blocks(cst[:, 0, :], t), ALU.subtract)
            ins.then_inc(cmp_shifted, 1)
            dve.wait_ge(cmp_exp, 1)
            link(dve.tensor_reduce(cst[:, 1, :], Pv, AX.X, ALU.add))
            link(dve.reciprocal(cst[:, 1, :], cst[:, 1, :]))
            dve.wait_ge(gates_taken, 1)
            link(dve.tensor_tensor(cst[:, 2, :].rearrange("p (t h) -> p t h", t=TT),
                                   cst[:, 1, :].rearrange("p (t h) -> p t h", t=TT), G[:, :, 0:24:3], ALU.mult))
            for t in range(TT):
                ins = dve.tensor_tensor(Pc[:, t, :, 0:N_CMP], Pc[:, t, :, 0:N_CMP], over_blocks(cst[:, 2, :], t), ALU.mult)
            link(ins)
            for t in range(TT):
                ins = dve.tensor_tensor(Pc[:, t, :, 0:N_CMP], Pc[:, t, :, 0:N_CMP],
                                        cmask[:, t:t + 1, 0:N_CMP].broadcast_to([P, 8, N_CMP]), ALU.mult)
            ins.then_inc(cmp_probs, 1)
            for g in range(4):
                dve.wait_ge(poolout_hi, g + 1)
                dve.scalar_tensor_tensor(pool_lo[:, g, :], bank(4 + g % 2), colv[:, C_PSCALE + g:C_PSCALE + g + 1],
                                         pool_hi[:, g, :].bitcast(F32), ALU.mult, ALU.subtract).then_inc(poolout_split, 1)
            for v in range(2):
                dve.wait_ge(v_turned, v + 1)
                dve.tensor_copy(V[:, v, :, :].rearrange("p t c -> p (t c)"), bank(2 + v)).then_inc(v_taken, 1)
            for g in range(GROUPS):
                dve.wait_ge(cmp_PT, g + 1)
                dve.tensor_copy(PcT[:, g, :], bank(4 + g)).then_inc(cmp_PT_taken, 1)

            def alibi(h):
                dve.tensor_scalar(abias[:, h % 2, :], dist[:, :], 2.0 ** -(h + 1), None, ALU.mult).then_inc(bias_made, 1)

            def shift(u):
                h, br = UNITS[u]
                dve.wait_ge(bias_made, h + 1)
                if u >= 2:
                    dve.wait_ge(turned, 3 * (u - 1))
                for t in range(TT):
                    n = 4 * u + t
                    w = P * (t + 1)
                    dve.wait_ge(scored, n + 1)
                    dve.tensor_tensor_reduce(Pr[:, u % 2, P_OFF[t]:P_OFF[t] + w], bank(1 + n % 3, w),
                                             abias[:, h % 2, T - w:T], -1.0, 1e30, ALU.add, ALU.min,
                                             nmax[:, n:n + 1]).then_inc(shifted, 1)

            def normalize(u):
                h, br = UNITS[u]
                dve.wait_ge(exp_done, 4 * u + 4)
                s4 = slice(4 * u, 4 * u + 4)
                link(dve.reciprocal(pscl[:, s4], psumv[:, s4]))
                link(dve.tensor_tensor(pscl[:, s4], pscl[:, s4], G[:, :, 3 * h + 1 + br], ALU.mult))
                for t in range(TT):
                    n = 4 * u + t
                    pr = Pr[:, u % 2, P_OFF[t]:P_OFF[t] + P * (t + 1)]
                    ins = dve.tensor_scalar(pr, pr, pscl[:, n:n + 1], None, ALU.mult)
                ins.then_inc(probs_ready, 1)
                if br == 0 and h + 1 < HEADS:
                    alibi(h + 1)

            def take_turned(u):
                if u >= 2:
                    dve.wait_ge(o_made, u - 1)
                dve.wait_ge(turned, 3 * u + 2)
                off = PT_OFF[1]
                dve.tensor_copy(PT[:, u % 2, off:off + 384], bank(PT_BANK[1], 384)).then_inc(turned_dve, 1)

            def take_head(h):
                j, g = h % HPG, h // HPG
                dve.wait_ge(o_hi_done, h + 1)
                rows = slice(64 * g, 64 * g + 64)
                dve.tensor_tensor(o_lo[rows, j, :], psum[rows, 6 + h % 2, :], o_hi[rows, j, :].bitcast(F32),
                                  ALU.subtract).then_inc(o_split, 1)

            alibi(0)
            for s in range(len(UNITS) + 2):
                if s < len(UNITS):
                    shift(s)
                if 1 <= s <= len(UNITS):
                    take_turned(s - 1)
                if s < len(UNITS):
                    normalize(s)
                if s >= 2 and UNITS[s - 2][1] == 1:
                    take_head(UNITS[s - 2][0])

            def mixed_lo_part(m):
                dve.wait_ge(br_hi, m + 1)
                dve.tensor_tensor(mixed_lo[:, m, :], tab[:, m % 2, 0, :], mixed_hi[:, m, :].bitcast(F32),
                                  ALU.subtract).then_inc(br_split, 1)

            for m in range(KT):
                b = 4 * (m % 2)
                for q in range(6):
                    ada_unit("mix", m, q)
                dve.wait_ge(panels_used, B_BRANCH + 3 * m + 3)
                for q in range(2):
                    dve.wait_ge(br_tanh, 2 * m + q + 1)
                    dve.scalar_tensor_tensor(tab[:, m % 2, q, :], tab[:, m % 2, q, :], 1.0, bank(b + 2 + q),
                                             ALU.add, ALU.mult).then_inc(br_gated, 1)
                dve.wait_ge(br_gated, 2 * m + 2)
                dve.tensor_tensor(tab[:, m % 2, 0, :], tab[:, m % 2, 0, :], tab[:, m % 2, 1, :],
                                  ALU.add).then_inc(br_mixed, 1)
                mixed_lo_part(m)
            residual(2, 5, 0.5, lambda m: B_MIXOUT + m + 1)
            norm(2)
            norm_tiles(2)
            feed_forward(2)
            ob2 = B_FFN2 + IN_PANELS
            residual(3, 8, 0.25, lambda m: ob2 + 3 * m + 3)
            norm(3)
            norm_tiles(3)


def _tiles(w):
    K, N = w.shape
    return np.ascontiguousarray(w.reshape(K // P, P, N // P, P).transpose(2, 1, 0, 3)).reshape(N // P, P, K)


def _constants():
    p = np.arange(P)[:, None]
    rel = np.arange(T)[None, :] - (T - P)
    dist = np.where(rel > p, -1e34, -(p - rel)).astype(np.float32)
    t = np.arange(T)
    end = np.arange(N_CMP) * STRIDE + 2 * STRIDE - 1
    d = t[:, None] - end[None, :]
    slopes = 2.0 ** -np.arange(1.0, HEADS + 1)
    cb = np.where(d[:, None, :] < 0, NEG, -slopes[None, :, None] * d[:, None, :]).astype(np.float32)
    cb = cb.reshape(TT, P, HEADS, N_CMP).transpose(1, 0, 2, 3)
    cm = np.zeros((T, CPAD), np.float32)
    cm[:, :N_CMP] = d >= 0
    cm = cm.reshape(TT, P, CPAD).transpose(1, 0, 2)
    ic = np.stack([1.0 / np.minimum(np.arange(16) + 1, w) for w in WINDOWS]).astype(np.float32)
    return {"ident": np.eye(P, dtype=np.float32), "dist": dist, "cbias": np.ascontiguousarray(cb),
            "cmask": np.ascontiguousarray(cm), "icnt": np.ascontiguousarray(np.broadcast_to(ic, (P, 4, 16)))}


def _mixer_columns():
    q0, kv0, g0 = 512, 1024, 1792
    br0 = g0 + 24
    at = {f"u{g}": np.arange(P) + P * g for g in range(4)}
    for j in range(4):
        at[f"q{j}"] = np.concatenate([np.arange(64) + q0 + 64 * j, np.arange(64) + q0 + 64 * (4 + j)])
    for i, n in enumerate(("kc", "vc", "kslc", "vslc", "kwin", "vwin")):
        at[n] = np.arange(P) + kv0 + P * i
    at["gate"] = np.concatenate([np.arange(24) + g0, np.full(P - 24, -1)])
    order = [at[n] for n in MIX8]
    for m in range(KT):
        order += [np.arange(P) + br0 + P * m, np.arange(P) + br0 + D + P * m]
    return np.concatenate(order)


def kernel(**inputs):
    import concourse.bacc as _bacc
    from concourse.bass_utils import run_bass_kernel_spmd as _run

    a = {k: np.asarray(v) for k, v in inputs.items()}

    def column(v):
        return v.reshape(-1, P).T

    arrays = {}
    arrays["xT"] = np.ascontiguousarray(a["x"][0].T.reshape(KT, P, T).transpose(1, 0, 2))
    arrays["cols"] = np.ascontiguousarray(np.concatenate(
        [column(a["b_ada"][0])] + [column(v) for v in (a["ln_in_g"], a["ln1_g"][0], a["ln2_g"][0], a["ln3_g"][0],
                                                      a["ln_in_b"], a["ln1_b"][0], a["ln2_b"][0], a["ln3_b"][0])]
        + [column(a["pool_scale"][0]), column(a["c"][0])], axis=1))
    arrays["ada_w"] = np.ascontiguousarray(a["w_ada"][0]).reshape(KT, P, 9 * D)

    arrays["ada1"] = a["w_ada"][0][:, :2 * D].reshape(KT, P, 2, KT, P).transpose(3, 1, 0, 2, 4).reshape(KT, P, KT, 2 * P)

    def ffn_in(w):
        panels = np.stack([_tiles(w[:, :F]), _tiles(w[:, F:])], axis=1).reshape(2 * FT, P, KT, P)
        first = panels[:FIRST].transpose(2, 0, 1, 3).reshape(FIRST, KT, P, P).transpose(0, 2, 1, 3)
        return np.concatenate([first, panels[FIRST:]]).reshape(FT, 2, P, D)

    arrays["ffn_in"] = np.stack([ffn_in(a["ffn1_w_in"][0]), ffn_in(a["ffn2_w_in"][0])])
    arrays["ffn_out"] = np.stack([_tiles(a["ffn1_w_out"][0]), _tiles(a["ffn2_w_out"][0])])
    cols = _mixer_columns()
    padded = np.concatenate([a["w_mix_in"][0], np.zeros((D, 1), np.float32)], axis=1)
    arrays["mix_w"] = _tiles(padded[:, cols])
    arrays["pool_w"] = np.ascontiguousarray(a["pool_w"][0].transpose(1, 0, 2)).reshape(P, 4 * P)
    heads = np.concatenate([np.concatenate([np.arange(64) + 64 * j, np.arange(64) + 64 * (4 + j)]) for j in range(4)])
    arrays["branch_w"] = np.concatenate([_tiles(a["w_branch_a"][0]), _tiles(a["w_branch_b"][0][heads])], axis=2)
    arrays["mixout_w"] = _tiles(a["w_mix_out"][0])
    arrays["w1"] = np.stack([a[n][0].reshape(PAIRS, P, 256).transpose(1, 0, 2) for n in ("cmp_k_w1", "cmp_v_w1")])
    arrays["w2"] = np.ascontiguousarray(
        np.stack([a[n][0].reshape(HID_T, P, HEAD) for n in ("cmp_k_w2", "cmp_v_w2")]).transpose(2, 0, 1, 3))
    arrays["pos"] = np.ascontiguousarray(
        np.stack([a[n][0].reshape(PAIRS, P).T for n in ("cmp_pos_k", "cmp_pos_v")], axis=1))
    arrays.update(_constants())

    nc = _bacc.Bacc("TRN2", target_bir_lowering=False, num_devices=1)
    ins = {}
    for name in arrays:
        arrays[name] = np.ascontiguousarray(arrays[name])
        ins[name] = nc.dram_tensor(f"in_{name}", arrays[name].shape, F32, kind="ExternalInput").ap()
    out = nc.dram_tensor("out_0", (KT, P, T), F32, kind="ExternalOutput").ap()
    build(nc, *[ins[n] for n in ("xT", "cols", "ada_w", "ada1", "ffn_in", "ffn_out", "mix_w", "pool_w", "branch_w",
                                 "mixout_w", "w1", "w2", "pos", "ident", "dist", "cbias", "cmask", "icnt")], out)
    r = _run(nc, [{f"in_{n}": v for n, v in arrays.items()}], core_ids=[0])
    got = r.results[0]["out_0"]
    return np.ascontiguousarray(got.reshape(D, T).T).reshape(1, T, D)
```
